# Optimizing a Trainium2 kernel written in Bass

```python
import math
import jax, jax.numpy as jnp
from jax import lax
import numpy as np

D_MODEL = 1024
BATCH = 1
SEQ = 512
DEPTH = 2

HEAD_DIM = 64
FOX_HEADS = 6
DIFF_HEADS = 4
DIFF_QK_DIM = 32
DIFF_V_DIM = 64
DSA_HEADS = 6
DSA_KV_DIM = 64
IDX_HEADS = 4
IDX_DIM = 64
DSA_TOPK = 256
ROPE_THETA = 500000.0
ROPE_FRACTION = 4
Q_BLOCK = 128
NORM_EPS = 1e-6
FFN_HIDDEN = -(-8 * D_MODEL // (3 * 256)) * 256

MIX_WIDTH = FOX_HEADS * HEAD_DIM + DIFF_HEADS * DIFF_V_DIM + DSA_HEADS * HEAD_DIM

SPLIT_SIZES = (
    FOX_HEADS * HEAD_DIM,
    FOX_HEADS * HEAD_DIM,
    FOX_HEADS * HEAD_DIM,
    FOX_HEADS,
    DIFF_HEADS * 2 * DIFF_QK_DIM,
    DIFF_HEADS * 2 * DIFF_QK_DIM,
    DIFF_HEADS * DIFF_V_DIM,
    DSA_HEADS * HEAD_DIM,
    DSA_KV_DIM,
    DSA_KV_DIM,
    IDX_HEADS * IDX_DIM,
    IDX_DIM,
    IDX_HEADS,
)
IN_WIDTH = sum(SPLIT_SIZES)


def rms_norm(x, g):
    xf = x.astype(jnp.float32)
    y = xf * lax.rsqrt(jnp.mean(xf * xf, axis=-1, keepdims=True) + NORM_EPS)
    return (y * g.astype(jnp.float32)).astype(x.dtype)

def rope_tables(seq_len, head_dim):
    rot = head_dim // ROPE_FRACTION
    inv_freq = 1.0 / (ROPE_THETA ** (jnp.arange(0, rot, 2, dtype=jnp.float32) / rot))
    ang = jnp.arange(seq_len, dtype=jnp.float32)[:, None] * inv_freq[None, :]
    return jnp.cos(ang), jnp.sin(ang)

def partial_rope(x, cos, sin):
    rot = x.shape[-1] // ROPE_FRACTION
    half = rot // 2
    c = cos.astype(x.dtype)
    s = sin.astype(x.dtype)
    x1 = x[..., :half]
    x2 = x[..., half:rot]
    return jnp.concatenate([x1 * c - x2 * s, x2 * c + x1 * s, x[..., rot:]], axis=-1)

def blocks_to_seq(out):
    out = jnp.moveaxis(out, 0, 1)
    return out.reshape((out.shape[0], out.shape[1] * out.shape[2]) + out.shape[3:])

def causal_mask(start, seq_len):
    qpos = start + jnp.arange(Q_BLOCK)
    kpos = jnp.arange(seq_len)
    return kpos[None, :] <= qpos[:, None], qpos

def fox_attention(q, k, v, cum_logf):
    S = q.shape[2]
    scale = q.shape[-1] ** -0.5

    def block(i):
        start = i * Q_BLOCK
        qb = lax.dynamic_slice_in_dim(q, start, Q_BLOCK, axis=2)
        cb = lax.dynamic_slice_in_dim(cum_logf, start, Q_BLOCK, axis=2)
        logits = (jnp.einsum('bhqd,bhkd->bhqk', qb, k).astype(jnp.float32) * scale
                  + cb[..., :, None] - cum_logf[..., None, :])
        mask, _ = causal_mask(start, S)
        p = jax.nn.softmax(jnp.where(mask, logits, -jnp.inf), axis=-1).astype(v.dtype)
        return jnp.einsum('bhqk,bhkd->bqhd', p, v)

    return blocks_to_seq(lax.map(block, jnp.arange(S // Q_BLOCK)))

def diff_attention(q, k, v, lam):
    S = q.shape[3]
    scale = q.shape[-1] ** -0.5

    def block(i):
        start = i * Q_BLOCK
        qb = lax.dynamic_slice_in_dim(q, start, Q_BLOCK, axis=3)
        logits = jnp.einsum('bhmqd,bhmkd->bhmqk', qb, k).astype(jnp.float32) * scale
        mask, _ = causal_mask(start, S)
        p = jax.nn.softmax(jnp.where(mask, logits, -jnp.inf), axis=-1)
        a = (p[:, :, 0] - lam * p[:, :, 1]).astype(v.dtype)
        return jnp.einsum('bhqk,bhkd->bqhd', a, v)

    return blocks_to_seq(lax.map(block, jnp.arange(S // Q_BLOCK)))

def dsa_attention(q, k, v, q_idx, k_idx, w_idx, topk):
    S = q.shape[2]
    scale = q.shape[-1] ** -0.5
    idx_scale = q_idx.shape[-1] ** -0.5
    gather = jax.vmap(lambda table, ix: table[ix])

    def block(i):
        start = i * Q_BLOCK
        qib = lax.dynamic_slice_in_dim(q_idx, start, Q_BLOCK, axis=2)
        wib = lax.dynamic_slice_in_dim(w_idx, start, Q_BLOCK, axis=1).astype(jnp.float32)
        s_idx = jnp.einsum('bhqd,bkd->bhqk', qib, k_idx).astype(jnp.float32) * idx_scale
        score = jnp.einsum('bqh,bhqk->bqk', wib, jax.nn.relu(s_idx))
        mask, qpos = causal_mask(start, S)
        score = jnp.where(mask[None], score, -jnp.inf)
        _, sel = lax.top_k(score, topk)
        valid = sel <= qpos[None, :, None]
        kg = gather(k, sel)
        vg = gather(v, sel)
        qb = lax.dynamic_slice_in_dim(q, start, Q_BLOCK, axis=2)
        logits = jnp.einsum('bhqd,bqjd->bhqj', qb, kg).astype(jnp.float32) * scale
        p = jax.nn.softmax(jnp.where(valid[:, None], logits, -jnp.inf), axis=-1).astype(vg.dtype)
        return jnp.einsum('bhqj,bqjd->bqhd', p, vg)

    return blocks_to_seq(lax.map(block, jnp.arange(S // Q_BLOCK)))

def first_inputs(seed: int = 0) -> dict:
    key = jax.random.key(seed)
    ks = jax.random.split(key, 19)
    f32 = jnp.float32

    def nrm(k, shape, scale):
        return jax.random.normal(k, shape, f32) * scale

    res_scale = 1.0 / math.sqrt(2 * DEPTH)
    return {
        "x": nrm(ks[0], (BATCH, SEQ, D_MODEL), 1.0),
        "attn_norm": 1.0 + nrm(ks[1], (DEPTH, D_MODEL), 0.02),
        "w_in": nrm(ks[2], (DEPTH, D_MODEL, IN_WIDTH), D_MODEL ** -0.5),
        "fox_fb": jax.random.uniform(ks[3], (DEPTH, FOX_HEADS), f32, 1.0, 4.0),
        "fox_qn": 1.0 + nrm(ks[4], (DEPTH, HEAD_DIM), 0.02),
        "fox_kn": 1.0 + nrm(ks[5], (DEPTH, HEAD_DIM), 0.02),
        "diff_qn": 1.0 + nrm(ks[6], (DEPTH, DIFF_QK_DIM), 0.02),
        "diff_kn": 1.0 + nrm(ks[7], (DEPTH, DIFF_QK_DIM), 0.02),
        "diff_lq1": nrm(ks[8], (DEPTH, DIFF_QK_DIM), 0.1),
        "diff_lk1": nrm(ks[9], (DEPTH, DIFF_QK_DIM), 0.1),
        "diff_lq2": nrm(ks[10], (DEPTH, DIFF_QK_DIM), 0.1),
        "diff_lk2": nrm(ks[11], (DEPTH, DIFF_QK_DIM), 0.1),
        "diff_subln": 1.0 + nrm(ks[12], (DEPTH, DIFF_V_DIM), 0.02),
        "dsa_qn": 1.0 + nrm(ks[13], (DEPTH, HEAD_DIM), 0.02),
        "dsa_kn": 1.0 + nrm(ks[14], (DEPTH, DSA_KV_DIM), 0.02),
        "w_out": nrm(ks[15], (DEPTH, MIX_WIDTH, D_MODEL), MIX_WIDTH ** -0.5 * res_scale),
        "ffn_norm": 1.0 + nrm(ks[16], (DEPTH, D_MODEL), 0.02),
        "w_gate_up": nrm(ks[17], (DEPTH, D_MODEL, 2 * FFN_HIDDEN), D_MODEL ** -0.5),
        "w_down": nrm(ks[18], (DEPTH, FFN_HIDDEN, D_MODEL), FFN_HIDDEN ** -0.5 * res_scale),
    }

def first_block(x, attn_norm, w_in, fox_fb, fox_qn, fox_kn, diff_qn, diff_kn,
              diff_lq1, diff_lk1, diff_lq2, diff_lk2, diff_subln, dsa_qn, dsa_kn,
              w_out, ffn_norm, w_gate_up, w_down):
    B, S, _ = x.shape
    topk = min(DSA_TOPK, S // 4)
    cos64, sin64 = rope_tables(S, HEAD_DIM)
    cos32, sin32 = rope_tables(S, DIFF_QK_DIM)
    split_points = [int(v) for v in np.cumsum(SPLIT_SIZES)[:-1]]

    for l in range(DEPTH):
        h = rms_norm(x, attn_norm[l])
        proj = h @ w_in[l]
        (fq, fk, fv, ff, dq, dk, dv, sq, sk, sv, iq, ik, iw) = jnp.split(proj, split_points, axis=-1)

        fq = rms_norm(fq.reshape(B, S, FOX_HEADS, HEAD_DIM), fox_qn[l]).transpose(0, 2, 1, 3)
        fk = rms_norm(fk.reshape(B, S, FOX_HEADS, HEAD_DIM), fox_kn[l]).transpose(0, 2, 1, 3)
        fv = fv.reshape(B, S, FOX_HEADS, HEAD_DIM).transpose(0, 2, 1, 3)
        log_f = jax.nn.log_sigmoid(ff.astype(jnp.float32) + fox_fb[l].astype(jnp.float32))
        cum_logf = jnp.cumsum(log_f, axis=1).transpose(0, 2, 1)
        o_fox = fox_attention(fq, fk, fv, cum_logf).reshape(B, S, FOX_HEADS * HEAD_DIM)

        lam_init = 0.8 - 0.6 * math.exp(-0.3 * l)
        lam = (jnp.exp(jnp.sum(diff_lq1[l].astype(jnp.float32) * diff_lk1[l].astype(jnp.float32)))
               - jnp.exp(jnp.sum(diff_lq2[l].astype(jnp.float32) * diff_lk2[l].astype(jnp.float32)))
               + lam_init)
        dq = rms_norm(dq.reshape(B, S, DIFF_HEADS, 2, DIFF_QK_DIM), diff_qn[l]).transpose(0, 2, 3, 1, 4)
        dk = rms_norm(dk.reshape(B, S, DIFF_HEADS, 2, DIFF_QK_DIM), diff_kn[l]).transpose(0, 2, 3, 1, 4)
        dq = partial_rope(dq, cos32, sin32)
        dk = partial_rope(dk, cos32, sin32)
        dv = dv.reshape(B, S, DIFF_HEADS, DIFF_V_DIM).transpose(0, 2, 1, 3)
        o_diff = diff_attention(dq, dk, dv, lam)
        o_diff = (rms_norm(o_diff, diff_subln[l]) * (1.0 - lam_init)).reshape(B, S, DIFF_HEADS * DIFF_V_DIM)

        sq = partial_rope(rms_norm(sq.reshape(B, S, DSA_HEADS, HEAD_DIM), dsa_qn[l]).transpose(0, 2, 1, 3), cos64, sin64)
        sk = partial_rope(rms_norm(sk, dsa_kn[l]), cos64, sin64)
        iq = partial_rope(iq.reshape(B, S, IDX_HEADS, IDX_DIM).transpose(0, 2, 1, 3), cos64, sin64)
        ik = partial_rope(ik, cos64, sin64)
        iw = iw * (IDX_HEADS ** -0.5)
        o_dsa = dsa_attention(sq, sk, sv, iq, ik, iw, topk).reshape(B, S, DSA_HEADS * HEAD_DIM)

        x = x + jnp.concatenate([o_fox, o_diff, o_dsa], axis=-1) @ w_out[l]

        h = rms_norm(x, ffn_norm[l])
        gate, up = jnp.split(h @ w_gate_up[l], 2, axis=-1)
        x = x + (jax.nn.silu(gate) * up) @ w_down[l]
    return x


DEPTH_2 = 1

CHUNK = 64
LEFT_CHUNKS = 8
BAND = LEFT_CHUNKS + 1
ATTN_HEADS = 8
D_ATTN = ATTN_HEADS * HEAD_DIM
MAX_REL = 256
REL_FUTURE = CHUNK - 1
N_REL = REL_FUTURE + MAX_REL + 1
D_SSM = D_MODEL // 2
SSM_GROUP = 16
SSM_GROUPS = D_SSM // SSM_GROUP
SSM_STATE = 64
STEP_MIN = 0.001
STEP_MAX = 0.1
N_BRANCH = 2
D_IN = 3 * D_ATTN + D_SSM + N_BRANCH * D_MODEL
N_GROUPS = 4
EXPERTS_PER_GROUP = 4
N_EXPERTS = N_GROUPS * EXPERTS_PER_GROUP
TOP_K = 2
D_EXPERT = D_MODEL // 4
EPS = 1e-6
NEG_INF = -1e30


def rms_norm_2(x, gain):
    xf = x.astype(jnp.float32)
    y = xf * lax.rsqrt(jnp.mean(xf * xf, axis=-1, keepdims=True) + EPS)
    return (y * gain.astype(jnp.float32)).astype(x.dtype)

def chunked_relpos_attention(q, k, v, q_gain, k_gain, rel_bias):
    b, l = q.shape[0], q.shape[1]
    nc = l // CHUNK
    q = rms_norm_2(q, q_gain)
    k = rms_norm_2(k, k_gain)
    pad = ((0, 0), (LEFT_CHUNKS * CHUNK, 0), (0, 0), (0, 0))
    kp = jnp.pad(k, pad).reshape(b, nc + LEFT_CHUNKS, CHUNK, ATTN_HEADS, HEAD_DIM)
    vp = jnp.pad(v, pad).reshape(b, nc + LEFT_CHUNKS, CHUNK, ATTN_HEADS, HEAD_DIM)
    band = jnp.arange(nc)[:, None] + jnp.arange(BAND)[None, :]
    kb = kp[:, band].reshape(b, nc, BAND * CHUNK, ATTN_HEADS, HEAD_DIM)
    vb = vp[:, band].reshape(b, nc, BAND * CHUNK, ATTN_HEADS, HEAD_DIM)
    qc = q.reshape(b, nc, CHUNK, ATTN_HEADS, HEAD_DIM)
    s = jnp.einsum('bnqhd,bnkhd->bhnqk', qc, kb).astype(jnp.float32) * (HEAD_DIM ** -0.5)
    q_off = jnp.arange(CHUNK)[:, None] + LEFT_CHUNKS * CHUNK
    k_off = jnp.arange(BAND * CHUNK)[None, :]
    rel_idx = jnp.clip(q_off - k_off, -REL_FUTURE, MAX_REL) + REL_FUTURE
    bias = rel_bias.astype(jnp.float32)[:, rel_idx]
    key_pos = (jnp.arange(nc)[:, None] - LEFT_CHUNKS) * CHUNK + k_off
    valid = key_pos >= 0
    s = jnp.where(valid[None, None, :, None, :], s + bias[None, :, None], NEG_INF)
    p = jax.nn.softmax(s, axis=-1).astype(v.dtype)
    o = jnp.einsum('bhnqk,bnkhd->bnqhd', p, vb)
    return o.reshape(b, l, D_ATTN)

def _complex_linear_combine(e1, e2):
    a1r, a1i, b1r, b1i = e1
    a2r, a2i, b2r, b2i = e2
    ar = a2r * a1r - a2i * a1i
    ai = a2r * a1i + a2i * a1r
    br = a2r * b1r - a2i * b1i + b2r
    bi = a2r * b1i + a2i * b1r + b2i
    return (ar, ai, br, bi)

def s5_ssm_glu(u, lambda_re, lambda_im, log_step, b_re, b_im, c_re, c_im, d_skip, w_glu, b_glu):
    bsz, l = u.shape[0], u.shape[1]
    uf = u.astype(jnp.float32).reshape(bsz, l, SSM_GROUPS, SSM_GROUP)
    lre = lambda_re.astype(jnp.float32)
    lim = lambda_im.astype(jnp.float32)
    step = jnp.exp(log_step.astype(jnp.float32))[:, None]
    mag = jnp.exp(lre * step)
    ang = lim * step
    a_re = mag * jnp.cos(ang)
    a_im = mag * jnp.sin(ang)
    num_re = a_re - 1.0
    num_im = a_im
    den = lre * lre + lim * lim
    f_re = (num_re * lre + num_im * lim) / den
    f_im = (num_im * lre - num_re * lim) / den
    br = b_re.astype(jnp.float32)
    bi = b_im.astype(jnp.float32)
    bb_re = f_re[..., None] * br - f_im[..., None] * bi
    bb_im = f_re[..., None] * bi + f_im[..., None] * br
    bu_re = jnp.einsum('blgc,gpc->blgp', uf, bb_re)
    bu_im = jnp.einsum('blgc,gpc->blgp', uf, bb_im)
    a_re_t = jnp.broadcast_to(a_re[None, None], (1, l, SSM_GROUPS, SSM_STATE))
    a_im_t = jnp.broadcast_to(a_im[None, None], (1, l, SSM_GROUPS, SSM_STATE))
    _, _, s_re, s_im = lax.associative_scan(
        _complex_linear_combine, (a_re_t, a_im_t, bu_re, bu_im), axis=1)
    y = (jnp.einsum('blgp,gcp->blgc', s_re, c_re.astype(jnp.float32))
         - jnp.einsum('blgp,gcp->blgc', s_im, c_im.astype(jnp.float32))
         + d_skip.astype(jnp.float32).reshape(SSM_GROUPS, SSM_GROUP) * uf)
    y = y.reshape(bsz, l, D_SSM).astype(u.dtype)
    z = jax.nn.gelu(y)
    return z * jax.nn.sigmoid(z @ w_glu + b_glu)

def hierarchical_moe(h, w_group_router, group_bias, w_expert_router, expert_bias, w_e_gate, w_e_up, w_e_down):
    bsz, l, d = h.shape
    t = bsz * l
    ht = h.reshape(t, d)
    group_logits = (ht @ w_group_router).astype(jnp.float32) + group_bias.astype(jnp.float32)
    group_prob = jax.nn.softmax(group_logits, axis=-1)
    g_prob, g_idx = lax.top_k(group_prob, 1)
    expert_logits = (ht @ w_expert_router).astype(jnp.float32) + expert_bias.astype(jnp.float32)
    expert_logits = expert_logits.reshape(t, N_GROUPS, EXPERTS_PER_GROUP)
    in_group = jnp.take_along_axis(expert_logits, g_idx[:, :, None], axis=1)[:, 0]
    e_prob = jax.nn.softmax(in_group, axis=-1)
    e_val, e_loc = lax.top_k(e_prob, TOP_K)
    e_val = e_val / jnp.sum(e_val, axis=-1, keepdims=True)
    weights = g_prob * e_val
    e_glob = g_idx * EXPERTS_PER_GROUP + e_loc
    gates = jnp.sum(jax.nn.one_hot(e_glob, N_EXPERTS, dtype=jnp.float32) * weights[..., None], axis=1)
    gates = gates.astype(h.dtype)
    a = jnp.einsum('td,edf->tef', ht, w_e_gate)
    u = jnp.einsum('td,edf->tef', ht, w_e_up)
    hid = jax.nn.silu(a) * u * gates[:, :, None]
    out = hid.reshape(t, N_EXPERTS * D_EXPERT) @ w_e_down.reshape(N_EXPERTS * D_EXPERT, d)
    return out.reshape(bsz, l, d)

def second_inputs(seed: int = 0) -> dict:
    key = jax.random.key(seed)
    ks = jax.random.split(key, 32)
    f32 = jnp.float32

    def nrm(k, shape, scale):
        return jax.random.normal(k, shape, f32) * scale

    n_idx = jnp.arange(SSM_STATE, dtype=f32)
    return {
        'x': nrm(ks[0], (BATCH, SEQ, D_MODEL), 1.0),
        'mix_norm_gain': 1.0 + nrm(ks[1], (DEPTH_2, D_MODEL), 0.02),
        'w_in': nrm(ks[2], (DEPTH_2, D_MODEL, D_IN), D_MODEL ** -0.5),
        'b_gate': nrm(ks[3], (DEPTH_2, N_BRANCH * D_MODEL), 0.02),
        'q_gain': 1.0 + nrm(ks[4], (DEPTH_2, HEAD_DIM), 0.02),
        'k_gain': 1.0 + nrm(ks[5], (DEPTH_2, HEAD_DIM), 0.02),
        'rel_bias': nrm(ks[6], (DEPTH_2, ATTN_HEADS, N_REL), 0.1),
        'ssm_lambda_re': -0.5 + nrm(ks[7], (DEPTH_2, SSM_GROUPS, SSM_STATE), 0.01),
        'ssm_lambda_im': math.pi * n_idx[None, None, :] + nrm(ks[8], (DEPTH_2, SSM_GROUPS, SSM_STATE), 0.01),
        'ssm_log_step': jax.random.uniform(ks[9], (DEPTH_2, SSM_GROUPS), f32, math.log(STEP_MIN), math.log(STEP_MAX)),
        'ssm_b_re': nrm(ks[10], (DEPTH_2, SSM_GROUPS, SSM_STATE, SSM_GROUP), (2 * SSM_GROUP) ** -0.5),
        'ssm_b_im': nrm(ks[11], (DEPTH_2, SSM_GROUPS, SSM_STATE, SSM_GROUP), (2 * SSM_GROUP) ** -0.5),
        'ssm_c_re': nrm(ks[12], (DEPTH_2, SSM_GROUPS, SSM_GROUP, SSM_STATE), (2 * SSM_STATE) ** -0.5),
        'ssm_c_im': nrm(ks[13], (DEPTH_2, SSM_GROUPS, SSM_GROUP, SSM_STATE), (2 * SSM_STATE) ** -0.5),
        'ssm_d': nrm(ks[14], (DEPTH_2, D_SSM), 1.0),
        'w_glu': nrm(ks[15], (DEPTH_2, D_SSM, D_SSM), D_SSM ** -0.5),
        'b_glu': nrm(ks[16], (DEPTH_2, D_SSM), 0.02),
        'w_branch': nrm(ks[17], (DEPTH_2, D_ATTN + D_SSM, D_MODEL), D_ATTN ** -0.5),
        'w_out': nrm(ks[18], (DEPTH_2, D_MODEL, D_MODEL), D_MODEL ** -0.5),
        'ffn_norm_gain': 1.0 + nrm(ks[19], (DEPTH_2, D_MODEL), 0.02),
        'w_group_router': nrm(ks[20], (DEPTH_2, D_MODEL, N_GROUPS), D_MODEL ** -0.5),
        'group_bias': nrm(ks[21], (DEPTH_2, N_GROUPS), 0.01),
        'w_expert_router': nrm(ks[22], (DEPTH_2, D_MODEL, N_EXPERTS), D_MODEL ** -0.5),
        'expert_bias': nrm(ks[23], (DEPTH_2, N_EXPERTS), 0.01),
        'w_e_gate': nrm(ks[24], (DEPTH_2, N_EXPERTS, D_MODEL, D_EXPERT), D_MODEL ** -0.5),
        'w_e_up': nrm(ks[25], (DEPTH_2, N_EXPERTS, D_MODEL, D_EXPERT), D_MODEL ** -0.5),
        'w_e_down': nrm(ks[26], (DEPTH_2, N_EXPERTS, D_EXPERT, D_MODEL), D_EXPERT ** -0.5),
    }

def second_block(x, mix_norm_gain, w_in, b_gate, q_gain, k_gain, rel_bias,
              ssm_lambda_re, ssm_lambda_im, ssm_log_step, ssm_b_re, ssm_b_im,
              ssm_c_re, ssm_c_im, ssm_d, w_glu, b_glu, w_branch, w_out,
              ffn_norm_gain, w_group_router, group_bias, w_expert_router, expert_bias,
              w_e_gate, w_e_up, w_e_down):
    bsz, l, _ = x.shape
    for i in range(DEPTH_2):
        h = rms_norm_2(x, mix_norm_gain[i])
        proj = h @ w_in[i]
        q = proj[..., :D_ATTN].reshape(bsz, l, ATTN_HEADS, HEAD_DIM)
        k = proj[..., D_ATTN:2 * D_ATTN].reshape(bsz, l, ATTN_HEADS, HEAD_DIM)
        v = proj[..., 2 * D_ATTN:3 * D_ATTN].reshape(bsz, l, ATTN_HEADS, HEAD_DIM)
        u = proj[..., 3 * D_ATTN:3 * D_ATTN + D_SSM]
        gate = jax.nn.sigmoid(proj[..., 3 * D_ATTN + D_SSM:] + b_gate[i])
        gate = gate.reshape(bsz, l, N_BRANCH, D_MODEL)
        y_attn = chunked_relpos_attention(q, k, v, q_gain[i], k_gain[i], rel_bias[i])
        y_ssm = s5_ssm_glu(u, ssm_lambda_re[i], ssm_lambda_im[i], ssm_log_step[i],
                           ssm_b_re[i], ssm_b_im[i], ssm_c_re[i], ssm_c_im[i],
                           ssm_d[i], w_glu[i], b_glu[i])
        wb = w_branch[i]
        merged = (gate[:, :, 0] * (y_attn @ wb[:D_ATTN])
                  + gate[:, :, 1] * (y_ssm @ wb[D_ATTN:]))
        x = x + merged @ w_out[i]
        h = rms_norm_2(x, ffn_norm_gain[i])
        x = x + hierarchical_moe(h, w_group_router[i], group_bias[i], w_expert_router[i],
                                 expert_bias[i], w_e_gate[i], w_e_up[i], w_e_down[i])
    return x


def setup_inputs(seed=0):
    out = dict(first_inputs(seed))
    for name, value in second_inputs(seed + 1).items():
        if name != "x":
            out[name + "_2"] = value
    return out


def reference(
    x, attn_norm, w_in, fox_fb, fox_qn, fox_kn, diff_qn, diff_kn, diff_lq1, diff_lk1, diff_lq2,
    diff_lk2, diff_subln, dsa_qn, dsa_kn, w_out, ffn_norm, w_gate_up, w_down, mix_norm_gain_2,
    w_in_2, b_gate_2, q_gain_2, k_gain_2, rel_bias_2, ssm_lambda_re_2, ssm_lambda_im_2,
    ssm_log_step_2, ssm_b_re_2, ssm_b_im_2, ssm_c_re_2, ssm_c_im_2, ssm_d_2, w_glu_2, b_glu_2,
    w_branch_2, w_out_2, ffn_norm_gain_2, w_group_router_2, group_bias_2, w_expert_router_2,
    expert_bias_2, w_e_gate_2, w_e_up_2, w_e_down_2,
):
    x = first_block(
        x, attn_norm, w_in, fox_fb, fox_qn, fox_kn, diff_qn, diff_kn, diff_lq1, diff_lk1,
        diff_lq2, diff_lk2, diff_subln, dsa_qn, dsa_kn, w_out, ffn_norm, w_gate_up, w_down,
    )
    return second_block(
        x, mix_norm_gain_2, w_in_2, b_gate_2, q_gain_2, k_gain_2, rel_bias_2, ssm_lambda_re_2,
        ssm_lambda_im_2, ssm_log_step_2, ssm_b_re_2, ssm_b_im_2, ssm_c_re_2, ssm_c_im_2,
        ssm_d_2, w_glu_2, b_glu_2, w_branch_2, w_out_2, ffn_norm_gain_2, w_group_router_2,
        group_bias_2, w_expert_router_2, expert_bias_2, w_e_gate_2, w_e_up_2, w_e_down_2,
    )


_drawn_inputs = setup_inputs


def setup_inputs(seed=0):
    import zlib

    import numpy as np

    out = dict(_drawn_inputs(seed))
    spreads = {}
    factors = {'fox_qn': 5.565,
     'fox_kn': 5.888,
     'diff_qn': 3.655,
     'diff_kn': 3.068,
     'diff_subln': 3.412,
     'dsa_qn': 8.0,
     'dsa_kn': 5.714,
     'mix_norm_gain_2': 3.372,
     'b_gate_2': 5.967,
     'q_gain_2': 8.0,
     'k_gain_2': 8.0,
     'rel_bias_2': 3.531,
     'ssm_lambda_re_2': 64.0,
     'ssm_lambda_im_2': 3.157,
     'ssm_b_re_2': 3.153,
     'ssm_b_im_2': 3.804,
     'ssm_c_re_2': 3.437,
     'ssm_c_im_2': 3.564,
     'b_glu_2': 26.963,
     'group_bias_2': 35.522,
     'expert_bias_2': 36.451,
     'ffn_norm_gain_2': 5.537}
    for name, (base, spread) in spreads.items():
        noise = np.random.default_rng([zlib.crc32(name.encode()), seed]).standard_normal(out[name].shape)
        drawn = base * np.exp(spread * noise) if base else spread * noise
        out[name] = __import__('jax').numpy.asarray(drawn.astype(out[name].dtype))
    for name, factor in factors.items():
        out[name] = (out[name] * factor).astype(out[name].dtype)
    return out
```

```python
import math
from contextlib import ExitStack

import concourse.bass as bass
from concourse import mybir

F32 = mybir.dt.float32
F32R = mybir.dt.float32r
ALU = mybir.AluOpType
ACT = mybir.ActivationFunctionType
AX = mybir.AxisListType.X

P = 128
SEQ = 512
TB = SEQ // P
D = 1024
KD = D // P
DEPTH = 2
NORM_EPS = 1e-6
NEG = -1e30
TAKEN = -3e38
TAKEN_EDGE = -2e38

HEAD = 64
FOX = 6
DIFF = 4
DIFF_D = 32
DSA = 6
IDX = 4
TOPK = min(256, SEQ // 4)
SPLITS = (FOX * HEAD, FOX * HEAD, FOX * HEAD, FOX, DIFF * 2 * DIFF_D, DIFF * 2 * DIFF_D, DIFF * HEAD,
          DSA * HEAD, HEAD, HEAD, IDX * HEAD, HEAD, IDX)
FQ, FK, FV, FF, DQ, DK, DV, SQ, SK, SV, IQ, IK, IW = (sum(SPLITS[:n]) for n in range(len(SPLITS)))
IN_WIDTH = sum(SPLITS)
IN_CHUNKS = 6
IN_COLS = -(-IN_WIDTH // (2 * IN_CHUNKS)) * 2
OUT_COLS = 512
OUT_CHUNKS = D // OUT_COLS
HID = 256
HB = HID // P
FFN = -(-8 * D // (3 * 256)) * 256
FFN_GROUPS = FFN // HID

HEADS2 = 8
ATTN2 = HEADS2 * HEAD
REL_FUTURE = 63
MAX_REL = 256
SSM = D // 2
GROUPS, GROUP, STATE = 32, 16, 64
ST = GROUPS * STATE // P
SQT = SSM // P
PER = ST // SQT
QKV_COLS, QKV_CHUNKS = 384, 4
FEAT_COLS = 256
MOE_G, MOE_E = 4, 4
EXPERTS = MOE_G * MOE_E
ROUTES = MOE_G + EXPERTS

C_ID, C_TRI, C_ONE, C_CAUSAL, C_CHUNK, C_ROPE = 0, P, 2 * P, 3 * P, 4 * P, 5 * P
ROPE64, ROPE32 = HEAD // 8, DIFF_D // 8
ROPE_COLS = 2 * ROPE64 + 2 * ROPE32
C_FOX = C_ROPE + TB * ROPE_COLS
C_RANK = C_FOX + 1
C_COLS = C_RANK + 4

PARAMS = (("fox_qn", HEAD), ("fox_kn", HEAD), ("diff_qn", DIFF_D), ("diff_kn", DIFF_D),
          ("diff_lq1", DIFF_D), ("diff_lk1", DIFF_D), ("diff_lq2", DIFF_D), ("diff_lk2", DIFF_D),
          ("diff_subln", HEAD), ("dsa_qn", HEAD), ("dsa_kn", HEAD), ("fox_fb", FOX))
PAR = {name: sum(n for _, n in PARAMS[:i]) for i, (name, _) in enumerate(PARAMS)}
PAR_COLS = sum(n for _, n in PARAMS)

U_FQ, U_FK, U_DQ, U_DK, U_SQ, U_SK, U_IQ, U_IK = 0, 6, 12, 20, 28, 34, 35, 39
UNITS = 40


class Core:

    def __init__(self, nc, ctx):
        self.nc, self.ctx = nc, ctx

    def sb(self, name, shape, dt=F32, ctx=None):
        return (ctx or self.ctx).enter_context(self.nc.sbuf_tensor(name, shape, dt))

    def psum(self, name, shape, ctx):
        return ctx.enter_context(self.nc.psum_tensor(name, shape, F32))

    def sem(self, name, ctx):
        s = ctx.enter_context(self.nc.semaphore(name))
        self.to_clear.append(s)
        return s

    def clear(self):
        for s in self.to_clear:
            self.nc.gpsimd.sem_clear(s)
        self.to_clear = []
        self.nc.all_engine_barrier()

    to_clear = []


def chained(engine, sem):
    count = [0]

    def link(ins):
        count[0] += 1
        ins.then_inc(sem, 1)
        engine.wait_ge(sem, count[0])

    return link


def pairs(engine, n, step, peel_last=False):
    step(0, 0, True)
    step(1, 1, True)
    turns = (n - (4 if peel_last else 2)) // 2
    if turns > 0:
        with engine.Fori(0, turns) as turn:
            step(2 * turn + 2, 0, False)
            step(2 * turn + 3, 1, False)
    for i in range(2 + 2 * max(turns, 0), n):
        step(i, i % 2, False)


def transpose_split(core, name, src, hi, lo, tiles, gain=None, gain_dram=None, norm=False):
    nc = core.nc
    with ExitStack() as st:
        scratch = core.sb(f"{name}_squares", [P, D], ctx=st)
        xs = core.sb(f"{name}_normed", [P, TB, D], ctx=st) if norm else src
        ss = core.sb(f"{name}_ss", [P, TB], ctx=st)
        rstd = core.sb(f"{name}_rstd", [P, TB], ctx=st)
        half = core.sb(f"{name}_half", [P, TB], ctx=st)
        banks = [core.psum(f"{name}_ps{b}", [P, SEQ], st) for b in range(4)]
        gain_in = core.sem(f"{name}_gain_in", st)
        squared = core.sem(f"{name}_squared", st)
        rooted = core.sem(f"{name}_rooted", st)
        scaled = core.sem(f"{name}_scaled", st)
        turned = core.sem(f"{name}_turned", st)
        hi_done = core.sem(f"{name}_hi_done", st)
        lo_done = core.sem(f"{name}_lo_done", st)
        ident = core.const[:, C_ID:C_ID + P]
        with nc.Block() as block:
            if gain is not None:
                @block.sync
                def _(sp):
                    sp.dma_start(gain[:], gain_dram).then_inc(gain_in, 16)

            if norm:
                @block.gpsimd
                def _(pool):
                    nc.gpsimd.memset(half[:], -0.5).then_inc(rooted, 1)
                    pool.wait_ge(squared, TB)
                    nc.gpsimd.tensor_scalar(ss[:], ss[:], 1.0 / D, NORM_EPS, ALU.mult, ALU.add).then_inc(rooted, 1)
                    pool.wait_ge(rooted, 2)
                    nc.gpsimd.tensor_tensor(rstd[:], ss[:], half[:], ALU.pow).then_inc(rooted, 1)

            @block.scalar
            def _(act):
                if norm:
                    for t in range(TB):
                        if t:
                            act.wait_ge(squared, t)
                        nc.scalar.activation(scratch[:], src[:, t, :], ACT.Square,
                                             accum_out=ss[:, t:t + 1]).then_inc(squared, 1)
                if gain is not None:
                    act.wait_ge(gain_in, 16)
                for k in range(tiles):
                    act.wait_ge(turned, k + 1)
                    if gain is None:
                        nc.scalar.copy(hi[:, k, :], banks[k % 4][:]).then_inc(hi_done, 1)
                    else:
                        nc.scalar.activation(hi[:, k, :], banks[k % 4][:], ACT.Copy,
                                             scale=gain[:, k:k + 1]).then_inc(hi_done, 1)

            @block.vector
            def _(dve):
                if norm:
                    dve.wait_ge(rooted, 3)
                    for t in range(TB):
                        nc.vector.tensor_scalar(xs[:, t, :], src[:, t, :], rstd[:, t:t + 1], None,
                                                ALU.mult).then_inc(scaled, 1)
                if gain is not None:
                    dve.wait_ge(gain_in, 16)
                for k in range(tiles):
                    dve.wait_ge(hi_done, k + 1)
                    hi_k = hi[:, k, :].bitcast(F32)
                    if gain is None:
                        nc.vector.tensor_tensor(lo[:, k, :], banks[k % 4][:], hi_k, ALU.subtract).then_inc(lo_done, 1)
                    else:
                        nc.vector.scalar_tensor_tensor(lo[:, k, :], banks[k % 4][:], gain[:, k:k + 1], hi_k,
                                                       ALU.mult, ALU.subtract).then_inc(lo_done, 1)

            @block.tensor
            def _(pe):
                for k in range(tiles):
                    if k >= 4:
                        pe.wait_ge(lo_done, k - 3)
                    for t in range(TB):
                        if norm and k == 0:
                            pe.wait_ge(scaled, t + 1)
                        last = nc.tensor.transpose(banks[k % 4][:, t * P:(t + 1) * P],
                                                   xs[:, t, k * P:(k + 1) * P], ident)
                    last.then_inc(turned, 1)


def project(core, name, hi, lo, w_dram, chunks, cols, by_token=None, by_feature=None, by_feature_dve=None, kd=KD):
    nc = core.nc
    tiles = TB if by_token else cols // P
    width = cols if by_token else SEQ
    with ExitStack() as st:
        raw = [core.sb(f"{name}_raw{s}", [P, kd, cols], ctx=st) for s in range(2)]
        whi = [core.sb(f"{name}_whi{s}", [P, kd, cols], F32R, ctx=st) for s in range(2)]
        wlo = [core.sb(f"{name}_wlo{s}", [P, kd, cols], F32R, ctx=st) for s in range(2)]
        banks = [[core.psum(f"{name}_ps{s}{t}", [P, 512], st) for t in range(tiles)] for s in range(2)]
        loaded = [core.sem(f"{name}_loaded{s}", st) for s in range(2)]
        hi_done = core.sem(f"{name}_whi_done", st)
        lo_done = core.sem(f"{name}_wlo_done", st)
        summed = core.sem(f"{name}_summed", st)
        out_done = core.sem(f"{name}_out_done", st)
        H = kd // 2

        with nc.Block() as block:
            @block.sync
            def _(sp):
                def step(c, s, first):
                    if not first:
                        sp.wait_ge(lo_done, 2 * (c - 1))
                    sp.dma_start(raw[s][:].rearrange("p k n -> p (k n)"), w_dram(c)).then_inc(loaded[s], 16)
                pairs(sp, chunks, step)

            def split_hi(act, c, s, first):
                act.wait_ge(loaded[s], 16 * (c // 2) + 16)
                if not first:
                    act.wait_ge(summed, tiles * (c - 1))
                for h in range(2):
                    nc.scalar.copy(whi[s][:, h * H:(h + 1) * H, :], raw[s][:, h * H:(h + 1) * H, :]).then_inc(hi_done, 1)

            def split_lo(dve, c, s, first):
                if not first:
                    dve.wait_ge(summed, tiles * (c - 1))
                for h in range(2):
                    dve.wait_ge(hi_done, 2 * c + h + 1)
                    nc.vector.tensor_tensor(wlo[s][:, h * H:(h + 1) * H, :], raw[s][:, h * H:(h + 1) * H, :],
                                            whi[s][:, h * H:(h + 1) * H, :].bitcast(F32),
                                            ALU.subtract).then_inc(lo_done, 1)

            def take_out(engine, emit, c, s):
                for t in range(tiles):
                    engine.wait_ge(summed, tiles * c + t + 1)
                    emit(c, t, banks[s][t][:, 0:width]).then_inc(out_done, 1)

            @block.scalar
            def _(act):
                def step(c, s, first):
                    split_hi(act, c, s, first)
                    if by_feature and not (isinstance(c, int) and c == 0):
                        take_out(act, by_feature, c - 1, 1 - s)
                pairs(act, chunks, step)
                if by_feature:
                    take_out(act, by_feature, chunks - 1, (chunks - 1) % 2)

            @block.vector
            def _(dve):
                emit = by_token or by_feature_dve

                def step(c, s, first):
                    split_lo(dve, c, s, first)
                    if emit and not (isinstance(c, int) and c == 0):
                        take_out(dve, emit, c - 1, 1 - s)
                pairs(dve, chunks, step)
                if emit:
                    take_out(dve, emit, chunks - 1, (chunks - 1) % 2)

            @block.tensor
            def _(pe):
                def step(c, s, first):
                    for t in range(tiles):
                        if not first:
                            pe.wait_ge(out_done, tiles * (c - 2) + t + 1)
                        n = 0
                        for k in range(kd):
                            if t == 0 and k % H == 0:
                                pe.wait_ge(lo_done, 2 * c + k // H + 1)
                            for aw, ww in ((hi, whi[s]), (lo, whi[s]), (hi, wlo[s])):
                                if by_token:
                                    ops = aw[:, k, t * P:(t + 1) * P], ww[:, k, :]
                                else:
                                    ops = ww[:, k, t * P:(t + 1) * P], aw[:, k, :]
                                last = nc.tensor.matmul(banks[s][t][:, 0:width], *ops, start=n == 0, stop=n == 3 * kd - 1)
                                n += 1
                        last.then_inc(summed, 1)
                pairs(pe, chunks, step)


def add_to_x(core, c, t, sums, cols):
    x_ct = core.x[:, t, bass.ds(c * cols, cols)]
    return core.nc.vector.tensor_tensor(x_ct, sums, x_ct, ALU.add)


def split(core, name, a, hi, lo, tiles, b=None, op=None, res=None):
    nc = core.nc
    with ExitStack() as st:
        made = core.sem(f"{name}_made", st)
        hi_done = core.sem(f"{name}_hi_done", st)
        lo_done = core.sem(f"{name}_lo_done", st)
        full = a if b is None else res
        with nc.Block() as block:
            @block.scalar
            def _(act):
                for k in range(tiles):
                    if b is not None:
                        act.wait_ge(made, k + 1)
                    nc.scalar.copy(hi[:, k, :], full[:, k, :]).then_inc(hi_done, 1)

            @block.vector
            def _(dve):
                if b is not None:
                    for k in range(tiles):
                        nc.vector.tensor_tensor(full[:, k, :], a[:, k, :], b[:, k, :], op).then_inc(made, 1)
                for k in range(tiles):
                    dve.wait_ge(hi_done, k + 1)
                    nc.vector.tensor_tensor(lo[:, k, :], full[:, k, :], hi[:, k, :].bitcast(F32),
                                            ALU.subtract).then_inc(lo_done, 1)


def feed_forward(core, name, hi, lo, groups, gate_dram, up_dram, down_dram, weight=None):
    nc = core.nc
    x = core.x
    KH = KD // 2
    with ExitStack() as st:
        raw_gu = core.sb(f"{name}_raw_gu", [P, 2, KD, HID], ctx=st)
        raw_d = core.sb(f"{name}_raw_d", [P, HB, D], ctx=st)
        gu_hi = [core.sb(f"{name}_gu_hi{s}", [P, 2, KD, HID], F32R, ctx=st) for s in range(2)]
        gu_lo = [core.sb(f"{name}_gu_lo{s}", [P, 2, KD, HID], F32R, ctx=st) for s in range(2)]
        d_hi = [core.sb(f"{name}_d_hi{s}", [P, HB, D], F32R, ctx=st) for s in range(2)]
        d_lo = [core.sb(f"{name}_d_lo{s}", [P, HB, D], F32R, ctx=st) for s in range(2)]
        act_t = core.sb(f"{name}_silu", [P, HB, SEQ], ctx=st)
        hid_hi = [core.sb(f"{name}_hid_hi{s}", [P, HB, SEQ], F32R, ctx=st) for s in range(2)]
        hid_lo = [core.sb(f"{name}_hid_lo{s}", [P, HB, SEQ], F32R, ctx=st) for s in range(2)]
        up_ps = [[core.psum(f"{name}_up{m}{b}", [P, SEQ], st) for b in range(HB)] for m in range(2)]
        down_ps = [core.psum(f"{name}_down{b}", [P, 512], st) for b in range(4)]
        gate_in = core.sem(f"{name}_gate_in", st)
        up_in = core.sem(f"{name}_up_in", st)
        down_in = core.sem(f"{name}_down_in", st)
        hi_done = core.sem(f"{name}_w_hi_done", st)
        lo_done = core.sem(f"{name}_w_lo_done", st)
        up_sum = core.sem(f"{name}_up_sum", st)
        down_sum = core.sem(f"{name}_down_sum", st)
        silu_done = core.sem(f"{name}_silu_done", st)
        prod_done = core.sem(f"{name}_prod_done", st)
        hid_hi_done = core.sem(f"{name}_hid_hi_done", st)
        hid_lo_done = core.sem(f"{name}_hid_lo_done", st)
        added = core.sem(f"{name}_added", st)
        NT = TB * (D // 512)

        with nc.Block() as block:
            @block.sync
            def _(sp):
                def step(g, s, first):
                    start = isinstance(g, int) and g == 0
                    for m, (dst, src, sem) in enumerate((
                            (raw_gu[:, 0], gate_dram, gate_in), (raw_gu[:, 1], up_dram, up_in),
                            (raw_d[:], down_dram, down_in))):
                        if not start:
                            sp.wait_ge(lo_done, 3 * (g - 1) + m + 1)
                        sp.dma_start(dst.rearrange("p k n -> p (k n)"), src(g)).then_inc(sem, 16)
                pairs(sp, groups, step)

            def parts(s):
                return ((raw_gu[:, 0], gu_hi[s][:, 0], gu_lo[s][:, 0]), (raw_gu[:, 1], gu_hi[s][:, 1], gu_lo[s][:, 1]),
                        (raw_d[:], d_hi[s][:], d_lo[s][:]))

            @block.scalar
            def _(act):
                def hidden(g, s):
                    for b in range(HB):
                        act.wait_ge(up_sum, 2 * HB * g + 2 * b + 2)
                        if not (isinstance(g, int) and g == 0):
                            act.wait_ge(hid_lo_done, HB * (g - 1) + b + 1)
                        nc.scalar.activation(act_t[:, b, :], up_ps[0][b][:], ACT.Silu).then_inc(silu_done, 1)
                    for b in range(HB):
                        act.wait_ge(prod_done, HB * g + b + 1)
                        nc.scalar.copy(hid_hi[s][:, b, :], act_t[:, b, :]).then_inc(hid_hi_done, 1)

                def split(g, s, m, sem):
                    raw, hi_w, _ = parts(s)[m]
                    act.wait_ge(sem, 16 * (g + 1))
                    nc.scalar.copy(hi_w, raw).then_inc(hi_done, 1)

                def step(g, s, first):
                    if not first:
                        act.wait_ge(up_sum, 2 * HB * (g - 1))
                    split(g, s, 0, gate_in)
                    split(g, s, 1, up_in)
                    if not (isinstance(g, int) and g == 0):
                        hidden(g - 1, 1 - s)
                    if not first:
                        act.wait_ge(down_sum, NT * (g - 1))
                    split(g, s, 2, down_in)
                pairs(act, groups, step)
                hidden(groups - 1, (groups - 1) % 2)

            @block.vector
            def _(dve):
                def hidden(g, s):
                    for b in range(HB):
                        dve.wait_ge(silu_done, HB * g + b + 1)
                        nc.vector.tensor_tensor(act_t[:, b, :], act_t[:, b, :], up_ps[1][b][:],
                                                ALU.mult).then_inc(prod_done, 1)
                    for b in range(HB):
                        dve.wait_ge(hid_hi_done, HB * g + b + 1)
                        nc.vector.tensor_tensor(hid_lo[s][:, b, :], act_t[:, b, :], hid_hi[s][:, b, :].bitcast(F32),
                                                ALU.subtract).then_inc(hid_lo_done, 1)

                def add(g):
                    for n in range(NT):
                        t, c = n // 2, n % 2
                        x_nt = x[:, t, c * 512:(c + 1) * 512]
                        dve.wait_ge(down_sum, NT * g + n + 1)
                        if weight is None:
                            nc.vector.tensor_tensor(x_nt, down_ps[n % 4][:], x_nt, ALU.add).then_inc(added, 1)
                        else:
                            nc.vector.scalar_tensor_tensor(x_nt, down_ps[n % 4][:], weight(t, g), x_nt,
                                                           ALU.mult, ALU.add).then_inc(added, 1)

                def split(g, s, m):
                    raw, hi_w, lo_w = parts(s)[m]
                    dve.wait_ge(hi_done, 3 * g + m + 1)
                    nc.vector.tensor_tensor(lo_w, raw, hi_w.bitcast(F32), ALU.subtract).then_inc(lo_done, 1)

                def step(g, s, first):
                    if not first:
                        dve.wait_ge(up_sum, 2 * HB * (g - 1))
                    split(g, s, 0)
                    split(g, s, 1)
                    if not (isinstance(g, int) and g == 0):
                        hidden(g - 1, 1 - s)
                    if not first:
                        add(g - 2)
                    split(g, s, 2)
                pairs(dve, groups, step)
                hidden(groups - 1, (groups - 1) % 2)
                add(groups - 2)
                add(groups - 1)

            @block.tensor
            def _(pe):
                def up(g, s):
                    if not (isinstance(g, int) and g == 0):
                        pe.wait_ge(prod_done, HB * g)
                    for b in range(HB):
                        for m in range(2):
                            if b == 0:
                                pe.wait_ge(lo_done, 3 * g + m + 1)
                            n = 0
                            for k in range(KD):
                                for ww, aw in ((gu_hi[s], hi), (gu_hi[s], lo), (gu_lo[s], hi)):
                                    last = nc.tensor.matmul(up_ps[m][b][:], ww[:, m, k, b * P:(b + 1) * P], aw[:, k, :],
                                                            start=n == 0, stop=n == 3 * KD - 1)
                                    n += 1
                            last.then_inc(up_sum, 1)

                def down(g, s):
                    pe.wait_ge(lo_done, 3 * g + 3)
                    pe.wait_ge(hid_lo_done, HB * g + HB)
                    for n in range(NT):
                        t, c = n // 2, n % 2
                        if not (isinstance(g, int) and g == 0) or n >= 4:
                            pe.wait_ge(added, NT * g + n - 3)
                        i = 0
                        for k in range(HB):
                            for aw, ww in ((hid_hi[s], d_hi[s]), (hid_lo[s], d_hi[s]), (hid_hi[s], d_lo[s])):
                                last = nc.tensor.matmul(down_ps[n % 4][:], aw[:, k, t * P:(t + 1) * P],
                                                        ww[:, k, c * 512:(c + 1) * 512], start=i == 0, stop=i == 3 * HB - 1)
                                i += 1
                        last.then_inc(down_sum, 1)

                def step(g, s, first):
                    up(g, s)
                    if not (isinstance(g, int) and g == 0):
                        down(g - 1, 1 - s)
                pairs(pe, groups, step)
                down(groups - 1, (groups - 1) % 2)


def attention(core, name, heads, rows, q_of, k_of, v_of, scale, bias_of, out_of, bias_dram=None):
    nc = core.nc
    with ExitStack() as st:
        q_slot = [core.sb(f"{name}_q{s}", [rows, SEQ], ctx=st) for s in range(2)]
        prob = [core.sb(f"{name}_p{i}", [P, (i + 1) * P], ctx=st) for i in range(TB)]
        prob_t = [core.sb(f"{name}_pt{s}", [P, SEQ], ctx=st) for s in range(2)]
        neg_max = core.sb(f"{name}_neg_max", [P, TB], ctx=st)
        row_sum = [core.sb(f"{name}_row_sum{s}", [P, TB], ctx=st) for s in range(2)]
        inv_sum = core.sb(f"{name}_inv_sum", [P, TB], ctx=st)
        bias_slot = [core.sb(f"{name}_bias{s}", [P, SEQ], ctx=st) for s in range(2)] if bias_dram else None
        s_ps = [core.psum(f"{name}_s{i}", [P, SEQ], st) for i in range(TB)]
        t_ps = [core.psum(f"{name}_t{s}", [P, SEQ], st) for s in range(2)]
        o_ps = [core.psum(f"{name}_o{s}", [P, HEAD], st) for s in range(2)]
        q_ready = core.sem(f"{name}_q_ready", st)
        bias_in = [core.sem(f"{name}_bias_in{s}", st) for s in range(2)]
        scored = core.sem(f"{name}_scored", st)
        maxed = core.sem(f"{name}_maxed", st)
        exped = core.sem(f"{name}_exped", st)
        turned = core.sem(f"{name}_turned", st)
        pt_dve = core.sem(f"{name}_pt_dve", st)
        pt_act = core.sem(f"{name}_pt_act", st)
        valued = core.sem(f"{name}_valued", st)
        inverted = core.sem(f"{name}_inverted", st)
        stored = core.sem(f"{name}_stored", st)
        ident = core.const[:, C_ID:C_ID + P]

        def zero(j):
            return isinstance(j, int) and j == 0

        with nc.Block() as block:
            if bias_dram:
                @block.sync
                def _(sp):
                    def step(j, s, first):
                        if not first:
                            sp.wait_ge(scored, TB * (j - 1))
                        sp.dma_start(bias_slot[s][:], bias_dram(j)).then_inc(bias_in[s], 16)
                    pairs(sp, heads, step)

            @block.scalar
            def _(act):
                def load_q(j, s, first):
                    if not first:
                        act.wait_ge(scored, TB * (j - 1))
                    nc.scalar.activation(q_slot[s][:], q_of(j), ACT.Copy, scale=scale).then_inc(q_ready, 1)

                def exps(j, s):
                    for i in range(TB):
                        act.wait_ge(maxed, TB * j + i + 1)
                        if not zero(j):
                            act.wait_ge(turned, TB * (j - 1) + i + 1)
                            if i == 0:
                                act.wait_ge(inverted, j - 1)
                        nc.scalar.activation(prob[i][:], s_ps[i][:, 0:(i + 1) * P], ACT.Exp, bias=neg_max[:, i:i + 1],
                                             accum_out=row_sum[s][:, i:i + 1]).then_inc(exped, 1)

                def copy_pt(j):
                    act.wait_ge(turned, TB * j + TB)
                    act.wait_ge(valued, TB * j + TB - 2)
                    nc.scalar.copy(prob_t[(TB - 1) % 2][:], t_ps[(TB - 1) % 2][:]).then_inc(pt_act, 1)

                load_q(0, 0, True)

                def step(j, s, first):
                    if not (isinstance(j, int) and j == heads - 1):
                        load_q(j + 1, 1 - s, zero(j))
                    exps(j, s)
                    if not zero(j):
                        copy_pt(j - 1)
                pairs(act, heads, step, peel_last=True)
                copy_pt(heads - 1)

            @block.vector
            def _(dve):
                def maxima(j, i):
                    dve.wait_ge(scored, TB * j + i + 1)
                    nc.vector.tensor_reduce(neg_max[:, i:i + 1], s_ps[i][:, 0:(i + 1) * P], AX, ALU.max,
                                            negate=True).then_inc(maxed, 1)

                def copy_pt(j, i):
                    dve.wait_ge(turned, TB * j + i + 1)
                    if not zero(j) or i >= 2:
                        dve.wait_ge(valued, TB * j + i - 1)
                    w = (i + 1) * P
                    nc.vector.tensor_copy(prob_t[i % 2][:, 0:w], t_ps[i % 2][:, 0:w]).then_inc(pt_dve, 1)

                def store(j, i):
                    dve.wait_ge(valued, TB * j + i + 1)
                    nc.vector.tensor_scalar(out_of(j, i), o_ps[i % 2][:], inv_sum[:, i:i + 1], None,
                                            ALU.mult).then_inc(stored, 1)

                def step(j, s, first, scores=True):
                    if not zero(j):
                        dve.wait_ge(exped, TB * j)
                        if not (isinstance(j, int) and j == 1):
                            dve.wait_ge(stored, TB * (j - 1))
                        nc.vector.reciprocal(inv_sum[:], row_sum[1 - s][:]).then_inc(inverted, 1)
                        dve.wait_ge(inverted, j)
                    for i in range(TB):
                        if scores:
                            maxima(j, i)
                        if not zero(j):
                            if i < TB - 1:
                                copy_pt(j - 1, i)
                            if i:
                                store(j - 1, i - 1)
                    if not zero(j):
                        store(j - 1, TB - 1)
                pairs(dve, heads, step)
                step(heads, 0, False, scores=False)

            @block.tensor
            def _(pe):
                def score(j, i, s):
                    if i == 0:
                        pe.wait_ge(q_ready, j + 1)
                        if bias_dram:
                            pe.wait_ge(bias_in[s], 16 * (j // 2) + 16)
                    if not zero(j):
                        pe.wait_ge(exped, TB * (j - 1) + i + 1)
                    w = (i + 1) * P
                    extra = bias_of(j, i, bias_slot[s] if bias_dram else None)
                    for n, (matrix, key) in enumerate(extra):
                        nc.tensor.matmul(s_ps[i][:, key:key + matrix.shape[-1]], ident, matrix, start=n == 0, stop=False,
                                         skip_group_check=True)
                    last = nc.tensor.matmul(s_ps[i][:, 0:w], q_slot[s][:, i * P:(i + 1) * P], k_of(j, w),
                                            start=False, stop=True, skip_group_check=True)
                    last.then_inc(scored, 1)

                def turn_probs(j, i):
                    pe.wait_ge(exped, TB * j + i + 1)
                    if i == 0 and not zero(j):
                        pe.wait_ge(pt_dve, (TB - 1) * j)
                    elif i == 1 and not zero(j):
                        pe.wait_ge(pt_act, j)
                    elif i >= 2:
                        pe.wait_ge(pt_dve, (TB - 1) * j + i - 1)
                    for b in range(i + 1):
                        last = nc.tensor.transpose(t_ps[i % 2][:, b * P:(b + 1) * P], prob[i][:, b * P:(b + 1) * P], ident)
                    last.then_inc(turned, 1)

                def value(j, i):
                    if i < TB - 1:
                        pe.wait_ge(pt_dve, (TB - 1) * j + i + 1)
                    else:
                        pe.wait_ge(pt_act, j + 1)
                    if not zero(j) or i >= 2:
                        pe.wait_ge(stored, TB * j + i - 1)
                    for b in range(i + 1):
                        last = nc.tensor.matmul(o_ps[i % 2][:], prob_t[i % 2][:, b * P:(b + 1) * P], v_of(j, b),
                                                start=b == 0, stop=b == i)
                    last.then_inc(valued, 1)

                def step(j, s, first, scores=True):
                    for i in range(TB):
                        if scores:
                            score(j, i, s)
                        if not zero(j):
                            turn_probs(j - 1, i)
                            if i:
                                value(j - 1, i - 1)
                    if not zero(j):
                        value(j - 1, TB - 1)
                pairs(pe, heads, step)
                step(heads, 0, False, scores=False)


def bcast(ap, shape):
    return ap.broadcast_to(shape)


def prepare_first(core, proj, T, select):
    nc = core.nc
    par, const = core.par, core.const
    groups = ((FQ, 2 * FOX, HEAD), (DQ, 4 * DIFF, DIFF_D), (SQ, DSA + 1, HEAD))
    NS = sum(n for _, n, _ in groups)
    with ExitStack() as st:
        sq = [core.sb(f"prep_sq{n}", [P, TB, h * d], ctx=st) for n, (_, h, d) in enumerate(groups)]
        ss = [core.sb(f"prep_ss{n}", [P, TB, h], ctx=st) for n, (_, h, _) in enumerate(groups)]
        half = core.sb("prep_half", [P, TB * max(h for _, h, _ in groups)], ctx=st)
        rope_a = core.sb("rope_a", [P, TB, 16 * ROPE32 + 12 * ROPE64], ctx=st)
        z = core.sb("forget_z", [P, TB, FOX], ctx=st)
        e = core.sb("forget_e", [P, TB, FOX], ctx=st)
        lf = core.sb("log_forget", [P, TB, FOX], ctx=st)
        cc = core.sb("forget_sums", [P, TB, 2 * FOX], ctx=st)
        ccT = core.sb("forget_sums_t", [2 * FOX, SEQ], ctx=st)
        banks = [core.psum(f"prep_ps{b}", [P, SEQ], st) for b in range(4)]
        c_ps = core.psum("forget_ps", [P, TB * FOX], st)
        ct_ps = core.psum("forget_t_ps", [2 * FOX, SEQ], st)
        squared = core.sem("prep_squared", st)
        meaned = core.sem("prep_meaned", st)
        rooted = core.sem("prep_rooted", st)
        zed = core.sem("forget_zed", st)
        logged = core.sem("forget_logged", st)
        lf_done = core.sem("forget_lf_done", st)
        c_sum = core.sem("forget_c_sum", st)
        cc_done = core.sem("forget_cc_done", st)
        cc_turned = core.sem("forget_cc_turned", st)
        ccT_done = core.sem("forget_ccT_done", st)
        ones_set = core.sem("forget_ones_set", st)
        c_rows = core.sem("forget_c_rows", st)
        ready = core.sem("prep_ready", st)
        chain = core.sem("prep_chain", st)
        turned = core.sem("prep_turned", st)
        out_act = core.sem("prep_out_act", st)
        out_dve = core.sem("prep_out_dve", st)
        ident = const[:, C_ID:C_ID + P]
        rope = const[:, C_ROPE:C_ROPE + TB * ROPE_COLS].rearrange("p (t c) -> p t c", t=TB)

        units = [(u, IQ + HEAD * (u - U_IQ), HEAD) for u in range(U_IQ, UNITS)]
        units += [(u, FQ + HEAD * (u - U_FQ), HEAD) for u in range(U_FQ, U_DQ)]
        units += [(u, DQ + DIFF_D * (u - U_DQ), DIFF_D) for u in range(U_DQ, U_SQ)]
        units += [(u, SQ + HEAD * (u - U_SQ), HEAD) for u in range(U_SQ, U_IQ)]

        with nc.Block() as block:
            @block.sync
            def _(sp):
                sp.wait_ge(ccT_done, 1)
                sp.wait_ge(ones_set, 1)
                for h in range(FOX):
                    sp.dma_start(T[HEAD:HEAD + 1, U_FQ + h, :], ccT[h:h + 1, :]).then_inc(c_rows, 16)
                    sp.dma_start(T[HEAD + 1:HEAD + 2, U_FK + h, :], ccT[FOX + h:FOX + h + 1, :]).then_inc(c_rows, 16)
                sp.wait_ge(c_rows, 2 * FOX * 16)

            @block.gpsimd
            def _(pool):
                nc.gpsimd.memset(T[HEAD:HEAD + 2, U_FQ:U_DQ, :], 1.0).then_inc(ones_set, 1)
                pool.wait_ge(ones_set, 1)
                nc.gpsimd.memset(half[:], -0.5).then_inc(rooted, 1)
                for n, (_, h, _) in enumerate(groups):
                    pool.wait_ge(meaned, n + 1)
                    pool.wait_ge(rooted, 1)
                    v = ss[n][:].rearrange("p t h -> p (t h)")
                    nc.gpsimd.tensor_tensor(v, v, half[:, 0:TB * h], ALU.pow).then_inc(rooted, 1)

            @block.scalar
            def _(act):
                act.wait_ge(zed, 1)
                nc.scalar.activation(e[:], z[:], ACT.Abs).then_inc(logged, 1)
                act.wait_ge(logged, 1)
                nc.scalar.activation(e[:], e[:], ACT.Exp, scale=-1.0).then_inc(logged, 1)
                act.wait_ge(logged, 2)
                nc.scalar.activation(e[:], e[:], ACT.Ln, bias=1.0).then_inc(logged, 1)
                for n, (c0, h, d) in enumerate(groups):
                    nc.scalar.activation(sq[n][:], proj[:, :, c0:c0 + h * d], ACT.Square).then_inc(squared, 1)
                for n, (u, c0, d) in enumerate(units):
                    if n % 2 == 0:
                        act.wait_ge(turned, n + 1)
                        nc.scalar.copy(T[0:d, u, :], banks[n % 4][0:d, :]).then_inc(out_act, 1)

            @block.vector
            def _(dve):
                link = chained(dve, chain)
                fb = par[:, PAR["fox_fb"]:PAR["fox_fb"] + FOX].unsqueeze(1)
                nc.vector.tensor_tensor(z[:], proj[:, :, FF:FF + FOX], bcast(fb, [P, TB, FOX]), ALU.add).then_inc(zed, 1)
                dve.wait_ge(logged, 3)
                nc.vector.scalar_tensor_tensor(lf[:], z[:], 0.0, e[:], ALU.min, ALU.subtract).then_inc(lf_done, 1)
                dve.wait_ge(c_sum, 1)
                cv = c_ps[:].rearrange("p (t h) -> p t h", t=TB)
                nc.vector.tensor_copy(cc[:, :, 0:FOX], cv).then_inc(cc_done, 1)
                nc.vector.tensor_scalar(cc[:, :, FOX:2 * FOX], cv, -1.0, None, ALU.mult).then_inc(cc_done, 1)

                def rotate(first, heads, d):
                    hw = d // 8
                    o = 0 if d == HEAD else 2 * ROPE64
                    cos = bcast(rope[:, :, o:o + hw].unsqueeze(2), [P, TB, heads, hw])
                    sin = bcast(rope[:, :, o + hw:o + 2 * hw].unsqueeze(2), [P, TB, heads, hw])
                    v = proj[:, :, first:first + heads * d].rearrange("p t (h d) -> p t h d", d=d)
                    x1, x2 = v[:, :, :, 0:hw], v[:, :, :, hw:2 * hw]
                    n = heads * hw
                    t1, t2 = (rope_a[:, :, m * n:(m + 1) * n].rearrange("p t (h d) -> p t h d", d=hw) for m in range(2))
                    link(nc.vector.tensor_tensor(t1, x2, sin, ALU.mult))
                    link(nc.vector.tensor_tensor(t2, x1, sin, ALU.mult))
                    link(nc.vector.tensor_tensor(x1, x1, cos, ALU.mult))
                    link(nc.vector.tensor_tensor(x2, x2, cos, ALU.mult))
                    link(nc.vector.tensor_tensor(x1, x1, t1, ALU.subtract))
                    nc.vector.tensor_tensor(x2, x2, t2, ALU.add).then_inc(ready, 1)

                rotate(IQ, IDX + 1, HEAD)
                dve.wait_ge(cc_turned, 1)
                nc.vector.tensor_copy(ccT[:], ct_ps[:]).then_inc(ccT_done, 1)
                for n, (c0, h, d) in enumerate(groups):
                    dve.wait_ge(squared, n + 1)
                    link(nc.vector.tensor_reduce(ss[n][:], sq[n][:].rearrange("p t (h d) -> p t h d", d=d), AX, ALU.add))
                    nc.vector.tensor_scalar(ss[n][:], ss[n][:], 1.0 / d, NORM_EPS, ALU.mult, ALU.add).then_inc(meaned, 1)
                for n, (c0, h, d) in enumerate(groups):
                    dve.wait_ge(rooted, n + 2)
                    v = proj[:, :, c0:c0 + h * d].rearrange("p t (h d) -> p t h d", d=d)
                    link(nc.vector.tensor_tensor(v, v, bcast(ss[n][:].unsqueeze(3), [P, TB, h, d]), ALU.mult))
                    halves = ((0, DSA, "dsa_qn"), (DSA, 1, "dsa_kn")) if n == 2 else \
                        ((0, h // 2, ("fox_qn", "diff_qn")[n]), (h // 2, h // 2, ("fox_kn", "diff_kn")[n]))
                    for h0, hn, g in halves:
                        w = v[:, :, h0:h0 + hn, :]
                        gain = par[:, PAR[g]:PAR[g] + d].unsqueeze(1).unsqueeze(1)
                        ins = nc.vector.tensor_tensor(w, w, bcast(gain, [P, TB, hn, d]), ALU.mult)
                        if n == 0:
                            ins.then_inc(ready, 1)
                        else:
                            link(ins)
                    if n:
                        rotate(c0, h, d)
                for n, (u, c0, d) in enumerate(units):
                    if n % 2:
                        dve.wait_ge(turned, n + 1)
                        nc.vector.tensor_copy(T[0:d, u, :], banks[n % 4][0:d, :]).then_inc(out_dve, 1)

            @block.tensor
            def _(pe):
                pe.wait_ge(lf_done, 1)
                for t in range(TB):
                    for b in range(t + 1):
                        m = C_TRI if b == t else C_ONE
                        last = nc.tensor.matmul(c_ps[:, t * FOX:(t + 1) * FOX], const[:, m:m + P], lf[:, b, :],
                                                start=b == 0, stop=b == t)
                last.then_inc(c_sum, 1)
                pe.wait_ge(cc_done, 2)
                for t in range(TB):
                    last = nc.tensor.transpose(ct_ps[:, t * P:(t + 1) * P], cc[:, t, :], ident)
                last.then_inc(cc_turned, 1)
                for n, (u, c0, d) in enumerate(units):
                    need = 1 if u >= U_IQ else 3 if u < U_DQ else 4 if u < U_SQ else 5
                    pe.wait_ge(ready, need)
                    if n >= 4:
                        if n % 2:
                            pe.wait_ge(out_dve, n // 2 - 1)
                        else:
                            pe.wait_ge(out_act, n // 2 - 1)
                    for t in range(TB):
                        last = nc.tensor.transpose(banks[n % 4][0:d, t * P:(t + 1) * P], proj[:, t, c0:c0 + d], ident)
                    last.then_inc(turned, 1)


def select_keys(core, proj, T, select):
    nc = core.nc
    blocks = range(1, TB)
    offs = {i: sum((b + 1) * P for b in range(1, i)) for i in blocks}
    with ExitStack() as st:
        work = core.sb("topk_work", [P, sum((i + 1) * P for i in blocks)], ctx=st)
        relu = [core.sb(f"topk_relu{s}", [P, SEQ], ctx=st) for s in range(2)]
        best = core.sb("topk_best", [P, TB, 8], ctx=st)
        spare = core.sb("topk_spare", [P, 1], ctx=st)
        iw = core.sb("topk_iw", [P, TB, IDX], ctx=st)
        banks = [core.psum(f"topk_ps{b}", [P, SEQ], st) for b in range(4)]
        scored = core.sem("topk_scored", st)
        relued = core.sem("topk_relued", st)
        weighed = core.sem("topk_weighed", st)
        w_done = core.sem("topk_w_done", st)
        masked = core.sem("topk_masked", st)
        found = core.sem("topk_found", st)
        taken = core.sem("topk_taken", st)
        rows = [(i, h) for i in blocks for h in range(IDX)]
        NBK = len(list(blocks))

        def scores(i):
            return work[:, offs[i]:offs[i] + (i + 1) * P]

        with nc.Block() as block:
            @block.tensor
            def _(pe):
                for n, (i, h) in enumerate(rows):
                    if n >= 4:
                        pe.wait_ge(relued, n - 3)
                    nc.tensor.matmul(banks[n % 4][:, 0:(i + 1) * P], T[0:HEAD, U_IQ + h, i * P:(i + 1) * P],
                                     T[0:HEAD, U_IK, 0:(i + 1) * P], start=True, stop=True).then_inc(scored, 1)

            @block.scalar
            def _(act):
                for n, (i, h) in enumerate(rows):
                    act.wait_ge(scored, n + 1)
                    if n >= 2:
                        act.wait_ge(weighed, n - 1)
                    nc.scalar.activation(relu[n % 2][:, 0:(i + 1) * P], banks[n % 4][:, 0:(i + 1) * P], ACT.Relu,
                                         scale=HEAD ** -0.5).then_inc(relued, 1)

            @block.vector
            def _(dve):
                nc.vector.tensor_scalar(iw[:], proj[:, :, IW:IW + IDX], IDX ** -0.5, None, ALU.mult).then_inc(w_done, 1)
                dve.wait_ge(w_done, 1)
                for n, (i, h) in enumerate(rows):
                    dve.wait_ge(relued, n + 1)
                    if h:
                        dve.wait_ge(weighed, n)
                        nc.vector.scalar_tensor_tensor(scores(i), relu[n % 2][:, 0:(i + 1) * P], iw[:, i, h:h + 1], scores(i),
                                                       ALU.mult, ALU.add).then_inc(weighed, 1)
                    else:
                        nc.vector.tensor_scalar(scores(i), relu[n % 2][:, 0:(i + 1) * P], iw[:, i, h:h + 1], 0.0,
                                                ALU.mult, ALU.add).then_inc(weighed, 1)
                dve.wait_ge(weighed, len(rows))
                for i in blocks:
                    diag = scores(i)[:, i * P:(i + 1) * P]
                    nc.vector.tensor_tensor(diag, diag, core.const[:, C_CAUSAL:C_CAUSAL + P], ALU.add).then_inc(masked, 1)
                dve.wait_ge(masked, NBK)
                def turn(r, first):
                    if not first:
                        dve.wait_ge(taken, NBK * r)
                        nc.vector.memset(spare[:], 0.0)
                    for n, i in enumerate(blocks):
                        nc.vector.max(best[:, i, :], scores(i)).then_inc(found, 1)
                    dve.wait_ge(found, NBK * r + NBK)
                    nc.vector.memset(spare[:], 0.0)
                    for n, i in enumerate(blocks):
                        nc.vector.match_replace(scores(i), best[:, i, :], scores(i), TAKEN).then_inc(taken, 1)
                turn(0, True)
                with dve.Fori(1, TOPK // 8) as r:
                    turn(r, False)
                dve.wait_ge(taken, NBK * (TOPK // 8))
                for i in blocks:
                    nc.vector.tensor_scalar(select[:, offs[i]:offs[i] + (i + 1) * P], scores(i), TAKEN_EDGE, NEG,
                                            ALU.is_ge, ALU.mult).then_inc(masked, 1)


def combine_diff(core, od, o):
    nc = core.nc
    par = core.par
    with ExitStack() as st:
        prod = core.sb("lam_prod", [P, 2, DIFF_D], ctx=st)
        dots = core.sb("lam_dots", [P, 2], ctx=st)
        lam = core.sb("lam", [P, 1], ctx=st)
        gain = core.sb("subln_gain", [P, HEAD], ctx=st)
        sq = core.sb("subln_sq", [P, TB * DIFF, HEAD], ctx=st)
        ss = core.sb("subln_ss", [P, TB * DIFF], ctx=st)
        half = core.sb("subln_half", [P, TB * DIFF], ctx=st)
        chain = core.sem("diff_chain", st)
        dotted = core.sem("diff_dotted", st)
        exped = core.sem("diff_exped", st)
        meaned = core.sem("diff_meaned", st)
        rooted = core.sem("diff_rooted", st)
        mixed = core.sem("diff_mixed", st)
        squared = core.sem("diff_squared", st)
        maps = od[:].rearrange("p t (h m) d -> p (t h) m d", m=2)
        even, odd = maps[:, :, 0, :], maps[:, :, 1, :]
        with nc.Block() as block:
            @block.gpsimd
            def _(pool):
                nc.gpsimd.memset(half[:], -0.5).then_inc(rooted, 1)
                pool.wait_ge(meaned, 1)
                pool.wait_ge(rooted, 1)
                nc.gpsimd.tensor_tensor(ss[:], ss[:], half[:], ALU.pow).then_inc(rooted, 1)

            @block.scalar
            def _(act):
                act.wait_ge(dotted, 1)
                nc.scalar.activation(dots[:], dots[:], ACT.Exp).then_inc(exped, 1)
                act.wait_ge(mixed, 1)
                nc.scalar.activation(sq[:], even, ACT.Square).then_inc(squared, 1)

            @block.vector
            def _(dve):
                link = chained(dve, chain)
                for n in range(2):
                    a, b = PAR[f"diff_lq{n + 1}"], PAR[f"diff_lk{n + 1}"]
                    link(nc.vector.tensor_tensor(prod[:, n, :], par[:, a:a + DIFF_D], par[:, b:b + DIFF_D], ALU.mult))
                nc.vector.tensor_reduce(dots[:], prod[:], AX, ALU.add).then_inc(dotted, 1)
                dve.wait_ge(exped, 1)
                link(nc.vector.tensor_tensor(lam[:], dots[:, 1:2], dots[:, 0:1], ALU.subtract))
                link(nc.vector.tensor_tensor(lam[:], lam[:], core.lam_init[:, 0:1], ALU.subtract))
                s0 = PAR["diff_subln"]
                link(nc.vector.tensor_scalar(gain[:], par[:, s0:s0 + HEAD], core.lam_init[:, 1:2], None, ALU.mult))
                nc.vector.scalar_tensor_tensor(even, odd, lam[:], even, ALU.mult, ALU.add).then_inc(mixed, 1)
                dve.wait_ge(squared, 1)
                link(nc.vector.tensor_reduce(ss[:], sq[:], AX, ALU.add))
                nc.vector.tensor_scalar(ss[:], ss[:], 1.0 / HEAD, NORM_EPS, ALU.mult, ALU.add).then_inc(meaned, 1)
                dve.wait_ge(rooted, 2)
                link(nc.vector.tensor_tensor(even, even, bcast(ss[:].unsqueeze(2), [P, TB * DIFF, HEAD]), ALU.mult))
                dst = o[:, :, FOX * HEAD:(FOX + DIFF) * HEAD].rearrange("p t (h d) -> p t h d", d=HEAD)
                src = od[:].rearrange("p t (h m) d -> p t h m d", m=2)[:, :, :, 0, :]
                link(nc.vector.tensor_tensor(dst, src, bcast(gain[:].unsqueeze(1).unsqueeze(1), [P, TB, DIFF, HEAD]), ALU.mult))


def first_block(core, w, layer):
    nc = core.nc
    offs = {i: sum((b + 1) * P for b in range(1, i)) for i in range(1, TB)}
    with ExitStack() as lay:
        core.par = core.sb("par", [P, PAR_COLS], ctx=lay)
        core.lam_init = core.sb("lam_init", [P, 2], ctx=lay)
        gain = core.sb("norm_gain", [P, KD], ctx=lay)
        par_in = core.sem("par_in", lay)
        with nc.Block() as block:
            @block.sync
            def _(sp):
                sp.dma_start(core.par[:], w["params"][layer].partition_broadcast(P)).then_inc(par_in, 16)
                sp.dma_start(core.lam_init[:], w["lam"][layer].partition_broadcast(P)).then_inc(par_in, 16)
                sp.wait_ge(par_in, 32)

        with ExitStack() as mix:
            o = core.sb("mix_out", [P, TB, D], ctx=mix)
            with ExitStack() as a:
                proj = core.sb("proj", [P, TB, IN_CHUNKS * IN_COLS], ctx=a)
                with ExitStack() as b:
                    hi = core.sb("h_hi", [P, KD, SEQ], F32R, ctx=b)
                    lo = core.sb("h_lo", [P, KD, SEQ], F32R, ctx=b)
                    transpose_split(core, "n1", core.x, hi, lo, KD, gain, w["attn_norm"][layer], norm=True)
                    project(core, "in", hi, lo, lambda c: w["w_in"][layer, c], IN_CHUNKS, IN_COLS,
                            by_token=lambda c, t, sums: nc.vector.tensor_copy(proj[:, t, bass.ds(c * IN_COLS, IN_COLS)], sums))
                T = core.sb("qk_t", [HEAD + 2, UNITS, SEQ], ctx=a)
                select = core.sb("select", [P, sum((i + 1) * P for i in range(1, TB))], ctx=a)
                prepare_first(core, proj, T, select)
                select_keys(core, proj, T, select)
                causal = core.const[:, C_CAUSAL:C_CAUSAL + P]
                od = core.sb("diff_out", [P, TB, 2 * DIFF, HEAD], ctx=a)
                attention(core, "fox", FOX, HEAD + 2, lambda j: T[:, U_FQ + j, :], lambda j, n: T[:, U_FK + j, 0:n],
                          lambda j, b: proj[:, b, bass.ds(j * HEAD + FV, HEAD)], core.const[0:HEAD + 2, C_FOX:C_FOX + 1],
                          lambda j, i, s: [(causal, i * P)], lambda j, i: o[:, i, bass.ds(j * HEAD, HEAD)])
                attention(core, "dif", 2 * DIFF, DIFF_D, lambda j: T[0:DIFF_D, U_DQ + j, :],
                          lambda j, n: T[0:DIFF_D, U_DK + j, 0:n],
                          lambda j, b: proj[:, b, bass.ds((j // 2) * HEAD + DV, HEAD)], DIFF_D ** -0.5,
                          lambda j, i, s: [(causal, i * P)], lambda j, i: od[:, i, j, :])
                attention(core, "dsa", DSA, HEAD, lambda j: T[0:HEAD, U_SQ + j, :], lambda j, n: T[0:HEAD, U_SK, 0:n],
                          lambda j, b: proj[:, b, SV:SV + HEAD], HEAD ** -0.5,
                          lambda j, i, s: [(select[:, offs[i]:offs[i] + (i + 1) * P], 0)] if i else [(causal, 0)],
                          lambda j, i: o[:, i, bass.ds(j * HEAD + (FOX + DIFF) * HEAD, HEAD)])
                combine_diff(core, od, o)
            hi = core.sb("o_hi", [P, KD, SEQ], F32R, ctx=mix)
            lo = core.sb("o_lo", [P, KD, SEQ], F32R, ctx=mix)
            transpose_split(core, "ot", o, hi, lo, KD)
            project(core, "out", hi, lo, lambda c: w["w_out"][layer, c], OUT_CHUNKS, OUT_COLS,
                    by_token=lambda c, t, sums: add_to_x(core, c, t, sums, OUT_COLS))
        with ExitStack() as b:
            hi = core.sb("f_hi", [P, KD, SEQ], F32R, ctx=b)
            lo = core.sb("f_lo", [P, KD, SEQ], F32R, ctx=b)
            transpose_split(core, "n2", core.x, hi, lo, KD, gain, w["ffn_norm"][layer], norm=True)
            feed_forward(core, "ffn", hi, lo, FFN_GROUPS, lambda g: w["w_gate"][layer, g], lambda g: w["w_up"][layer, g],
                         lambda g: w["w_down"][layer, g])
        core.clear()


Q_GAIN, K_GAIN, G_BIAS, PAR2_COLS = 0, HEAD, 2 * HEAD, 2 * HEAD + ROUTES
F_GATE, F_GLU, F_D, FEATURE_COLS = 0, 2 * D // P, 2 * D // P + SQT, 2 * D // P + 2 * SQT


def prepare_second(core, qkv, T):
    nc = core.nc
    N = 2 * HEADS2
    with ExitStack() as st:
        sq = core.sb("sq2", [P, TB, N * HEAD], ctx=st)
        ss = core.sb("ss2", [P, TB, N], ctx=st)
        half = core.sb("half2", [P, TB * N], ctx=st)
        banks = [core.psum(f"prep2_ps{b}", [P, SEQ], st) for b in range(4)]
        squared = core.sem("prep2_squared", st)
        meaned = core.sem("prep2_meaned", st)
        rooted = core.sem("prep2_rooted", st)
        chain = core.sem("prep2_chain", st)
        ready = core.sem("prep2_ready", st)
        turned = core.sem("prep2_turned", st)
        out_act = core.sem("prep2_out_act", st)
        out_dve = core.sem("prep2_out_dve", st)
        ident = core.const[:, C_ID:C_ID + P]
        with nc.Block() as block:
            @block.gpsimd
            def _(pool):
                nc.gpsimd.memset(half[:], -0.5).then_inc(rooted, 1)
                pool.wait_ge(meaned, 1)
                pool.wait_ge(rooted, 1)
                v = ss[:].rearrange("p t h -> p (t h)")
                nc.gpsimd.tensor_tensor(v, v, half[:], ALU.pow).then_inc(rooted, 1)

            @block.scalar
            def _(act):
                nc.scalar.activation(sq[:], qkv[:, :, 0:N * HEAD], ACT.Square).then_inc(squared, 1)
                for u in range(0, N, 2):
                    act.wait_ge(turned, u + 1)
                    nc.scalar.copy(T[:, u, :], banks[u % 4][0:HEAD, :]).then_inc(out_act, 1)

            @block.vector
            def _(dve):
                link = chained(dve, chain)
                dve.wait_ge(squared, 1)
                link(nc.vector.tensor_reduce(ss[:], sq[:].rearrange("p t (h d) -> p t h d", d=HEAD), AX, ALU.add))
                nc.vector.tensor_scalar(ss[:], ss[:], 1.0 / HEAD, NORM_EPS, ALU.mult, ALU.add).then_inc(meaned, 1)
                dve.wait_ge(rooted, 2)
                v = qkv[:, :, 0:N * HEAD].rearrange("p t (h d) -> p t h d", d=HEAD)
                link(nc.vector.tensor_tensor(v, v, bcast(ss[:].unsqueeze(3), [P, TB, N, HEAD]), ALU.mult))
                for n, g in enumerate((Q_GAIN, K_GAIN)):
                    part = v[:, :, n * HEADS2:(n + 1) * HEADS2, :]
                    gain = core.par2[:, g:g + HEAD].unsqueeze(1).unsqueeze(1)
                    nc.vector.tensor_tensor(part, part, bcast(gain, [P, TB, HEADS2, HEAD]), ALU.mult).then_inc(ready, 1)
                for u in range(1, N, 2):
                    dve.wait_ge(turned, u + 1)
                    nc.vector.tensor_copy(T[:, u, :], banks[u % 4][0:HEAD, :]).then_inc(out_dve, 1)

            @block.tensor
            def _(pe):
                for u in range(N):
                    pe.wait_ge(ready, 1 + u // HEADS2)
                    if u >= 4:
                        pe.wait_ge(out_dve if u % 2 else out_act, u // 2 - 1)
                    for t in range(TB):
                        last = nc.tensor.transpose(banks[u % 4][0:HEAD, t * P:(t + 1) * P],
                                                   qkv[:, t, u * HEAD:(u + 1) * HEAD], ident)
                    last.then_inc(turned, 1)


TWO_PI = 2 * math.pi
TWO_PI_HI = 6.28125
TWO_PI_LO = TWO_PI - TWO_PI_HI
ROUND = 1.5 * 2 ** 23
PI_EDGE = 3.1415925


def discretise(core, w, mag, cos_t, sin_t, b_t, c_t):
    nc = core.nc
    with ExitStack() as st:
        lam = core.sb("lambda", [P, 2 * ST], ctx=st)
        step = core.sb("step", [P, ST], ctx=st)
        small = core.sb("ssm_small", [P, 12, ST], ctx=st)
        raw_b = core.sb("raw_b", [P, 2, ST, 2 * GROUP], ctx=st)
        bb = core.sb("scaled_b", [P, 2, ST, 2 * GROUP], ctx=st)
        tmp = core.sb("b_tmp", [P, ST, SEQ // 4], ctx=st)
        tmp2 = core.sb("b_tmp2", [P, ST, SEQ // 4], ctx=st)
        banks = [core.psum(f"b_ps{b}", [P, P], st) for b in range(2 * SQT)]
        b_in = core.sem("ssm_in", st)
        mults = core.sem("ssm_step_mult", st)
        exped = core.sem("ssm_exped", st)
        sined = core.sem("ssm_sined", st)
        halved = core.sem("ssm_angle", st)
        chain = core.sem("ssm_chain", st)
        scaled = core.sem("ssm_scaled", st)
        turned = core.sem("ssm_turned", st)
        out = core.sem("ssm_b_out", st)
        lre, lim = lam[:, 0:ST], lam[:, ST:2 * ST]
        ang, rnd, sn, cs, hs, a_re, a_im, den, f_re, f_im, t0, t1 = (small[:, n, :] for n in range(12))
        with nc.Block() as block:
            @block.sync
            def _(sp):
                sp.dma_start(lam[:], w["lambda2"]).then_inc(b_in, 16)
                for n in range(2):
                    sp.dma_start(step[n * STATE:(n + 1) * STATE, :],
                                 w["log_step2"][n].partition_broadcast(STATE)).then_inc(b_in, 16)
                sp.dma_start(raw_b[:].rearrange("p m t c -> p (m t c)"), w["b_diag2"]).then_inc(b_in, 16)
                sp.dma_start(c_t[:].rearrange("p m t c -> p (m t c)"), w["c_diag2"]).then_inc(b_in, 16)

            @block.scalar
            def _(act):
                act.wait_ge(b_in, 5 * 16)
                nc.scalar.activation(step[:], step[:], ACT.Exp).then_inc(exped, 1)
                act.wait_ge(mults, 1)
                nc.scalar.activation(mag[:], mag[:], ACT.Exp).then_inc(exped, 1)
                act.wait_ge(halved, 1)
                nc.scalar.activation(sn, ang, ACT.Sin).then_inc(sined, 1)
                nc.scalar.activation(hs, ang, ACT.Sin, scale=0.5).then_inc(sined, 1)
                for n in range(2 * SQT):
                    act.wait_ge(turned, n + 1)
                    nc.scalar.copy(b_t[:, n // SQT, n % SQT, :], banks[n][:]).then_inc(out, 1)

            @block.vector
            def _(dve):
                link = chained(dve, chain)

                def tt(o, a, b, op):
                    link(nc.vector.tensor_tensor(o, a, b, op))

                def ts(o, a, m, b, op0=ALU.mult, op1=ALU.add):
                    link(nc.vector.tensor_scalar(o, a, m, b, op0, op1))

                dve.wait_ge(b_in, 5 * 16)
                ts(c_t[:, 1], c_t[:, 1], -1.0, 0.0)
                dve.wait_ge(exped, 1)
                nc.vector.tensor_tensor(mag[:], lre, step[:], ALU.mult).then_inc(mults, 1)
                tt(ang, lim, step[:], ALU.mult)
                ts(rnd, ang, 1.0 / TWO_PI, ROUND)
                ts(rnd, rnd, ROUND, None, ALU.subtract, ALU.bypass)
                link(nc.vector.scalar_tensor_tensor(ang, rnd, -TWO_PI_HI, ang, ALU.mult, ALU.add))
                link(nc.vector.scalar_tensor_tensor(ang, rnd, -TWO_PI_LO, ang, ALU.mult, ALU.add))
                nc.vector.tensor_scalar(ang, ang, PI_EDGE, -PI_EDGE, ALU.min, ALU.max).then_inc(halved, 1)
                dve.wait_ge(exped, 2)
                dve.wait_ge(sined, 2)
                tt(cs, hs, hs, ALU.mult)
                ts(cs, cs, -2.0, 1.0)
                tt(a_re, mag[:], cs, ALU.mult)
                tt(a_im, mag[:], sn, ALU.mult)
                ts(a_re, a_re, -1.0, None, ALU.add, ALU.bypass)
                tt(den, lre, lre, ALU.mult)
                tt(t0, lim, lim, ALU.mult)
                tt(den, den, t0, ALU.add)
                link(nc.vector.reciprocal(den, den))
                tt(t0, a_re, lre, ALU.mult)
                tt(t1, a_im, lim, ALU.mult)
                tt(t0, t0, t1, ALU.add)
                tt(f_re, t0, den, ALU.mult)
                tt(t0, a_im, lre, ALU.mult)
                tt(t1, a_re, lim, ALU.mult)
                tt(t0, t0, t1, ALU.subtract)
                tt(f_im, t0, den, ALU.mult)
                shape = [P, ST, 2 * GROUP]
                fr, fi = bcast(f_re.unsqueeze(2), shape), bcast(f_im.unsqueeze(2), shape)
                part = tmp[:, :, 0:2 * GROUP]
                tt(bb[:, 0], raw_b[:, 0], fr, ALU.mult)
                tt(part, raw_b[:, 1], fi, ALU.mult)
                nc.vector.tensor_tensor(bb[:, 0], bb[:, 0], part, ALU.subtract).then_inc(scaled, 1)
                tt(bb[:, 1], raw_b[:, 1], fr, ALU.mult)
                dve.wait_ge(scaled, 1)
                tt(part, raw_b[:, 0], fi, ALU.mult)
                nc.vector.tensor_tensor(bb[:, 1], bb[:, 1], part, ALU.add).then_inc(scaled, 1)
                dve.wait_ge(scaled, 2)
                link(nc.vector.memset(cos_t[:, :, 0:1], 1.0))
                link(nc.vector.memset(sin_t[:, :, 0:1], 0.0))
                n = 1
                while n < SEQ:
                    for k0 in range(0, n, SEQ // 4):
                        k1 = min(n, k0 + SEQ // 4)
                        shape = [P, ST, k1 - k0]
                        c_n, s_n = bcast(cs.unsqueeze(2), shape), bcast(sn.unsqueeze(2), shape)
                        c_k, s_k = cos_t[:, :, k0:k1], sin_t[:, :, k0:k1]
                        p, q = tmp[:, :, 0:k1 - k0], tmp2[:, :, 0:k1 - k0]
                        new = slice(n + k0, n + k1)
                        tt(p, c_k, c_n, ALU.mult)
                        tt(q, s_k, s_n, ALU.mult)
                        tt(cos_t[:, :, new], p, q, ALU.subtract)
                        tt(p, s_k, c_n, ALU.mult)
                        tt(q, c_k, s_n, ALU.mult)
                        tt(sin_t[:, :, new], p, q, ALU.add)
                    tt(t0, cs, cs, ALU.mult)
                    tt(t1, sn, sn, ALU.mult)
                    tt(sn, sn, cs, ALU.mult)
                    ts(sn, sn, 2.0, 0.0)
                    tt(cs, t0, t1, ALU.subtract)
                    n *= 2

            @block.tensor
            def _(pe):
                for m in range(2):
                    pe.wait_ge(scaled, m + 1)
                    for q in range(SQT):
                        v = bb[:, m, q * PER:(q + 1) * PER, :].rearrange("p t c -> p (t c)")
                        nc.tensor.transpose(banks[m * SQT + q][:], v, core.const[:, C_ID:C_ID + P]).then_inc(turned, 1)


def state_space(core, u_t, mag, cos_t, sin_t, b_t, c_t, z):
    nc = core.nc
    with ExitStack() as st:
        b_s = core.sb("b_slot", [P, 2, P], ctx=st)
        c_s = core.sb("c_slot", [P, 2, PER, 2 * GROUP], ctx=st)
        u_s = core.sb("u_slot", [P, SEQ], ctx=st)
        prods = [core.sb(f"turn_in{s}", [P, 4, SEQ], ctx=st) for s in range(2)]
        scanned = [core.sb(f"scanned{s}", [P, 2, SEQ], ctx=st) for s in range(2)]
        back = [core.sb(f"turn_back{s}", [P, 4, SEQ], ctx=st) for s in range(2)]
        y = core.sb("ssm_y", [P, SEQ], ctx=st)
        in_ps = [[core.psum(f"bu_ps{s}{m}", [P, SEQ], st) for m in range(2)] for s in range(2)]
        y_ps = core.psum("y_ps", [P, SEQ], st)
        slots = core.sem("ssm_slots", st)
        bu = core.sem("ssm_bu", st)
        mixed = core.sem("ssm_mixed", st)
        summed = core.sem("ssm_summed", st)
        scan = core.sem("ssm_scan", st)
        back_dve = core.sem("ssm_back_dve", st)
        back_pool = core.sem("ssm_back_pool", st)
        states = core.sem("ssm_states", st)
        read = core.sem("ssm_read", st)
        y_done = core.sem("ssm_y_done", st)
        z_done = core.sem("ssm_z_done", st)

        def quarters(engine, body):
            body(0)
            with engine.Fori(1, SQT) as q:
                body(q)

        def later(q):
            return not isinstance(q, int)

        with nc.Block() as block:
            @block.scalar
            def _(act):
                def body(q):
                    if later(q):
                        act.wait_ge(bu, PER * q)
                        act.wait_ge(y_done, q)
                        act.wait_ge(read, PER * q)
                    nc.scalar.copy(b_s[:], b_t[:, :, q, :]).then_inc(slots, 1)
                    nc.scalar.copy(u_s[:], u_t[:, q, :]).then_inc(slots, 1)
                    nc.scalar.copy(c_s[:], c_t[:, :, bass.ds(q * PER, PER), :]).then_inc(slots, 1)
                    act.wait_ge(y_done, q + 1)
                    nc.scalar.activation(z[:, q, :], y[:], ACT.Gelu_apprx_tanh).then_inc(z_done, 1)
                quarters(act, body)

            @block.tensor
            def _(pe):
                def inputs(q, j):
                    i, s = PER * q + j, j % 2
                    if later(q) or j >= 2:
                        pe.wait_ge(mixed, i - 1)
                    rows = slice(2 * GROUP * j, 2 * GROUP * (j + 1))
                    for m in range(2):
                        last = nc.tensor.matmul(in_ps[s][m][:], b_s[rows, m, :], u_s[rows, :], start=True, stop=True)
                    last.then_inc(bu, 1)

                def outputs(q, j):
                    pe.wait_ge(states, PER * q + j + 1)
                    if j == 0 and later(q):
                        pe.wait_ge(y_done, q)
                    rows = slice(2 * GROUP * j, 2 * GROUP * (j + 1))
                    for m in range(2):
                        last = nc.tensor.matmul(y_ps[rows, :], c_s[:, m, j, :], back[j % 2][:, 2 * m, :], start=m == 0, stop=m == 1)
                    last.then_inc(read, 1)

                def body(q):
                    pe.wait_ge(slots, 3 * q + 3)
                    for j in range(PER):
                        inputs(q, j)
                        if j:
                            outputs(q, j - 1)
                    outputs(q, PER - 1)
                quarters(pe, body)

            @block.vector
            def _(dve):
                def mix(q, j):
                    i, s = PER * q + j, j % 2
                    dve.wait_ge(bu, i + 1)
                    if later(q) or j >= 2:
                        dve.wait_ge(scan, i - 1)
                    c, sn = cos_t[:, i, :], sin_t[:, i, :]
                    re, im = in_ps[s][0][:], in_ps[s][1][:]
                    nc.vector.tensor_tensor(prods[s][:, 0, :], re, c, ALU.mult)
                    nc.vector.tensor_tensor(prods[s][:, 1, :], im, sn, ALU.mult)
                    nc.vector.tensor_tensor(prods[s][:, 2, :], im, c, ALU.mult)
                    nc.vector.tensor_tensor(prods[s][:, 3, :], re, sn, ALU.mult).then_inc(mixed, 1)

                def recur(q, j):
                    i, s = PER * q + j, j % 2
                    dve.wait_ge(summed, i + 1)
                    if later(q) or j >= 2:
                        dve.wait_ge(back_pool, i - 1)
                        dve.wait_ge(back_dve, i - 1)
                    factor = bcast(mag[:, bass.ds(i, 1)], [P, SEQ])
                    for m in range(2):
                        last = nc.vector.tensor_tensor_scan(scanned[s][:, m, :], factor, prods[s][:, 2 * m, :], 0.0, ALU.mult, ALU.add)
                    last.then_inc(scan, 1)

                def turn_back(q, j):
                    i, s = PER * q + j, j % 2
                    dve.wait_ge(scan, i + 1)
                    if later(q) or j >= 2:
                        dve.wait_ge(read, i - 1)
                    nc.vector.tensor_tensor(back[s][:, 0, :], scanned[s][:, 0, :], cos_t[:, i, :], ALU.mult)
                    nc.vector.tensor_tensor(back[s][:, 2, :], scanned[s][:, 1, :], cos_t[:, i, :], ALU.mult).then_inc(back_dve, 1)

                def body(q):
                    for j in range(PER):
                        mix(q, j)
                        if j:
                            turn_back(q, j - 1)
                        recur(q, j)
                    turn_back(q, PER - 1)
                    dve.wait_ge(read, PER * q + PER)
                    if later(q):
                        dve.wait_ge(z_done, q)
                    nc.vector.scalar_tensor_tensor(y[:], u_s[:], core.feature2[:, bass.ds(q + F_D, 1)], y_ps[:],
                                                   ALU.mult, ALU.add).then_inc(y_done, 1)
                quarters(dve, body)

            @block.gpsimd
            def _(pool):
                def turn(q, j):
                    i, s = PER * q + j, j % 2
                    pool.wait_ge(mixed, i + 1)
                    nc.gpsimd.tensor_tensor(prods[s][:, 0, :], prods[s][:, 0, :], prods[s][:, 1, :], ALU.add)
                    nc.gpsimd.tensor_tensor(prods[s][:, 2, :], prods[s][:, 2, :], prods[s][:, 3, :], ALU.subtract).then_inc(summed, 1)

                def make_states(q, j):
                    i, s = PER * q + j, j % 2
                    pool.wait_ge(scan, i + 1)
                    nc.gpsimd.tensor_tensor(back[s][:, 1, :], scanned[s][:, 1, :], sin_t[:, i, :], ALU.mult)
                    nc.gpsimd.tensor_tensor(back[s][:, 3, :], scanned[s][:, 0, :], sin_t[:, i, :], ALU.mult).then_inc(back_pool, 1)
                    pool.wait_ge(back_pool, i + 1)
                    pool.wait_ge(back_dve, i + 1)
                    nc.gpsimd.tensor_tensor(back[s][:, 0, :], back[s][:, 0, :], back[s][:, 1, :], ALU.subtract)
                    nc.gpsimd.tensor_tensor(back[s][:, 2, :], back[s][:, 2, :], back[s][:, 3, :], ALU.add).then_inc(states, 1)

                def body(q):
                    for j in range(PER):
                        turn(q, j)
                        if j:
                            make_states(q, j - 1)
                    make_states(q, PER - 1)
                quarters(pool, body)


def route(core, w, hi, lo, gates):
    nc = core.nc
    with ExitStack() as st:
        raw = core.sb("route_raw", [P, KD, ROUTES], ctx=st)
        whi = core.sb("route_hi", [P, KD, ROUTES], F32R, ctx=st)
        wlo = core.sb("route_lo", [P, KD, ROUTES], F32R, ctx=st)
        logit = core.sb("route_logit", [P, TB, ROUTES], ctx=st)
        four = core.sb("route_four", [P, 9, TB, MOE_G], ctx=st)
        one = core.sb("route_one", [P, 7, TB], ctx=st)
        grid = core.sb("route_grid", [P, TB, MOE_G, MOE_E], ctx=st)
        ps = core.psum("route_ps", [P, TB * ROUTES], st)
        w_in = core.sem("route_w_in", st)
        hi_done = core.sem("route_hi_done", st)
        lo_done = core.sem("route_lo_done", st)
        summed = core.sem("route_summed", st)
        shifted = core.sem("route_shifted", st)
        exped = core.sem("route_exped", st)
        chain = core.sem("route_chain", st)
        g_exp, one_g, pos, e_sel, prob, one_1, one_2, left, pair = (four[:, n] for n in range(9))
        g_max, g_prob, best, e_max, e_sum, p1, p2 = (one[:, n] for n in range(7))
        with nc.Block() as block:
            @block.sync
            def _(sp):
                sp.dma_start(raw[:].rearrange("p k n -> p (k n)"), w["w_route2"]).then_inc(w_in, 16)

            @block.tensor
            def _(pe):
                pe.wait_ge(lo_done, 1)
                for t in range(TB):
                    n = 0
                    for k in range(KD):
                        for aw, ww in ((hi, whi), (lo, whi), (hi, wlo)):
                            last = nc.tensor.matmul(ps[:, t * ROUTES:(t + 1) * ROUTES], aw[:, k, t * P:(t + 1) * P],
                                                    ww[:, k, :], start=n == 0, stop=n == 3 * KD - 1)
                            n += 1
                last.then_inc(summed, 1)

            @block.scalar
            def _(act):
                act.wait_ge(w_in, 16)
                nc.scalar.copy(whi[:], raw[:]).then_inc(hi_done, 1)
                act.wait_ge(shifted, 1)
                nc.scalar.activation(g_exp, g_exp, ACT.Exp).then_inc(exped, 1)
                act.wait_ge(shifted, 2)
                nc.scalar.activation(prob, prob, ACT.Exp).then_inc(exped, 1)

            @block.vector
            def _(dve):
                link = chained(dve, chain)

                def tt(o, a, b, op):
                    link(nc.vector.tensor_tensor(o, a, b, op))

                def wide(v):
                    return bcast(v.unsqueeze(2), [P, TB, MOE_G])

                rank = bcast(core.const[:, C_RANK:C_RANK + 4].unsqueeze(1), [P, TB, 4])

                def first_best(o, v, top):
                    link(nc.vector.tensor_reduce(top, v, AX, ALU.max))
                    tt(pos, v, wide(top), ALU.is_equal)
                    tt(pos, pos, rank, ALU.mult)
                    link(nc.vector.tensor_reduce(best, pos, AX, ALU.max))
                    tt(o, pos, wide(best), ALU.is_equal)

                dve.wait_ge(hi_done, 1)
                nc.vector.tensor_tensor(wlo[:], raw[:], whi[:].bitcast(F32), ALU.subtract).then_inc(lo_done, 1)
                dve.wait_ge(summed, 1)
                bias = bcast(core.par2[:, G_BIAS:G_BIAS + ROUTES].unsqueeze(1), [P, TB, ROUTES])
                tt(logit[:], ps[:].rearrange("p (t r) -> p t r", t=TB), bias, ALU.add)
                g_logit = logit[:, :, 0:MOE_G]
                first_best(one_g, g_logit, g_max)
                nc.vector.tensor_tensor(g_exp, g_logit, wide(g_max), ALU.subtract).then_inc(shifted, 1)
                e_logit = logit[:, :, MOE_G:ROUTES].rearrange("p t (g e) -> p t g e", g=MOE_G)
                chosen = bcast(one_g.unsqueeze(3), [P, TB, MOE_G, MOE_E])
                tt(grid[:], e_logit, chosen, ALU.mult)
                link(nc.vector.tensor_reduce(e_sel, grid[:].rearrange("p t g e -> p t e g"), AX, ALU.add))
                link(nc.vector.tensor_reduce(e_max, e_sel, AX, ALU.max))
                nc.vector.tensor_tensor(prob, e_sel, wide(e_max), ALU.subtract).then_inc(shifted, 1)
                dve.wait_ge(exped, 2)
                link(nc.vector.tensor_reduce(g_prob, g_exp, AX, ALU.add))
                link(nc.vector.reciprocal(g_prob, g_prob))
                link(nc.vector.tensor_reduce(e_sum, prob, AX, ALU.add))
                link(nc.vector.reciprocal(e_sum, e_sum))
                tt(prob, prob, wide(e_sum), ALU.mult)
                first_best(one_1, prob, p1)
                link(nc.vector.scalar_tensor_tensor(left, one_1, -2.0, prob, ALU.mult, ALU.add))
                first_best(one_2, left, p2)
                tt(pair, one_1, one_2, ALU.add)
                tt(pair, pair, prob, ALU.mult)
                tt(p1, p1, p2, ALU.add)
                link(nc.vector.reciprocal(p1, p1))
                tt(pair, pair, wide(p1), ALU.mult)
                tt(pair, pair, wide(g_prob), ALU.mult)
                out = gates[:].rearrange("p t (g e) -> p t g e", g=MOE_G)
                tt(out, chosen, bcast(pair.unsqueeze(2), [P, TB, MOE_G, MOE_E]), ALU.mult)


def second_block(core, w):
    nc = core.nc
    x = core.x
    with ExitStack() as blk:
        core.par2 = core.sb("par2", [P, PAR2_COLS], ctx=blk)
        core.feature2 = core.sb("feature2", [P, FEATURE_COLS], ctx=blk)
        gain = core.sb("norm_gain2", [P, KD], ctx=blk)
        with ExitStack() as st:
            par_in = core.sem("par2_in", st)
            with nc.Block() as block:
                @block.sync
                def _(sp):
                    sp.dma_start(core.par2[:], w["params2"].partition_broadcast(P)).then_inc(par_in, 16)
                    sp.dma_start(core.feature2[:], w["feature2"]).then_inc(par_in, 16)
                    sp.wait_ge(par_in, 32)

        with ExitStack() as mix:
            gate_t = core.sb("gate_t", [P, 2 * KD, SEQ], ctx=mix)
            a_hi = core.sb("a_hi", [P, SQT, SEQ], F32R, ctx=mix)
            a_lo = core.sb("a_lo", [P, SQT, SEQ], F32R, ctx=mix)
            u_t = core.sb("u_t", [P, SQT, SEQ], ctx=mix)
            FT = FEAT_COLS // P
            with ExitStack() as at:
                qkv = core.sb("qkv", [P, TB, 3 * ATTN2], ctx=at)
                with ExitStack() as b:
                    hi = core.sb("h2_hi", [P, KD, SEQ], F32R, ctx=b)
                    lo = core.sb("h2_lo", [P, KD, SEQ], F32R, ctx=b)
                    transpose_split(core, "m1", x, hi, lo, KD, gain, w["norm2"][0], norm=True)
                    project(core, "u2", hi, lo, lambda c: w["w_u2"][c], SSM // FEAT_COLS, FEAT_COLS,
                            by_feature=lambda c, t, sums: nc.scalar.copy(u_t[:, c * FT + t, :], sums))
                    project(core, "gate2", hi, lo, lambda c: w["w_gates2"][c], 2 * D // FEAT_COLS, FEAT_COLS,
                            by_feature=lambda c, t, sums: nc.scalar.activation(
                                gate_t[:, c * FT + t, :], sums, ACT.Sigmoid,
                                bias=core.feature2[:, bass.ds(c * FT + (F_GATE + t), 1)]))
                    project(core, "qkv2", hi, lo, lambda c: w["w_qkv2"][c], QKV_CHUNKS, QKV_COLS,
                            by_token=lambda c, t, sums: nc.vector.tensor_copy(qkv[:, t, bass.ds(c * QKV_COLS, QKV_COLS)], sums))
                T = core.sb("qk2_t", [HEAD, 2 * HEADS2, SEQ], ctx=at)
                o = core.sb("o2", [P, TB, ATTN2], ctx=at)
                prepare_second(core, qkv, T)
                chunk = core.const[:, C_CHUNK:C_CHUNK + P]
                attention(core, "rel", HEADS2, HEAD, lambda j: T[:, j, :], lambda j, n: T[:, HEADS2 + j, 0:n],
                          lambda j, b: qkv[:, b, bass.ds(j * HEAD + 2 * ATTN2, HEAD)], HEAD ** -0.5,
                          lambda j, i, s: [(s[:, (TB - 1 - i) * P:TB * P], 0), (chunk, i * P)],
                          lambda j, i: o[:, i, bass.ds(j * HEAD, HEAD)], bias_dram=lambda j: w["rel"][j])
                transpose_split(core, "at", o, a_hi, a_lo, SQT)
            core.clear()
            z = core.sb("z", [P, SQT, SEQ], ctx=mix)
            with ExitStack() as ss:
                mag = core.sb("mag", [P, ST], ctx=ss)
                cos_t = core.sb("cos_t", [P, ST, SEQ], ctx=ss)
                sin_t = core.sb("sin_t", [P, ST, SEQ], ctx=ss)
                b_t = core.sb("b_t", [P, 2, SQT, P], ctx=ss)
                c_t = core.sb("c_t", [P, 2, ST, 2 * GROUP], ctx=ss)
                discretise(core, w, mag, cos_t, sin_t, b_t, c_t)
                state_space(core, u_t, mag, cos_t, sin_t, b_t, c_t, z)
            s_hi = core.sb("s_hi", [P, SQT, SEQ], F32R, ctx=mix)
            s_lo = core.sb("s_lo", [P, SQT, SEQ], F32R, ctx=mix)
            with ExitStack() as gl:
                glu = core.sb("glu", [P, SQT, SEQ], ctx=gl)
                split(core, "z", z, s_hi, s_lo, SQT)
                project(core, "glu", s_hi, s_lo, lambda c: w["w_glu2"][c], SSM // FEAT_COLS, FEAT_COLS, kd=SQT,
                        by_feature=lambda c, t, sums: nc.scalar.activation(
                            glu[:, c * FT + t, :], sums, ACT.Sigmoid, bias=core.feature2[:, c * FT + F_GLU + t:c * FT + F_GLU + t + 1]))
                split(core, "zg", z, s_hi, s_lo, SQT, b=glu, op=ALU.mult, res=glu)
            core.clear()

            def gated(half):
                def emit(c, t, sums):
                    g = gate_t[:, c * FT + (half * KD + t), :]
                    return nc.vector.tensor_tensor(g, sums, g, ALU.mult)
                return emit
            project(core, "bra", a_hi, a_lo, lambda c: w["w_branch_a2"][c], D // FEAT_COLS, FEAT_COLS, kd=SQT,
                    by_feature_dve=gated(0))
            project(core, "brs", s_hi, s_lo, lambda c: w["w_branch_s2"][c], D // FEAT_COLS, FEAT_COLS, kd=SQT,
                    by_feature_dve=gated(1))
            with ExitStack() as b:
                hi = core.sb("m_hi", [P, KD, SEQ], F32R, ctx=b)
                lo = core.sb("m_lo", [P, KD, SEQ], F32R, ctx=b)
                merged = gate_t[:, 0:KD, :]
                split(core, "mg", merged, hi, lo, KD, b=gate_t[:, KD:2 * KD, :], op=ALU.add, res=merged)
                project(core, "out2", hi, lo, lambda c: w["w_out2"][c], D // FEAT_COLS, FEAT_COLS,
                        by_token=lambda c, t, sums: add_to_x(core, c, t, sums, FEAT_COLS))
        with ExitStack() as b:
            hi = core.sb("e_hi", [P, KD, SEQ], F32R, ctx=b)
            lo = core.sb("e_lo", [P, KD, SEQ], F32R, ctx=b)
            gates = core.sb("gates", [P, TB, EXPERTS], ctx=b)
            transpose_split(core, "m2", x, hi, lo, KD, gain, w["norm2"][1], norm=True)
            route(core, w, hi, lo, gates)
            feed_forward(core, "moe", hi, lo, EXPERTS, lambda e: w["w_e_gate2"][e], lambda e: w["w_e_up2"][e],
                         lambda e: w["w_e_down2"][e], weight=lambda t, e: gates[:, t, bass.ds(e, 1)])
        core.clear()


def build(nc, w, out):
    with ExitStack() as ctx:
        core = Core(nc, ctx)
        core.x = core.sb("x", [P, TB, D])
        core.const = core.sb("const", [P, C_COLS])
        with ExitStack() as st:
            x_in = core.sem("x_in", st)
            with nc.Block() as block:
                @block.sync
                def _(sp):
                    sp.dma_start(core.x[:], w["x"].rearrange("a (t p) d -> p (a t) d", p=P)).then_inc(x_in, 16)
                    sp.dma_start(core.const[:], w["const"]).then_inc(x_in, 16)
                    sp.wait_ge(x_in, 32)
            core.clear()
        with nc.Fori(0, DEPTH) as layer:
            first_block(core, w, layer)
        second_block(core, w)
        with ExitStack() as st:
            stored = core.sem("stored", st)
            with nc.Block() as block:
                @block.sync
                def _(sp):
                    sp.dma_start(out.rearrange("a (t p) d -> p (a t) d", p=P), core.x[:]).then_inc(stored, 16)
                    sp.wait_ge(stored, 16)


def constants():
    import numpy as np
    f = np.float32
    r = np.arange(P)
    c = np.zeros((P, C_COLS), f)
    c[:, C_ID:C_ID + P] = np.eye(P)
    c[:, C_TRI:C_TRI + P] = r[:, None] <= r[None, :]
    c[:, C_ONE:C_ONE + P] = 1
    c[:, C_CAUSAL:C_CAUSAL + P] = np.where(r[None, :] <= r[:, None], 0, f(NEG))
    c[:, C_CHUNK:C_CHUNK + P] = np.where(r[None, :] // 64 <= r[:, None] // 64, 0, f(NEG))
    table = []
    for d in (HEAD, DIFF_D):
        rot = d // 4
        inv = (1.0 / (f(500000.0) ** (np.arange(0, rot, 2, dtype=f) / f(rot)))).astype(f)
        ang = np.arange(SEQ, dtype=f)[:, None] * inv[None, :]
        table += [np.cos(ang), np.sin(ang)]
    rope = np.concatenate(table, 1).reshape(TB, P, ROPE_COLS).transpose(1, 0, 2)
    c[:, C_ROPE:C_ROPE + TB * ROPE_COLS] = rope.reshape(P, -1)
    c[:HEAD, C_FOX] = HEAD ** -0.5
    c[HEAD:HEAD + 2, C_FOX] = 1
    c[:, C_RANK:C_RANK + 4] = [4, 3, 2, 1]
    return c


def kernel(**inputs):
    import numpy as np
    import concourse.bacc as bacc
    from concourse.bass_utils import run_bass_kernel_spmd as run

    a = {k: np.asarray(v) for k, v in inputs.items()}

    def chunks(m, n, cols):
        m = np.pad(m, [(0, 0)] * (m.ndim - 1) + [(0, n * cols - m.shape[-1])])
        m = m.reshape(*m.shape[:-2], m.shape[-2] // P, P, n, cols)
        nd = m.ndim
        m = m.transpose(*range(nd - 4), nd - 2, nd - 3, nd - 4, nd - 1)
        return m.reshape(*m.shape[:-2], -1)

    def rows(m, groups):
        m = m.reshape(*m.shape[:-2], groups, -1, P, m.shape[-1])
        m = m.swapaxes(-3, -2)
        return m.reshape(*m.shape[:-2], -1)

    def per_feature(g):
        return g.reshape(*g.shape[:-1], -1, P).swapaxes(-1, -2)

    lam = np.array([[0.8 - 0.6 * math.exp(-0.3 * l), 1 - (0.8 - 0.6 * math.exp(-0.3 * l))] for l in range(DEPTH)], np.float32)
    gu = a["w_gate_up"]
    w = {
        "x": a["x"], "const": constants(), "lam": lam,
        "params": np.concatenate([a[n] for n, _ in PARAMS], 1),
        "attn_norm": per_feature(a["attn_norm"]), "ffn_norm": per_feature(a["ffn_norm"]),
        "w_in": chunks(a["w_in"], IN_CHUNKS, IN_COLS), "w_out": chunks(a["w_out"], OUT_CHUNKS, OUT_COLS),
        "w_gate": chunks(gu[:, :, :FFN], FFN_GROUPS, HID), "w_up": chunks(gu[:, :, FFN:], FFN_GROUPS, HID),
        "w_down": rows(a["w_down"], FFN_GROUPS),
    }
    b = {k[:-2]: v[0] for k, v in a.items() if k.endswith("_2")}
    rel = np.clip(np.arange(P)[:, None] - np.arange(SEQ)[None, :] + SEQ - P, -REL_FUTURE, MAX_REL) + REL_FUTURE

    def by_state(m):
        m = m.reshape(ST, P, *m.shape[2:])
        return m.swapaxes(0, 1)

    def block_diagonal(m):
        wide = np.zeros((ST, 2, STATE, 2, GROUP), m.dtype)
        for n in range(2):
            wide[:, n, :, n] = m.reshape(ST, 2, STATE, GROUP)[:, n]
        return wide.reshape(ST, P, 2 * GROUP).swapaxes(0, 1)

    w.update({
        "params2": np.concatenate([b["q_gain"], b["k_gain"], b["group_bias"], b["expert_bias"]]),
        "norm2": np.stack([per_feature(b["mix_norm_gain"]), per_feature(b["ffn_norm_gain"])]),
        "rel": b["rel_bias"][:, rel],
        "w_qkv2": chunks(b["w_in"][:, :3 * ATTN2], QKV_CHUNKS, QKV_COLS),
        "w_u2": chunks(b["w_in"][:, 3 * ATTN2:3 * ATTN2 + SSM], SSM // FEAT_COLS, FEAT_COLS),
        "w_gates2": chunks(b["w_in"][:, 3 * ATTN2 + SSM:], 2 * D // FEAT_COLS, FEAT_COLS),
        "feature2": np.concatenate([per_feature(b["b_gate"]), per_feature(b["b_glu"]), per_feature(b["ssm_d"])], 1),
        "w_glu2": chunks(b["w_glu"], SSM // FEAT_COLS, FEAT_COLS),
        "w_branch_a2": chunks(b["w_branch"][:ATTN2], D // FEAT_COLS, FEAT_COLS),
        "w_branch_s2": chunks(b["w_branch"][ATTN2:], D // FEAT_COLS, FEAT_COLS),
        "w_out2": chunks(b["w_out"], D // FEAT_COLS, FEAT_COLS),
        "lambda2": np.concatenate([by_state(b["ssm_lambda_re"]), by_state(b["ssm_lambda_im"])], 1),
        "log_step2": b["ssm_log_step"].reshape(ST, 2).T,
        "b_diag2": np.stack([block_diagonal(b["ssm_b_re"]), block_diagonal(b["ssm_b_im"])], 1).reshape(P, -1),
        "c_diag2": np.stack([block_diagonal(b["ssm_c_re"].swapaxes(1, 2)),
                             block_diagonal(b["ssm_c_im"].swapaxes(1, 2))], 1).reshape(P, -1),
        "w_route2": chunks(np.concatenate([b["w_group_router"], b["w_expert_router"]], 1), 1, ROUTES)[0],
        "w_e_gate2": chunks(b["w_e_gate"], 1, HID)[:, 0], "w_e_up2": chunks(b["w_e_up"], 1, HID)[:, 0],
        "w_e_down2": rows(b["w_e_down"], 1)[:, 0],
    })
    nc = bacc.Bacc("TRN2", target_bir_lowering=False, num_devices=1)
    arrays = {f"in_{k}": np.ascontiguousarray(v) for k, v in w.items()}
    args = {k: nc.dram_tensor(f"in_{k}", list(arrays[f"in_{k}"].shape), F32, kind="ExternalInput").ap() for k in w}
    out = nc.dram_tensor("out_x", [1, SEQ, D], F32, kind="ExternalOutput").ap()
    build(nc, args, out)
    return run(nc, [arrays], core_ids=[0]).results[0]["out_x"]
```

```python
import math
from contextlib import ExitStack

import concourse.bass as bass
from concourse import mybir

F32 = mybir.dt.float32
F32R = mybir.dt.float32r
ALU = mybir.AluOpType
ACT = mybir.ActivationFunctionType
AX = mybir.AxisListType.X

P = 128
SEQ = 512
TB = SEQ // P
D = 1024
KD = D // P
DEPTH = 2
NORM_EPS = 1e-6
NEG = -1e30
TAKEN = -3e38
TAKEN_EDGE = -2e38

HEAD = 64
FOX = 6
DIFF = 4
DIFF_D = 32
DSA = 6
IDX = 4
TOPK = min(256, SEQ // 4)
SPLITS = (FOX * HEAD, FOX * HEAD, FOX * HEAD, FOX, DIFF * 2 * DIFF_D, DIFF * 2 * DIFF_D, DIFF * HEAD,
          DSA * HEAD, HEAD, HEAD, IDX * HEAD, HEAD, IDX)
FQ, FK, FV, FF, DQ, DK, DV, SQ, SK, SV, IQ, IK, IW = (sum(SPLITS[:n]) for n in range(len(SPLITS)))
IN_WIDTH = sum(SPLITS)
IN_CHUNKS = 6
IN_COLS = -(-IN_WIDTH // (2 * IN_CHUNKS)) * 2
OUT_COLS = 512
OUT_CHUNKS = D // OUT_COLS
HID = 256
HB = HID // P
FFN = -(-8 * D // (3 * 256)) * 256
FFN_GROUPS = FFN // HID

HEADS2 = 8
ATTN2 = HEADS2 * HEAD
REL_FUTURE = 63
MAX_REL = 256
SSM = D // 2
GROUPS, GROUP, STATE = 32, 16, 64
ST = GROUPS * STATE // P
SQT = SSM // P
PER = ST // SQT
QKV_COLS, QKV_CHUNKS = 384, 4
FEAT_COLS = 256
MOE_G, MOE_E = 4, 4
EXPERTS = MOE_G * MOE_E
ROUTES = MOE_G + EXPERTS

C_ID, C_TRI, C_ONE, C_CHUNK, C_CAUSAL = 0, P, 2 * P, 3 * P, 4 * P
C_ROPE = C_CAUSAL + SEQ
ROPE64, ROPE32 = HEAD // 8, DIFF_D // 8
ROPE_COLS = 2 * ROPE64 + 2 * ROPE32
C_FOX = C_ROPE + TB * ROPE_COLS
C_RANK = C_FOX + 1
C_COLS = C_RANK + 4

PARAMS = (("fox_qn", HEAD), ("fox_kn", HEAD), ("diff_qn", DIFF_D), ("diff_kn", DIFF_D),
          ("diff_lq1", DIFF_D), ("diff_lk1", DIFF_D), ("diff_lq2", DIFF_D), ("diff_lk2", DIFF_D),
          ("diff_subln", HEAD), ("dsa_qn", HEAD), ("dsa_kn", HEAD), ("fox_fb", FOX))
PAR = {name: sum(n for _, n in PARAMS[:i]) for i, (name, _) in enumerate(PARAMS)}
PAR_COLS = sum(n for _, n in PARAMS)

U_FQ, U_FK, U_DQ, U_DK, U_SQ, U_SK, U_IQ, U_IK = 0, 6, 12, 20, 28, 34, 35, 39
UNITS = 40


class Core:

    def __init__(self, nc, ctx):
        self.nc, self.ctx = nc, ctx

    def sb(self, name, shape, dt=F32, ctx=None):
        return (ctx or self.ctx).enter_context(self.nc.sbuf_tensor(name, shape, dt))

    def psum(self, name, shape, ctx):
        return ctx.enter_context(self.nc.psum_tensor(name, shape, F32))

    def sem(self, name, ctx):
        s = ctx.enter_context(self.nc.semaphore(name))
        self.to_clear.append(s)
        return s

    def clear(self):
        for s in self.to_clear:
            self.nc.gpsimd.sem_clear(s)
        self.to_clear = []
        self.nc.all_engine_barrier()

    to_clear = []


def chained(engine, sem):
    count = [0]

    def link(ins):
        count[0] += 1
        ins.then_inc(sem, 1)
        engine.wait_ge(sem, count[0])

    return link


def inverse_root(nc, link, v, root, t):
    link(nc.vector.reciprocal(root, root))
    link(nc.vector.tensor_tensor(t, root, root, ALU.mult))
    link(nc.vector.tensor_tensor(t, t, v, ALU.mult))
    link(nc.vector.tensor_scalar(t, t, -0.5, 1.5, ALU.mult, ALU.add))
    link(nc.vector.tensor_tensor(root, root, t, ALU.mult))


def pairs(engine, n, step, peel_last=False):
    step(0, 0, True)
    step(1, 1, True)
    turns = (n - (4 if peel_last else 2)) // 2
    if turns > 0:
        with engine.Fori(0, turns) as turn:
            step(2 * turn + 2, 0, False)
            step(2 * turn + 3, 1, False)
    for i in range(2 + 2 * max(turns, 0), n):
        step(i, i % 2, False)


class Weights:

    def __init__(self, core, name, dram, chunks, cols, ctx, kd=KD, raw=None, width=None):
        self.dram, self.chunks, self.cols, self.kd = dram, chunks, cols, kd
        self.flat = raw or [core.sb(f"{name}_raw{s}", [P, width or kd * cols], ctx=ctx) for s in range(2)]
        self.raw = [t[:, 0:kd * cols].rearrange("p (k n) -> p k n", k=kd) for t in self.flat]
        self.loaded = [core.sem(f"{name}_loaded{s}", ctx) for s in range(2)]
        self.started = False

    def load(self, sp, c, s):
        sp.dma_start(self.flat[s][:, 0:self.kd * self.cols], self.dram(c)).then_inc(self.loaded[s], 16)

    def ahead(self, sp, s=None):
        self.started = True
        for slot in range(2) if s is None else (s,):
            self.load(sp, slot, slot)


def transpose_split(core, name, src, hi, lo, tiles, gain=None, gain_dram=None, norm=False, ahead=None):
    nc = core.nc
    with ExitStack() as st:
        scratch = [core.sb(f"{name}_squares{t}", [P, D], ctx=st) for t in range(TB)] if norm else None
        xs = core.sb(f"{name}_normed", [P, TB, D], ctx=st) if norm else src
        ss = core.sb(f"{name}_ss", [P, TB], ctx=st)
        rstd = core.sb(f"{name}_rstd", [P, TB], ctx=st)
        half = core.sb(f"{name}_half", [P, TB], ctx=st)
        banks = [core.psum(f"{name}_ps{b}", [P, SEQ], st) for b in range(4)]
        gain_in = core.sem(f"{name}_gain_in", st)
        squared = core.sem(f"{name}_squared", st)
        squared_dve = core.sem(f"{name}_squared_dve", st)
        rooted = core.sem(f"{name}_rooted", st)
        scaled = core.sem(f"{name}_scaled", st)
        turned = core.sem(f"{name}_turned", st)
        hi_done = core.sem(f"{name}_hi_done", st)
        lo_done = core.sem(f"{name}_lo_done", st)
        ident = core.const[:, C_ID:C_ID + P]
        with nc.Block() as block:
            @block.sync
            def _(sp):
                if gain is not None:
                    sp.dma_start(gain[:], gain_dram).then_inc(gain_in, 16)
                if ahead:
                    ahead(sp)

            if norm:
                @block.gpsimd
                def _(pool):
                    nc.gpsimd.memset(half[:], -0.5).then_inc(rooted, 1)
                    for t in range(TB):
                        pool.wait_ge(squared_dve if t % 2 else squared, t // 2 + 1)
                        s_t = ss[:, t:t + 1]
                        nc.gpsimd.tensor_scalar(s_t, s_t, 1.0 / D, NORM_EPS, ALU.mult, ALU.add).then_inc(rooted, 1)
                        pool.wait_ge(rooted, 2 * t + 2)
                        nc.gpsimd.tensor_tensor(rstd[:, t:t + 1], s_t, half[:, t:t + 1], ALU.pow).then_inc(rooted, 1)

            @block.scalar
            def _(act):
                if norm:
                    for t in range(0, TB, 2):
                        nc.scalar.activation(scratch[t][:], src[:, t, :], ACT.Square,
                                             accum_out=ss[:, t:t + 1]).then_inc(squared, 1)
                if gain is not None:
                    act.wait_ge(gain_in, 16)
                for k in range(tiles):
                    act.wait_ge(turned, k + 1)
                    if gain is None:
                        nc.scalar.copy(hi[:, k, :], banks[k % 4][:]).then_inc(hi_done, 1)
                    else:
                        nc.scalar.activation(hi[:, k, :], banks[k % 4][:], ACT.Copy,
                                             scale=gain[:, k:k + 1]).then_inc(hi_done, 1)

            @block.vector
            def _(dve):
                if norm:
                    for t in range(1, TB, 2):
                        nc.vector.tensor_tensor_reduce(out=scratch[t][:], in0=src[:, t, :], in1=src[:, t, :], scale=1.0,
                                                       scalar=0.0, op0=ALU.mult, op1=ALU.add,
                                                       accum_out=ss[:, t:t + 1]).then_inc(squared_dve, 1)
                    for t in range(TB):
                        dve.wait_ge(rooted, 2 * t + 3)
                        nc.vector.tensor_scalar(xs[:, t, :], src[:, t, :], rstd[:, t:t + 1], None,
                                                ALU.mult).then_inc(scaled, 1)
                if gain is not None:
                    dve.wait_ge(gain_in, 16)
                for k in range(tiles):
                    dve.wait_ge(hi_done, k + 1)
                    hi_k = hi[:, k, :].bitcast(F32)
                    if gain is None:
                        nc.vector.tensor_tensor(lo[:, k, :], banks[k % 4][:], hi_k, ALU.subtract).then_inc(lo_done, 1)
                    else:
                        nc.vector.scalar_tensor_tensor(lo[:, k, :], banks[k % 4][:], gain[:, k:k + 1], hi_k,
                                                       ALU.mult, ALU.subtract).then_inc(lo_done, 1)

            @block.tensor
            def _(pe):
                def turn(k, t):
                    last = nc.tensor.transpose(banks[k % 4][:, t * P:(t + 1) * P], xs[:, t, k * P:(k + 1) * P], ident)
                    if t == TB - 1:
                        last.then_inc(turned, 1)

                early = 4 if norm else 0
                for t in range(TB if norm else 0):
                    pe.wait_ge(scaled, t + 1)
                    for k in range(early):
                        turn(k, t)
                for k in range(early, tiles):
                    if k >= 4:
                        pe.wait_ge(lo_done, k - 3)
                    for t in range(TB):
                        turn(k, t)


def project(core, name, hi, lo, w, by_token=None, by_feature=None, by_feature_dve=None, ahead=None):
    nc = core.nc
    chunks, cols, kd, raw, loaded = w.chunks, w.cols, w.kd, w.raw, w.loaded
    tiles = TB if by_token else cols // P
    width = cols if by_token else SEQ
    with ExitStack() as st:
        whi = [core.sb(f"{name}_whi{s}", [P, kd, cols], F32R, ctx=st) for s in range(2)]
        wlo = [core.sb(f"{name}_wlo{s}", [P, kd, cols], F32R, ctx=st) for s in range(2)]
        banks = [[core.psum(f"{name}_ps{s}{t}", [P, 512], st) for t in range(tiles)] for s in range(2)]
        hi_done = core.sem(f"{name}_whi_done", st)
        lo_done = core.sem(f"{name}_wlo_done", st)
        summed = core.sem(f"{name}_summed", st)
        out_done = core.sem(f"{name}_out_done", st)
        H = kd // 2

        with nc.Block() as block:
            @block.sync
            def _(sp):
                def step(c, s, first):
                    if not first:
                        sp.wait_ge(lo_done, 2 * (c - 1))
                    if not (first and w.started):
                        w.load(sp, c, s)
                pairs(sp, chunks, step)
                if ahead:
                    for c in (chunks - 2, chunks - 1):
                        sp.wait_ge(lo_done, 2 * (c + 1))
                        ahead.ahead(sp, c % 2)

            def split_hi(act, c, s, first):
                act.wait_ge(loaded[s], 16 * (c // 2) + 16)
                if not first:
                    act.wait_ge(summed, tiles * (c - 1))
                for h in range(2):
                    nc.scalar.copy(whi[s][:, h * H:(h + 1) * H, :], raw[s][:, h * H:(h + 1) * H, :]).then_inc(hi_done, 1)

            def split_lo(dve, c, s, first):
                if not first:
                    dve.wait_ge(summed, tiles * (c - 1))
                for h in range(2):
                    dve.wait_ge(hi_done, 2 * c + h + 1)
                    nc.vector.tensor_tensor(wlo[s][:, h * H:(h + 1) * H, :], raw[s][:, h * H:(h + 1) * H, :],
                                            whi[s][:, h * H:(h + 1) * H, :].bitcast(F32),
                                            ALU.subtract).then_inc(lo_done, 1)

            def take_out(engine, emit, c, s):
                for t in range(tiles):
                    engine.wait_ge(summed, tiles * c + t + 1)
                    emit(c, t, banks[s][t][:, 0:width]).then_inc(out_done, 1)

            @block.scalar
            def _(act):
                def step(c, s, first):
                    split_hi(act, c, s, first)
                    if by_feature and not (isinstance(c, int) and c == 0):
                        take_out(act, by_feature, c - 1, 1 - s)
                pairs(act, chunks, step)
                if by_feature:
                    take_out(act, by_feature, chunks - 1, (chunks - 1) % 2)

            @block.vector
            def _(dve):
                emit = by_token or by_feature_dve

                def step(c, s, first):
                    split_lo(dve, c, s, first)
                    if emit and not (isinstance(c, int) and c == 0):
                        take_out(dve, emit, c - 1, 1 - s)
                pairs(dve, chunks, step)
                if emit:
                    take_out(dve, emit, chunks - 1, (chunks - 1) % 2)

            @block.tensor
            def _(pe):
                def step(c, s, first):
                    for t in range(tiles):
                        if not first:
                            pe.wait_ge(out_done, tiles * (c - 2) + t + 1)
                        n = 0
                        for k in range(kd):
                            if t == 0 and k % H == 0:
                                pe.wait_ge(lo_done, 2 * c + k // H + 1)
                            for aw, ww in ((hi, whi[s]), (lo, whi[s]), (hi, wlo[s])):
                                if by_token:
                                    ops = aw[:, k, t * P:(t + 1) * P], ww[:, k, :]
                                else:
                                    ops = ww[:, k, t * P:(t + 1) * P], aw[:, k, :]
                                last = nc.tensor.matmul(banks[s][t][:, 0:width], *ops, start=n == 0, stop=n == 3 * kd - 1)
                                n += 1
                        last.then_inc(summed, 1)
                pairs(pe, chunks, step)


def add_to_x(core, c, t, sums, cols):
    x_ct = core.x[:, t, bass.ds(c * cols, cols)]
    return core.nc.vector.tensor_tensor(x_ct, sums, x_ct, ALU.add)


def split(core, name, a, hi, lo, tiles, b=None, op=None, res=None, ahead=None):
    nc = core.nc
    with ExitStack() as st:
        made = core.sem(f"{name}_made", st)
        hi_done = core.sem(f"{name}_hi_done", st)
        lo_done = core.sem(f"{name}_lo_done", st)
        full = a if b is None else res
        with nc.Block() as block:
            if ahead:
                @block.sync
                def _(sp):
                    ahead(sp)

            @block.scalar
            def _(act):
                for k in range(tiles):
                    if b is not None:
                        act.wait_ge(made, k + 1)
                    nc.scalar.copy(hi[:, k, :], full[:, k, :]).then_inc(hi_done, 1)

            @block.vector
            def _(dve):
                if b is not None:
                    for k in range(tiles):
                        nc.vector.tensor_tensor(full[:, k, :], a[:, k, :], b[:, k, :], op).then_inc(made, 1)
                for k in range(tiles):
                    dve.wait_ge(hi_done, k + 1)
                    nc.vector.tensor_tensor(lo[:, k, :], full[:, k, :], hi[:, k, :].bitcast(F32),
                                            ALU.subtract).then_inc(lo_done, 1)


class GroupWeights:

    def __init__(self, core, name, gate_dram, up_dram, down_dram, ctx):
        self.gate_up = core.sb(f"{name}_raw_gu", [P, 2, KD, HID], ctx=ctx)
        self.down = core.sb(f"{name}_raw_d", [P, HB, D], ctx=ctx)
        self.loaded = [core.sem(f"{name}_{part}_in", ctx) for part in ("gate", "up", "down")]
        self.dram = gate_dram, up_dram, down_dram
        self.started = False

    def load(self, sp, g, m):
        dst = (self.gate_up[:, 0], self.gate_up[:, 1], self.down[:])[m]
        sp.dma_start(dst.rearrange("p k n -> p (k n)"), self.dram[m](g)).then_inc(self.loaded[m], 16)

    def ahead(self, sp):
        self.started = True
        for m in range(3):
            self.load(sp, 0, m)


def feed_forward(core, name, hi, lo, groups, w, weight=None, beside=None):
    nc = core.nc
    x = core.x
    KH = KD // 2
    with ExitStack() as st:
        gu_hi = [core.sb(f"{name}_gu_hi{s}", [P, 2, KD, HID], F32R, ctx=st) for s in range(2)]
        gu_lo = [core.sb(f"{name}_gu_lo{s}", [P, 2, KD, HID], F32R, ctx=st) for s in range(2)]
        d_hi = [core.sb(f"{name}_d_hi{s}", [P, HB, D], F32R, ctx=st) for s in range(2)]
        d_lo = [core.sb(f"{name}_d_lo{s}", [P, HB, D], F32R, ctx=st) for s in range(2)]
        act_t = core.sb(f"{name}_silu", [P, HB, SEQ], ctx=st)
        hid_hi = [core.sb(f"{name}_hid_hi{s}", [P, HB, SEQ], F32R, ctx=st) for s in range(2)]
        hid_lo = [core.sb(f"{name}_hid_lo{s}", [P, HB, SEQ], F32R, ctx=st) for s in range(2)]
        up_ps = [[core.psum(f"{name}_up{m}{b}", [P, SEQ], st) for b in range(HB)] for m in range(2)]
        down_ps = [core.psum(f"{name}_down{b}", [P, 512], st) for b in range(4)]
        gate_in, up_in, down_in = w.loaded
        raw_gu, raw_d = w.gate_up, w.down
        hi_done = core.sem(f"{name}_w_hi_done", st)
        lo_done = core.sem(f"{name}_w_lo_done", st)
        up_sum = core.sem(f"{name}_up_sum", st)
        down_sum = core.sem(f"{name}_down_sum", st)
        silu_done = core.sem(f"{name}_silu_done", st)
        prod_done = core.sem(f"{name}_prod_done", st)
        hid_hi_done = core.sem(f"{name}_hid_hi_done", st)
        hid_lo_done = core.sem(f"{name}_hid_lo_done", st)
        added = core.sem(f"{name}_added", st)
        NT = TB * (D // 512)

        with nc.Block() as block:
            @block.sync
            def _(sp):
                def step(g, s, first):
                    start = isinstance(g, int) and g == 0
                    for m in range(3):
                        if not start:
                            sp.wait_ge(lo_done, 3 * (g - 1) + m + 1)
                        if not (start and w.started):
                            w.load(sp, g, m)
                pairs(sp, groups, step)

            def parts(s):
                return ((raw_gu[:, 0], gu_hi[s][:, 0], gu_lo[s][:, 0]), (raw_gu[:, 1], gu_hi[s][:, 1], gu_lo[s][:, 1]),
                        (raw_d[:], d_hi[s][:], d_lo[s][:]))

            @block.scalar
            def _(act):
                def hidden(g, s):
                    for b in range(HB):
                        act.wait_ge(up_sum, 2 * HB * g + 2 * b + 2)
                        if not (isinstance(g, int) and g == 0):
                            act.wait_ge(hid_lo_done, HB * (g - 1) + b + 1)
                        nc.scalar.activation(act_t[:, b, :], up_ps[0][b][:], ACT.Silu).then_inc(silu_done, 1)
                    for b in range(HB):
                        act.wait_ge(prod_done, HB * g + b + 1)
                        nc.scalar.copy(hid_hi[s][:, b, :], act_t[:, b, :]).then_inc(hid_hi_done, 1)

                def split(g, s, m, sem):
                    raw, hi_w, _ = parts(s)[m]
                    act.wait_ge(sem, 16 * (g + 1))
                    nc.scalar.copy(hi_w, raw).then_inc(hi_done, 1)

                def step(g, s, first):
                    if not first:
                        act.wait_ge(up_sum, 2 * HB * (g - 1))
                    split(g, s, 0, gate_in)
                    split(g, s, 1, up_in)
                    if beside and isinstance(g, int) and g == 1:
                        beside.on_scalar(act)
                    if not (isinstance(g, int) and g == 0):
                        hidden(g - 1, 1 - s)
                    if not first:
                        act.wait_ge(down_sum, NT * (g - 1))
                    split(g, s, 2, down_in)
                pairs(act, groups, step)
                hidden(groups - 1, (groups - 1) % 2)

            @block.vector
            def _(dve):
                def hidden(g, s):
                    for b in range(HB):
                        dve.wait_ge(silu_done, HB * g + b + 1)
                        nc.vector.tensor_tensor(act_t[:, b, :], act_t[:, b, :], up_ps[1][b][:],
                                                ALU.mult).then_inc(prod_done, 1)
                    for b in range(HB):
                        dve.wait_ge(hid_hi_done, HB * g + b + 1)
                        nc.vector.tensor_tensor(hid_lo[s][:, b, :], act_t[:, b, :], hid_hi[s][:, b, :].bitcast(F32),
                                                ALU.subtract).then_inc(hid_lo_done, 1)

                def add(g):
                    for n in range(NT):
                        t, c = n // 2, n % 2
                        x_nt = x[:, t, c * 512:(c + 1) * 512]
                        dve.wait_ge(down_sum, NT * g + n + 1)
                        if weight is None:
                            nc.vector.tensor_tensor(x_nt, down_ps[n % 4][:], x_nt, ALU.add).then_inc(added, 1)
                        else:
                            nc.vector.scalar_tensor_tensor(x_nt, down_ps[n % 4][:], weight(t, g), x_nt,
                                                           ALU.mult, ALU.add).then_inc(added, 1)

                def split(g, s, m):
                    raw, hi_w, lo_w = parts(s)[m]
                    dve.wait_ge(hi_done, 3 * g + m + 1)
                    nc.vector.tensor_tensor(lo_w, raw, hi_w.bitcast(F32), ALU.subtract).then_inc(lo_done, 1)

                def step(g, s, first):
                    if not first:
                        dve.wait_ge(up_sum, 2 * HB * (g - 1))
                    split(g, s, 0)
                    split(g, s, 1)
                    if beside and isinstance(g, int) and g == 1:
                        beside.on_vector(dve)
                    if not (isinstance(g, int) and g == 0):
                        hidden(g - 1, 1 - s)
                    if not first:
                        add(g - 2)
                    split(g, s, 2)
                pairs(dve, groups, step)
                hidden(groups - 1, (groups - 1) % 2)
                add(groups - 2)
                add(groups - 1)

            @block.tensor
            def _(pe):
                def up(g, s):
                    if not (isinstance(g, int) and g == 0):
                        pe.wait_ge(prod_done, HB * g)
                    for b in range(HB):
                        for m in range(2):
                            if b == 0:
                                pe.wait_ge(lo_done, 3 * g + m + 1)
                            n = 0
                            for k in range(KD):
                                for ww, aw in ((gu_hi[s], hi), (gu_hi[s], lo), (gu_lo[s], hi)):
                                    last = nc.tensor.matmul(up_ps[m][b][:], ww[:, m, k, b * P:(b + 1) * P], aw[:, k, :],
                                                            start=n == 0, stop=n == 3 * KD - 1)
                                    n += 1
                            last.then_inc(up_sum, 1)

                def down(g, s):
                    pe.wait_ge(lo_done, 3 * g + 3)
                    pe.wait_ge(hid_lo_done, HB * g + HB)
                    for n in range(NT):
                        t, c = n // 2, n % 2
                        if not (isinstance(g, int) and g == 0) or n >= 4:
                            pe.wait_ge(added, NT * g + n - 3)
                        i = 0
                        for k in range(HB):
                            for aw, ww in ((hid_hi[s], d_hi[s]), (hid_lo[s], d_hi[s]), (hid_hi[s], d_lo[s])):
                                last = nc.tensor.matmul(down_ps[n % 4][:], aw[:, k, t * P:(t + 1) * P],
                                                        ww[:, k, c * 512:(c + 1) * 512], start=i == 0, stop=i == 3 * HB - 1)
                                i += 1
                        last.then_inc(down_sum, 1)

                def step(g, s, first):
                    up(g, s)
                    if not (isinstance(g, int) and g == 0):
                        down(g - 1, 1 - s)
                pairs(pe, groups, step)
                down(groups - 1, (groups - 1) % 2)


def attention(core, name, heads, rows, q_of, k_of, v_of, scale, bias_of, out_of, bias_dram=None, beside=None, after=None):
    nc = core.nc
    with ExitStack() as st:
        q_slot = [core.sb(f"{name}_q{s}", [rows, SEQ], ctx=st) for s in range(2)]
        prob = [core.sb(f"{name}_p{i}", [P, (i + 1) * P], ctx=st) for i in range(TB)]
        prob_t = [core.sb(f"{name}_pt{s}", [P, SEQ], ctx=st) for s in range(2)]
        neg_max = core.sb(f"{name}_neg_max", [P, TB], ctx=st)
        spare = core.sb(f"{name}_spare", [P, TB], ctx=st)
        row_sum = [core.sb(f"{name}_row_sum{s}", [P, TB], ctx=st) for s in range(2)]
        inv_sum = core.sb(f"{name}_inv_sum", [P, TB], ctx=st)
        bias_slot = [core.sb(f"{name}_bias{s}", [P, SEQ], ctx=st) for s in range(2)] if bias_dram else None
        s_ps = [core.psum(f"{name}_s{i}", [P, SEQ], st) for i in range(TB)]
        t_ps = [core.psum(f"{name}_t{s}", [P, SEQ], st) for s in range(2)]
        o_ps = [core.psum(f"{name}_o{s}", [P, HEAD], st) for s in range(2)]
        q_ready = core.sem(f"{name}_q_ready", st)
        bias_in = [core.sem(f"{name}_bias_in{s}", st) for s in range(2)]
        bias_done = core.sem(f"{name}_bias_done", st)
        scored = core.sem(f"{name}_scored", st)
        maxed = core.sem(f"{name}_maxed", st)
        exped = core.sem(f"{name}_exped", st)
        turned = core.sem(f"{name}_turned", st)
        pt_dve = core.sem(f"{name}_pt_dve", st)
        pt_act = core.sem(f"{name}_pt_act", st)
        valued = core.sem(f"{name}_valued", st)
        inverted = core.sem(f"{name}_inverted", st)
        stored = core.sem(f"{name}_stored", st)
        ident = core.const[:, C_ID:C_ID + P]

        def zero(j):
            return isinstance(j, int) and j == 0

        with nc.Block() as block:
            if bias_dram:
                @block.sync
                def _(sp):
                    def step(j, s, first):
                        if not first:
                            sp.wait_ge(maxed, TB * (j - 1))
                        sp.dma_start(bias_slot[s][:], bias_dram(j)).then_inc(bias_in[s], 16)
                    pairs(sp, heads, step)

                @block.gpsimd
                def _(pool):
                    def step(j, s, first):
                        pool.wait_ge(bias_in[s], 16 * (j // 2) + 16)
                        diag = bias_slot[s][:, SEQ - P:SEQ]
                        nc.gpsimd.tensor_tensor(diag, diag, core.const[:, C_CHUNK:C_CHUNK + P], ALU.add).then_inc(bias_done, 1)
                    pairs(pool, heads, step)

            @block.scalar
            def _(act):
                def load_q(j, s, first):
                    if not first:
                        act.wait_ge(scored, TB * (j - 1))
                    nc.scalar.activation(q_slot[s][:], q_of(j), ACT.Copy, scale=scale).then_inc(q_ready, 1)

                def exps(j, s):
                    for i in range(TB):
                        if i == TB - 1 and not zero(j):
                            copy_pt(j - 1)
                        act.wait_ge(maxed, TB * j + i + 1)
                        if not zero(j):
                            act.wait_ge(turned, TB * (j - 1) + i + 1)
                            if i == 0:
                                act.wait_ge(inverted, j - 1)
                        nc.scalar.activation(prob[i][:], s_ps[i][:, 0:(i + 1) * P], ACT.Exp, bias=neg_max[:, i:i + 1],
                                             scale=-1.0, accum_out=row_sum[s][:, i:i + 1]).then_inc(exped, 1)

                def copy_pt(j):
                    act.wait_ge(turned, TB * j + TB)
                    act.wait_ge(valued, TB * j + TB - 2)
                    nc.scalar.copy(prob_t[(TB - 1) % 2][:], t_ps[(TB - 1) % 2][:]).then_inc(pt_act, 1)

                load_q(0, 0, True)

                def step(j, s, first):
                    if not (isinstance(j, int) and j == heads - 1):
                        load_q(j + 1, 1 - s, zero(j))
                    exps(j, s)
                pairs(act, heads, step, peel_last=True)
                copy_pt(heads - 1)

            @block.vector
            def _(dve):
                def maxima(j, i, s):
                    if bias_dram and i == 0:
                        dve.wait_ge(bias_done, j + 1)
                    dve.wait_ge(scored, TB * j + i + 1)
                    nc.vector.memset(spare[:, i:i + 1], 0.0)
                    sc = s_ps[i][:, 0:(i + 1) * P]
                    nc.vector.tensor_tensor_reduce(out=sc, in0=sc, in1=bias_of(i, bias_slot[s] if bias_dram else None),
                                                   scale=-1.0, scalar=-NEG * 10, op0=ALU.add, op1=ALU.min,
                                                   accum_out=neg_max[:, i:i + 1]).then_inc(maxed, 1)

                def copy_pt(j, i):
                    dve.wait_ge(turned, TB * j + i + 1)
                    if not zero(j) or i >= 2:
                        dve.wait_ge(valued, TB * j + i - 1)
                    w = (i + 1) * P
                    nc.vector.tensor_copy(prob_t[i % 2][:, 0:w], t_ps[i % 2][:, 0:w]).then_inc(pt_dve, 1)

                def store(j, i):
                    dve.wait_ge(valued, TB * j + i + 1)
                    nc.vector.tensor_scalar(out_of(j, i), o_ps[i % 2][:], inv_sum[:, i:i + 1], None,
                                            ALU.mult).then_inc(stored, 1)

                def invert(j, s):
                    dve.wait_ge(exped, TB * j)
                    if not (isinstance(j, int) and j == 1):
                        dve.wait_ge(stored, TB * (j - 1))
                    nc.vector.reciprocal(inv_sum[:], row_sum[1 - s][:]).then_inc(inverted, 1)
                    dve.wait_ge(inverted, j)

                def step(j, s, first, scores=True):
                    for i in range(TB):
                        if i < TB - 1 and not zero(j):
                            copy_pt(j - 1, i)
                        if scores:
                            maxima(j, i, s)
                        if i == 1 and not zero(j):
                            invert(j, s)
                        if i and not zero(j):
                            store(j - 1, i - 1)
                        if scores and beside:
                            beside(dve, j, i)
                    if not zero(j):
                        store(j - 1, TB - 1)
                pairs(dve, heads, step)
                step(heads, 0, False, scores=False)
                if after:
                    after(dve)

            @block.tensor
            def _(pe):
                def score(j, i, s):
                    w = (i + 1) * P
                    last = nc.tensor.matmul(s_ps[i][:, 0:w], q_slot[s][:, i * P:(i + 1) * P], k_of(j, w), start=True, stop=True)
                    last.then_inc(scored, 1)

                def turn_probs(j, i):
                    pe.wait_ge(exped, TB * j + i + 1)
                    if i == 0 and not zero(j):
                        pe.wait_ge(pt_dve, (TB - 1) * j)
                    elif i == 1 and not zero(j):
                        pe.wait_ge(pt_act, j)
                    elif i >= 2:
                        pe.wait_ge(pt_dve, (TB - 1) * j + i - 1)
                    for b in range(i + 1):
                        last = nc.tensor.transpose(t_ps[i % 2][:, b * P:(b + 1) * P], prob[i][:, b * P:(b + 1) * P], ident)
                    last.then_inc(turned, 1)

                def value(j, i):
                    if i < TB - 1:
                        pe.wait_ge(pt_dve, (TB - 1) * j + i + 1)
                    else:
                        pe.wait_ge(pt_act, j + 1)
                    if not zero(j) or i >= 2:
                        pe.wait_ge(stored, TB * j + i - 1)
                    for b in range(i + 1):
                        last = nc.tensor.matmul(o_ps[i % 2][:], prob_t[i % 2][:, b * P:(b + 1) * P], v_of(j, b),
                                                start=b == 0, stop=b == i)
                    last.then_inc(valued, 1)

                def step(j, s, first, scores=True):
                    for i in range(TB):
                        if scores and i == 0:
                            pe.wait_ge(q_ready, j + 1)
                        if not zero(j):
                            turn_probs(j - 1, i)
                        if scores:
                            score(j, i, s)
                        if i and not zero(j):
                            value(j - 1, i - 1)
                    if not zero(j):
                        value(j - 1, TB - 1)
                pairs(pe, heads, step)
                step(heads, 0, False, scores=False)


def bcast(ap, shape):
    return ap.broadcast_to(shape)


def prepare_first(core, proj, T):
    nc = core.nc
    par, const = core.par, core.const
    groups = ((FQ, 2 * FOX, HEAD), (DQ, 4 * DIFF, DIFF_D), (SQ, DSA + 1, HEAD))
    NS = sum(n for _, n, _ in groups)
    with ExitStack() as st:
        sq = [core.sb(f"prep_sq{n}", [P, TB, h * d], ctx=st) for n, (_, h, d) in enumerate(groups)]
        ss = [core.sb(f"prep_ss{n}", [P, TB, h], ctx=st) for n, (_, h, _) in enumerate(groups)]
        root = [core.sb(f"prep_root{n}", [P, TB, h], ctx=st) for n, (_, h, _) in enumerate(groups)]
        newton = [core.sb(f"prep_newton{n}", [P, TB, h], ctx=st) for n, (_, h, _) in enumerate(groups)]
        rope_a = core.sb("rope_a", [P, TB, 16 * ROPE32 + 12 * ROPE64], ctx=st)
        z = core.sb("forget_z", [P, TB, FOX], ctx=st)
        e = core.sb("forget_e", [P, TB, FOX], ctx=st)
        lf = core.sb("log_forget", [P, TB, FOX], ctx=st)
        cc = core.sb("forget_sums", [P, TB, 2 * FOX], ctx=st)
        ccT = core.sb("forget_sums_t", [2 * FOX, SEQ], ctx=st)
        banks = [core.psum(f"prep_ps{b}", [P, SEQ], st) for b in range(4)]
        c_ps = core.psum("forget_ps", [P, TB * FOX], st)
        ct_ps = core.psum("forget_t_ps", [2 * FOX, SEQ], st)
        squared = core.sem("prep_squared", st)
        meaned = core.sem("prep_meaned", st)
        rooted = core.sem("prep_rooted", st)
        zed = core.sem("forget_zed", st)
        logged = core.sem("forget_logged", st)
        lf_done = core.sem("forget_lf_done", st)
        c_sum = core.sem("forget_c_sum", st)
        cc_done = core.sem("forget_cc_done", st)
        cc_turned = core.sem("forget_cc_turned", st)
        ccT_done = core.sem("forget_ccT_done", st)
        ones_set = core.sem("forget_ones_set", st)
        c_rows = core.sem("forget_c_rows", st)
        ready = core.sem("prep_ready", st)
        chain = core.sem("prep_chain", st)
        turned = core.sem("prep_turned", st)
        out = core.sem("prep_out", st)
        ident = const[:, C_ID:C_ID + P]
        rope = const[:, C_ROPE:C_ROPE + TB * ROPE_COLS].rearrange("p (t c) -> p t c", t=TB)

        units = [(u, IQ + HEAD * (u - U_IQ), HEAD) for u in range(U_IQ, UNITS)]
        units += [(u, FQ + HEAD * (u - U_FQ), HEAD) for u in range(U_FQ, U_DQ)]
        units += [(u, DQ + DIFF_D * (u - U_DQ), DIFF_D) for u in range(U_DQ, U_SQ)]
        units += [(u, SQ + HEAD * (u - U_SQ), HEAD) for u in range(U_SQ, U_IQ)]

        with nc.Block() as block:
            @block.sync
            def _(sp):
                sp.wait_ge(ccT_done, 1)
                sp.wait_ge(ones_set, 1)
                for h in range(FOX):
                    sp.dma_start(T[HEAD:HEAD + 1, U_FQ + h, :], ccT[h:h + 1, :]).then_inc(c_rows, 16)
                    sp.dma_start(T[HEAD + 1:HEAD + 2, U_FK + h, :], ccT[FOX + h:FOX + h + 1, :]).then_inc(c_rows, 16)
                sp.wait_ge(c_rows, 2 * FOX * 16)

            @block.gpsimd
            def _(pool):
                nc.gpsimd.memset(T[HEAD:HEAD + 2, U_FQ:U_DQ, :], 1.0).then_inc(ones_set, 1)

            @block.scalar
            def _(act):
                act.wait_ge(zed, 1)
                nc.scalar.activation(e[:], z[:], ACT.Abs).then_inc(logged, 1)
                act.wait_ge(logged, 1)
                nc.scalar.activation(e[:], e[:], ACT.Exp, scale=-1.0).then_inc(logged, 1)
                act.wait_ge(logged, 2)
                nc.scalar.activation(e[:], e[:], ACT.Ln, bias=1.0).then_inc(logged, 1)
                for n, (c0, h, d) in enumerate(groups):
                    nc.scalar.activation(sq[n][:], proj[:, :, c0:c0 + h * d], ACT.Square).then_inc(squared, 1)
                for n, (u, c0, d) in enumerate(units):
                    if n == UNITS - U_IQ:
                        for m in range(len(groups)):
                            act.wait_ge(meaned, m + 1)
                            nc.scalar.activation(root[m][:], ss[m][:], ACT.Sqrt).then_inc(rooted, 1)
                    act.wait_ge(turned, n + 1)
                    nc.scalar.copy(T[0:d, u, :], banks[n % 4][0:d, :]).then_inc(out, 1)

            @block.vector
            def _(dve):
                link = chained(dve, chain)
                fb = par[:, PAR["fox_fb"]:PAR["fox_fb"] + FOX].unsqueeze(1)
                nc.vector.tensor_tensor(z[:], proj[:, :, FF:FF + FOX], bcast(fb, [P, TB, FOX]), ALU.add).then_inc(zed, 1)
                dve.wait_ge(logged, 3)
                nc.vector.scalar_tensor_tensor(lf[:], z[:], 0.0, e[:], ALU.min, ALU.subtract).then_inc(lf_done, 1)
                dve.wait_ge(c_sum, 1)
                cv = c_ps[:].rearrange("p (t h) -> p t h", t=TB)
                nc.vector.tensor_copy(cc[:, :, 0:FOX], cv).then_inc(cc_done, 1)
                nc.vector.tensor_scalar(cc[:, :, FOX:2 * FOX], cv, -1.0, None, ALU.mult).then_inc(cc_done, 1)

                def rotate(first, heads, d):
                    hw = d // 8
                    o = 0 if d == HEAD else 2 * ROPE64
                    cos = bcast(rope[:, :, o:o + hw].unsqueeze(2), [P, TB, heads, hw])
                    sin = bcast(rope[:, :, o + hw:o + 2 * hw].unsqueeze(2), [P, TB, heads, hw])
                    v = proj[:, :, first:first + heads * d].rearrange("p t (h d) -> p t h d", d=d)
                    x1, x2 = v[:, :, :, 0:hw], v[:, :, :, hw:2 * hw]
                    n = heads * hw
                    t1, t2 = (rope_a[:, :, m * n:(m + 1) * n].rearrange("p t (h d) -> p t h d", d=hw) for m in range(2))
                    link(nc.vector.tensor_tensor(t1, x2, sin, ALU.mult))
                    link(nc.vector.tensor_tensor(t2, x1, sin, ALU.mult))
                    link(nc.vector.tensor_tensor(x1, x1, cos, ALU.mult))
                    link(nc.vector.tensor_tensor(x2, x2, cos, ALU.mult))
                    link(nc.vector.tensor_tensor(x1, x1, t1, ALU.subtract))
                    nc.vector.tensor_tensor(x2, x2, t2, ALU.add).then_inc(ready, 1)

                rotate(IQ, IDX + 1, HEAD)
                dve.wait_ge(cc_turned, 1)
                nc.vector.tensor_copy(ccT[:], ct_ps[:]).then_inc(ccT_done, 1)
                for n, (c0, h, d) in enumerate(groups):
                    dve.wait_ge(squared, n + 1)
                    link(nc.vector.tensor_reduce(ss[n][:], sq[n][:].rearrange("p t (h d) -> p t h d", d=d), AX, ALU.add))
                    nc.vector.tensor_scalar(ss[n][:], ss[n][:], 1.0 / d, NORM_EPS, ALU.mult, ALU.add).then_inc(meaned, 1)
                for n, (c0, h, d) in enumerate(groups):
                    dve.wait_ge(rooted, n + 1)
                    dve.wait_ge(meaned, n + 1)
                    inverse_root(nc, link, ss[n][:], root[n][:], newton[n][:])
                    v = proj[:, :, c0:c0 + h * d].rearrange("p t (h d) -> p t h d", d=d)
                    link(nc.vector.tensor_tensor(v, v, bcast(root[n][:].unsqueeze(3), [P, TB, h, d]), ALU.mult))
                    halves = ((0, DSA, "dsa_qn"), (DSA, 1, "dsa_kn")) if n == 2 else \
                        ((0, h // 2, ("fox_qn", "diff_qn")[n]), (h // 2, h // 2, ("fox_kn", "diff_kn")[n]))
                    for h0, hn, g in halves:
                        w = v[:, :, h0:h0 + hn, :]
                        gain = par[:, PAR[g]:PAR[g] + d].unsqueeze(1).unsqueeze(1)
                        ins = nc.vector.tensor_tensor(w, w, bcast(gain, [P, TB, hn, d]), ALU.mult)
                        if n == 0:
                            ins.then_inc(ready, 1)
                        else:
                            link(ins)
                    if n:
                        rotate(c0, h, d)

            @block.tensor
            def _(pe):
                pe.wait_ge(lf_done, 1)
                for t in range(TB):
                    for b in range(t + 1):
                        m = C_TRI if b == t else C_ONE
                        last = nc.tensor.matmul(c_ps[:, t * FOX:(t + 1) * FOX], const[:, m:m + P], lf[:, b, :],
                                                start=b == 0, stop=b == t)
                last.then_inc(c_sum, 1)
                pe.wait_ge(cc_done, 2)
                for t in range(TB):
                    last = nc.tensor.transpose(ct_ps[:, t * P:(t + 1) * P], cc[:, t, :], ident)
                last.then_inc(cc_turned, 1)
                for n, (u, c0, d) in enumerate(units):
                    need = 1 if u >= U_IQ else 3 if u < U_DQ else 4 if u < U_SQ else 5
                    pe.wait_ge(ready, need)
                    if n >= 4:
                        pe.wait_ge(out, n - 3)
                    for t in range(TB):
                        last = nc.tensor.transpose(banks[n % 4][0:d, t * P:(t + 1) * P], proj[:, t, c0:c0 + d], ident)
                    last.then_inc(turned, 1)


class TopKeys:

    def __init__(self, core, ctx):
        self.core = core
        self.blocks = range(1, TB)
        self.offs = {i: sum((b + 1) * P for b in range(1, i)) for i in self.blocks}
        width = sum((i + 1) * P for i in self.blocks)
        self.work = core.sb("topk_work", [P, width], ctx=ctx)
        self.best = core.sb("topk_best", [P, TB, 8], ctx=ctx)
        self.spare = core.sb("topk_spare", [P, 2], ctx=ctx)
        self.masked = core.sem("topk_masked", ctx)
        self.found = core.sem("topk_found", ctx)
        self.taken = core.sem("topk_taken", ctx)

    def of(self, i):
        return self.work[:, self.offs[i]:self.offs[i] + (i + 1) * P]

    def find(self, dve, r):
        nc, n = self.core.nc, len(self.blocks)
        if not (isinstance(r, int) and r == 0):
            dve.wait_ge(self.taken, n * r)
            nc.vector.memset(self.spare[:, 0:1], 0.0)
        for i in self.blocks:
            nc.vector.max(self.best[:, i, :], self.of(i)).then_inc(self.found, 1)

    def take(self, dve, r):
        nc, n = self.core.nc, len(self.blocks)
        dve.wait_ge(self.found, n * r + n)
        nc.vector.memset(self.spare[:, 1:2], 0.0)
        for i in self.blocks:
            nc.vector.match_replace(self.of(i), self.best[:, i, :], self.of(i), TAKEN).then_inc(self.taken, 1)

    def beside(self, first):
        def work(dve, j, i):
            if i == 0:
                self.find(dve, first + j)
            if i == 2:
                self.take(dve, first + j)
        return work

    def finish(self, dve):
        nc, n = self.core.nc, len(self.blocks)
        dve.wait_ge(self.taken, n * (TOPK // 8))
        for i in self.blocks:
            nc.vector.tensor_scalar(self.of(i), self.of(i), TAKEN_EDGE, NEG, ALU.is_ge, ALU.mult).then_inc(self.masked, 1)

    def scores(self, proj, T, turns):
        core, nc = self.core, self.core.nc
        with ExitStack() as st:
            relu = [core.sb(f"topk_relu{s}", [P, SEQ], ctx=st) for s in range(2)]
            iw = core.sb("topk_iw", [P, TB, IDX], ctx=st)
            banks = [core.psum(f"topk_ps{b}", [P, SEQ], st) for b in range(4)]
            scored = core.sem("topk_scored", st)
            relued = core.sem("topk_relued", st)
            weighed = core.sem("topk_weighed", st)
            w_done = core.sem("topk_w_done", st)
            rows = [(i, h) for i in self.blocks for h in range(IDX)]

            with nc.Block() as block:
                @block.tensor
                def _(pe):
                    for n, (i, h) in enumerate(rows):
                        if n >= 4:
                            pe.wait_ge(relued, n - 3)
                        nc.tensor.matmul(banks[n % 4][:, 0:(i + 1) * P], T[0:HEAD, U_IQ + h, i * P:(i + 1) * P],
                                         T[0:HEAD, U_IK, 0:(i + 1) * P], start=True, stop=True).then_inc(scored, 1)

                @block.scalar
                def _(act):
                    for n, (i, h) in enumerate(rows):
                        act.wait_ge(scored, n + 1)
                        if n >= 2:
                            act.wait_ge(weighed, n - 1)
                        nc.scalar.activation(relu[n % 2][:, 0:(i + 1) * P], banks[n % 4][:, 0:(i + 1) * P], ACT.Relu,
                                             scale=HEAD ** -0.5).then_inc(relued, 1)

                @block.vector
                def _(dve):
                    nc.vector.tensor_scalar(iw[:], proj[:, :, IW:IW + IDX], IDX ** -0.5, None, ALU.mult).then_inc(w_done, 1)
                    dve.wait_ge(w_done, 1)
                    for n, (i, h) in enumerate(rows):
                        dve.wait_ge(relued, n + 1)
                        r_n = relu[n % 2][:, 0:(i + 1) * P]
                        if h:
                            dve.wait_ge(weighed, n)
                            nc.vector.scalar_tensor_tensor(self.of(i), r_n, iw[:, i, h:h + 1], self.of(i),
                                                           ALU.mult, ALU.add).then_inc(weighed, 1)
                        else:
                            nc.vector.tensor_scalar(self.of(i), r_n, iw[:, i, h:h + 1], 0.0,
                                                    ALU.mult, ALU.add).then_inc(weighed, 1)
                    dve.wait_ge(weighed, len(rows))
                    for i in self.blocks:
                        diag = self.of(i)[:, i * P:(i + 1) * P]
                        nc.vector.tensor_tensor(diag, diag, core.const[:, C_ROPE - P:C_ROPE], ALU.add).then_inc(self.masked, 1)
                    dve.wait_ge(self.masked, len(self.blocks))
                    for r in range(turns):
                        self.find(dve, r)
                        self.take(dve, r)


def combine_diff(core, od, o):
    nc = core.nc
    par = core.par
    with ExitStack() as st:
        prod = core.sb("lam_prod", [P, 2, DIFF_D], ctx=st)
        dots = core.sb("lam_dots", [P, 2], ctx=st)
        lam = core.sb("lam", [P, 1], ctx=st)
        gain = core.sb("subln_gain", [P, HEAD], ctx=st)
        sq = core.sb("subln_sq", [P, TB * DIFF, HEAD], ctx=st)
        ss = core.sb("subln_ss", [P, TB * DIFF], ctx=st)
        half = core.sb("subln_half", [P, TB * DIFF], ctx=st)
        chain = core.sem("diff_chain", st)
        dotted = core.sem("diff_dotted", st)
        exped = core.sem("diff_exped", st)
        meaned = core.sem("diff_meaned", st)
        rooted = core.sem("diff_rooted", st)
        mixed = core.sem("diff_mixed", st)
        squared = core.sem("diff_squared", st)
        maps = od[:].rearrange("p t (h m) d -> p (t h) m d", m=2)
        even, odd = maps[:, :, 0, :], maps[:, :, 1, :]
        with nc.Block() as block:
            @block.gpsimd
            def _(pool):
                nc.gpsimd.memset(half[:], -0.5).then_inc(rooted, 1)
                pool.wait_ge(meaned, 1)
                pool.wait_ge(rooted, 1)
                nc.gpsimd.tensor_tensor(ss[:], ss[:], half[:], ALU.pow).then_inc(rooted, 1)

            @block.scalar
            def _(act):
                act.wait_ge(dotted, 1)
                nc.scalar.activation(dots[:], dots[:], ACT.Exp).then_inc(exped, 1)
                act.wait_ge(mixed, 1)
                nc.scalar.activation(sq[:], even, ACT.Square).then_inc(squared, 1)

            @block.vector
            def _(dve):
                link = chained(dve, chain)
                for n in range(2):
                    a, b = PAR[f"diff_lq{n + 1}"], PAR[f"diff_lk{n + 1}"]
                    link(nc.vector.tensor_tensor(prod[:, n, :], par[:, a:a + DIFF_D], par[:, b:b + DIFF_D], ALU.mult))
                nc.vector.tensor_reduce(dots[:], prod[:], AX, ALU.add).then_inc(dotted, 1)
                dve.wait_ge(exped, 1)
                link(nc.vector.tensor_tensor(lam[:], dots[:, 1:2], dots[:, 0:1], ALU.subtract))
                link(nc.vector.tensor_tensor(lam[:], lam[:], core.lam_init[:, 0:1], ALU.subtract))
                s0 = PAR["diff_subln"]
                link(nc.vector.tensor_scalar(gain[:], par[:, s0:s0 + HEAD], core.lam_init[:, 1:2], None, ALU.mult))
                nc.vector.scalar_tensor_tensor(even, odd, lam[:], even, ALU.mult, ALU.add).then_inc(mixed, 1)
                dve.wait_ge(squared, 1)
                link(nc.vector.tensor_reduce(ss[:], sq[:], AX, ALU.add))
                nc.vector.tensor_scalar(ss[:], ss[:], 1.0 / HEAD, NORM_EPS, ALU.mult, ALU.add).then_inc(meaned, 1)
                dve.wait_ge(rooted, 2)
                link(nc.vector.tensor_tensor(even, even, bcast(ss[:].unsqueeze(2), [P, TB * DIFF, HEAD]), ALU.mult))
                dst = o[:, :, FOX * HEAD:(FOX + DIFF) * HEAD].rearrange("p t (h d) -> p t h d", d=HEAD)
                src = od[:].rearrange("p t (h m) d -> p t h m d", m=2)[:, :, :, 0, :]
                link(nc.vector.tensor_tensor(dst, src, bcast(gain[:].unsqueeze(1).unsqueeze(1), [P, TB, DIFF, HEAD]), ALU.mult))


def first_block(core, w, layer):
    nc = core.nc
    with ExitStack() as lay:
        core.par = core.sb("par", [P, PAR_COLS], ctx=lay)
        core.lam_init = core.sb("lam_init", [P, 2], ctx=lay)
        gain = core.sb("norm_gain", [P, KD], ctx=lay)
        par_in = core.sem("par_in", lay)

        def load_first(sp, weights):
            sp.dma_start(core.par[:], w["params"][layer].partition_broadcast(P)).then_inc(par_in, 16)
            sp.dma_start(core.lam_init[:], w["lam"][layer].partition_broadcast(P)).then_inc(par_in, 16)
            weights.ahead(sp)
            sp.wait_ge(par_in, 32)

        with ExitStack() as mix:
            o = core.sb("mix_out", [P, TB, D], ctx=mix)
            with ExitStack() as a:
                proj = core.sb("proj", [P, TB, IN_CHUNKS * IN_COLS], ctx=a)
                with ExitStack() as b:
                    hi = core.sb("h_hi", [P, KD, SEQ], F32R, ctx=b)
                    lo = core.sb("h_lo", [P, KD, SEQ], F32R, ctx=b)
                    w_in = Weights(core, "in", lambda c: w["w_in"][layer, c], IN_CHUNKS, IN_COLS, b)
                    transpose_split(core, "n1", core.x, hi, lo, KD, gain, w["attn_norm"][layer], norm=True,
                                    ahead=lambda sp: load_first(sp, w_in))
                    project(core, "in", hi, lo, w_in,
                            by_token=lambda c, t, sums: nc.vector.tensor_copy(proj[:, t, bass.ds(c * IN_COLS, IN_COLS)], sums))
                T = core.sb("qk_t", [HEAD + 2, UNITS, SEQ], ctx=a)
                top = TopKeys(core, a)
                prepare_first(core, proj, T)
                top.scores(proj, T, TOPK // 8 - FOX - 2 * DIFF)

                def causal(i, slot):
                    return core.const[:, C_ROPE - (i + 1) * P:C_ROPE]

                od = core.sb("diff_out", [P, TB, 2 * DIFF, HEAD], ctx=a)
                attention(core, "fox", FOX, HEAD + 2, lambda j: T[:, U_FQ + j, :], lambda j, n: T[:, U_FK + j, 0:n],
                          lambda j, b: proj[:, b, bass.ds(j * HEAD + FV, HEAD)], core.const[0:HEAD + 2, C_FOX:C_FOX + 1],
                          causal, lambda j, i: o[:, i, bass.ds(j * HEAD, HEAD)],
                          beside=top.beside(TOPK // 8 - FOX - 2 * DIFF))
                attention(core, "dif", 2 * DIFF, DIFF_D, lambda j: T[0:DIFF_D, U_DQ + j, :],
                          lambda j, n: T[0:DIFF_D, U_DK + j, 0:n],
                          lambda j, b: proj[:, b, bass.ds((j // 2) * HEAD + DV, HEAD)], DIFF_D ** -0.5,
                          causal, lambda j, i: od[:, i, j, :], beside=top.beside(TOPK // 8 - 2 * DIFF), after=top.finish)
                attention(core, "dsa", DSA, HEAD, lambda j: T[0:HEAD, U_SQ + j, :], lambda j, n: T[0:HEAD, U_SK, 0:n],
                          lambda j, b: proj[:, b, SV:SV + HEAD], HEAD ** -0.5,
                          lambda i, s: top.of(i) if i else causal(i, s),
                          lambda j, i: o[:, i, bass.ds(j * HEAD + (FOX + DIFF) * HEAD, HEAD)])
                combine_diff(core, od, o)
            hi = core.sb("o_hi", [P, KD, SEQ], F32R, ctx=mix)
            lo = core.sb("o_lo", [P, KD, SEQ], F32R, ctx=mix)
            w_out = Weights(core, "out", lambda c: w["w_out"][layer, c], OUT_CHUNKS, OUT_COLS, mix)
            transpose_split(core, "ot", o, hi, lo, KD, ahead=w_out.ahead)
            project(core, "out", hi, lo, w_out,
                    by_token=lambda c, t, sums: add_to_x(core, c, t, sums, OUT_COLS))
        with ExitStack() as b:
            hi = core.sb("f_hi", [P, KD, SEQ], F32R, ctx=b)
            lo = core.sb("f_lo", [P, KD, SEQ], F32R, ctx=b)
            w_ffn = GroupWeights(core, "ffn", lambda g: w["w_gate"][layer, g], lambda g: w["w_up"][layer, g],
                                 lambda g: w["w_down"][layer, g], b)
            transpose_split(core, "n2", core.x, hi, lo, KD, gain, w["ffn_norm"][layer], norm=True, ahead=w_ffn.ahead)
            feed_forward(core, "ffn", hi, lo, FFN_GROUPS, w_ffn)
        core.clear()


Q_GAIN, K_GAIN, G_BIAS, PAR2_COLS = 0, HEAD, 2 * HEAD, 2 * HEAD + ROUTES
F_GATE, F_GLU, F_D, FEATURE_COLS = 0, 2 * D // P, 2 * D // P + SQT, 2 * D // P + 2 * SQT


def prepare_second(core, qkv, T):
    nc = core.nc
    N = 2 * HEADS2
    with ExitStack() as st:
        sq = [core.sb(f"sq2_{n}", [P, TB, ATTN2], ctx=st) for n in range(2)]
        ss = [core.sb(f"ss2_{n}", [P, TB, HEADS2], ctx=st) for n in range(2)]
        root = [core.sb(f"root2_{n}", [P, TB, HEADS2], ctx=st) for n in range(2)]
        newton = [core.sb(f"newton2_{n}", [P, TB, HEADS2], ctx=st) for n in range(2)]
        banks = [core.psum(f"prep2_ps{b}", [P, SEQ], st) for b in range(4)]
        squared = core.sem("prep2_squared", st)
        meaned = core.sem("prep2_meaned", st)
        rooted = core.sem("prep2_rooted", st)
        ready = core.sem("prep2_ready", st)
        chain = core.sem("prep2_chain", st)
        turned = core.sem("prep2_turned", st)
        out = core.sem("prep2_out", st)
        ident = core.const[:, C_ID:C_ID + P]
        with nc.Block() as block:
            @block.scalar
            def _(act):
                for n in range(2):
                    nc.scalar.activation(sq[n][:], qkv[:, :, n * ATTN2:(n + 1) * ATTN2], ACT.Square).then_inc(squared, 1)
                for n in range(2):
                    act.wait_ge(meaned, n + 1)
                    nc.scalar.activation(root[n][:], ss[n][:], ACT.Sqrt).then_inc(rooted, 1)
                for u in range(N):
                    act.wait_ge(turned, u + 1)
                    nc.scalar.copy(T[:, u, :], banks[u % 4][0:HEAD, :]).then_inc(out, 1)

            @block.vector
            def _(dve):
                link = chained(dve, chain)
                for n in range(2):
                    dve.wait_ge(squared, n + 1)
                    link(nc.vector.tensor_reduce(ss[n][:], sq[n][:].rearrange("p t (h d) -> p t h d", d=HEAD), AX, ALU.add))
                    nc.vector.tensor_scalar(ss[n][:], ss[n][:], 1.0 / HEAD, NORM_EPS, ALU.mult, ALU.add).then_inc(meaned, 1)
                for n, g in enumerate((Q_GAIN, K_GAIN)):
                    dve.wait_ge(rooted, n + 1)
                    dve.wait_ge(meaned, n + 1)
                    inverse_root(nc, link, ss[n][:], root[n][:], newton[n][:])
                    v = qkv[:, :, n * ATTN2:(n + 1) * ATTN2].rearrange("p t (h d) -> p t h d", d=HEAD)
                    link(nc.vector.tensor_tensor(v, v, bcast(root[n][:].unsqueeze(3), [P, TB, HEADS2, HEAD]), ALU.mult))
                    gain = core.par2[:, g:g + HEAD].unsqueeze(1).unsqueeze(1)
                    nc.vector.tensor_tensor(v, v, bcast(gain, [P, TB, HEADS2, HEAD]), ALU.mult).then_inc(ready, 1)

            @block.tensor
            def _(pe):
                for u in range(N):
                    pe.wait_ge(ready, 1 + u // HEADS2)
                    if u >= 4:
                        pe.wait_ge(out, u - 3)
                    for t in range(TB):
                        last = nc.tensor.transpose(banks[u % 4][0:HEAD, t * P:(t + 1) * P],
                                                   qkv[:, t, u * HEAD:(u + 1) * HEAD], ident)
                    last.then_inc(turned, 1)


TWO_PI = 2 * math.pi
TWO_PI_HI = 6.28125
TWO_PI_LO = TWO_PI - TWO_PI_HI
ROUND = 1.5 * 2 ** 23
PI_EDGE = 3.1415925
LONG = 64
LEVELS = [n for n in (1 << b for b in range(SEQ.bit_length())) if LONG <= n < SEQ]


def discretise(core, w, mag, cos_t, sin_t, b_t, c_t):
    nc = core.nc
    with ExitStack() as st:
        lam = core.sb("lambda", [P, 2 * ST], ctx=st)
        step = core.sb("step", [P, ST], ctx=st)
        small = core.sb("ssm_small", [P, 12, ST], ctx=st)
        long_cs = [core.sb(f"long_cos{n}", [P, ST], ctx=st) for n in LEVELS]
        long_sn = [core.sb(f"long_sin{n}", [P, ST], ctx=st) for n in LEVELS]
        raw_b = core.sb("raw_b", [P, 2, ST, 2 * GROUP], ctx=st)
        bb = core.sb("scaled_b", [P, 2, ST, 2 * GROUP], ctx=st)
        tmp = core.sb("b_tmp", [P, ST, LONG // 2], ctx=st)
        tmp2 = core.sb("b_tmp2", [P, ST, LONG // 2], ctx=st)
        cross = [core.sb(f"phase_cross{s}", [P, PER, 2, SEQ // 2], ctx=st) for s in range(2)]
        banks = [core.psum(f"b_ps{b}", [P, P], st) for b in range(2 * SQT)]
        rates_in = core.sem("ssm_rates_in", st)
        mats_in = core.sem("ssm_mats_in", st)
        mults = core.sem("ssm_step_mult", st)
        exped = core.sem("ssm_exped", st)
        sined = core.sem("ssm_sined", st)
        halved = core.sem("ssm_angle", st)
        chain = core.sem("ssm_chain", st)
        scaled = core.sem("ssm_scaled", st)
        turned = core.sem("ssm_turned", st)
        out = core.sem("ssm_b_out", st)
        angled = core.sem("ssm_angled", st)
        crossed = core.sem("ssm_crossed", st)
        phased = core.sem("ssm_phased", st)
        lre, lim = lam[:, 0:ST], lam[:, ST:2 * ST]
        ang, rnd, sn, cs, hs, a_re, a_im, den, f_re, f_im, t0, t1 = (small[:, n, :] for n in range(12))
        with nc.Block() as block:
            @block.sync
            def _(sp):
                sp.dma_start(lam[:], w["lambda2"]).then_inc(rates_in, 16)
                for n in range(2):
                    sp.dma_start(step[n * STATE:(n + 1) * STATE, :],
                                 w["log_step2"][n].partition_broadcast(STATE)).then_inc(rates_in, 16)
                sp.dma_start(raw_b[:].rearrange("p m t c -> p (m t c)"), w["b_diag2"]).then_inc(mats_in, 16)
                sp.dma_start(c_t[:].rearrange("p m t c -> p (m t c)"), w["c_diag2"]).then_inc(mats_in, 16)

            @block.scalar
            def _(act):
                act.wait_ge(rates_in, 3 * 16)
                nc.scalar.activation(step[:], step[:], ACT.Exp).then_inc(exped, 1)
                act.wait_ge(mults, 1)
                nc.scalar.activation(mag[:], mag[:], ACT.Exp).then_inc(exped, 1)
                act.wait_ge(halved, 1)
                nc.scalar.activation(sn, ang, ACT.Sin).then_inc(sined, 1)
                nc.scalar.activation(hs, ang, ACT.Sin, scale=0.5).then_inc(sined, 1)
                for level, n in enumerate(LEVELS):
                    act.wait_ge(angled, level + 1)

                    def long_step(q, s, first):
                        if not first or level:
                            act.wait_ge(phased, SQT * level + q - 1)
                        for j in range(PER):
                            i = PER * q + j
                            sin_n = long_sn[level][:, bass.ds(i, 1)]
                            nc.scalar.activation(cross[s][:, j, 0, 0:n], cos_t[:, i, 0:n], ACT.Copy, scale=sin_n)
                            last = nc.scalar.activation(cross[s][:, j, 1, 0:n], sin_t[:, i, 0:n], ACT.Copy, scale=sin_n)
                        last.then_inc(crossed, 1)
                    pairs(act, SQT, long_step)
                for n in range(2 * SQT):
                    act.wait_ge(turned, n + 1)
                    nc.scalar.copy(b_t[:, n // SQT, n % SQT, :], banks[n][:]).then_inc(out, 1)

            @block.vector
            def _(dve):
                link = chained(dve, chain)

                def tt(o, a, b, op):
                    link(nc.vector.tensor_tensor(o, a, b, op))

                def ts(o, a, m, b, op0=ALU.mult, op1=ALU.add):
                    link(nc.vector.tensor_scalar(o, a, m, b, op0, op1))

                dve.wait_ge(rates_in, 3 * 16)
                dve.wait_ge(exped, 1)
                nc.vector.tensor_tensor(mag[:], lre, step[:], ALU.mult).then_inc(mults, 1)
                tt(ang, lim, step[:], ALU.mult)
                ts(rnd, ang, 1.0 / TWO_PI, ROUND)
                ts(rnd, rnd, ROUND, None, ALU.subtract, ALU.bypass)
                link(nc.vector.scalar_tensor_tensor(ang, rnd, -TWO_PI_HI, ang, ALU.mult, ALU.add))
                link(nc.vector.scalar_tensor_tensor(ang, rnd, -TWO_PI_LO, ang, ALU.mult, ALU.add))
                nc.vector.tensor_scalar(ang, ang, PI_EDGE, -PI_EDGE, ALU.min, ALU.max).then_inc(halved, 1)
                dve.wait_ge(exped, 2)
                dve.wait_ge(sined, 2)
                tt(cs, hs, hs, ALU.mult)
                ts(cs, cs, -2.0, 1.0)
                tt(a_re, mag[:], cs, ALU.mult)
                tt(a_im, mag[:], sn, ALU.mult)
                ts(a_re, a_re, -1.0, None, ALU.add, ALU.bypass)
                def double_angle(c, s, level=None):
                    c2, s2 = (cs, sn) if level is None else (long_cs[level][:], long_sn[level][:])
                    tt(t0, c, c, ALU.mult)
                    tt(t1, s, s, ALU.mult)
                    tt(s2, s, c, ALU.mult)
                    ts(s2, s2, 2.0, 0.0)
                    if level is None:
                        tt(c2, t0, t1, ALU.subtract)
                    else:
                        nc.vector.tensor_tensor(c2, t0, t1, ALU.subtract).then_inc(angled, 1)
                        dve.wait_ge(angled, level + 1)

                link(nc.vector.memset(cos_t[:, :, 0:1], 1.0))
                link(nc.vector.memset(sin_t[:, :, 0:1], 0.0))
                n = 1
                while n < LONG:
                    shape = [P, ST, n]
                    c_n, s_n = bcast(cs.unsqueeze(2), shape), bcast(sn.unsqueeze(2), shape)
                    c_k, s_k = cos_t[:, :, 0:n], sin_t[:, :, 0:n]
                    p, q = tmp[:, :, 0:n], tmp2[:, :, 0:n]
                    tt(p, c_k, c_n, ALU.mult)
                    tt(q, s_k, s_n, ALU.mult)
                    tt(cos_t[:, :, n:2 * n], p, q, ALU.subtract)
                    tt(p, s_k, c_n, ALU.mult)
                    tt(q, c_k, s_n, ALU.mult)
                    tt(sin_t[:, :, n:2 * n], p, q, ALU.add)
                    n *= 2
                    if n < LONG:
                        double_angle(cs, sn)
                double_angle(cs, sn, 0)
                for level in range(1, len(LEVELS)):
                    double_angle(long_cs[level - 1][:], long_sn[level - 1][:], level)
                tt(den, lre, lre, ALU.mult)
                tt(t0, lim, lim, ALU.mult)
                tt(den, den, t0, ALU.add)
                link(nc.vector.reciprocal(den, den))
                tt(t0, a_re, lre, ALU.mult)
                tt(t1, a_im, lim, ALU.mult)
                tt(t0, t0, t1, ALU.add)
                tt(f_re, t0, den, ALU.mult)
                tt(t0, a_im, lre, ALU.mult)
                tt(t1, a_re, lim, ALU.mult)
                tt(t0, t0, t1, ALU.subtract)
                tt(f_im, t0, den, ALU.mult)
                dve.wait_ge(mats_in, 2 * 16)
                ts(c_t[:, 1], c_t[:, 1], -1.0, 0.0)
                shape = [P, ST, 2 * GROUP]
                fr, fi = bcast(f_re.unsqueeze(2), shape), bcast(f_im.unsqueeze(2), shape)
                part = tmp[:, :, 0:2 * GROUP]
                tt(bb[:, 0], raw_b[:, 0], fr, ALU.mult)
                tt(part, raw_b[:, 1], fi, ALU.mult)
                nc.vector.tensor_tensor(bb[:, 0], bb[:, 0], part, ALU.subtract).then_inc(scaled, 1)
                tt(bb[:, 1], raw_b[:, 1], fr, ALU.mult)
                dve.wait_ge(scaled, 1)
                tt(part, raw_b[:, 0], fi, ALU.mult)
                nc.vector.tensor_tensor(bb[:, 1], bb[:, 1], part, ALU.add).then_inc(scaled, 1)
                dve.wait_ge(scaled, 2)
                for level, n in enumerate(LEVELS):
                    def long_step(q, s, first):
                        dve.wait_ge(crossed, SQT * level + q + 1)
                        for j in range(PER):
                            i = PER * q + j
                            cos_n = long_cs[level][:, bass.ds(i, 1)]
                            nc.vector.scalar_tensor_tensor(cos_t[:, i, n:2 * n], cos_t[:, i, 0:n], cos_n, cross[s][:, j, 1, 0:n],
                                                           ALU.mult, ALU.subtract)
                            last = nc.vector.scalar_tensor_tensor(sin_t[:, i, n:2 * n], sin_t[:, i, 0:n], cos_n,
                                                                  cross[s][:, j, 0, 0:n], ALU.mult, ALU.add)
                        last.then_inc(phased, 1)
                    pairs(dve, SQT, long_step)

            @block.tensor
            def _(pe):
                for m in range(2):
                    pe.wait_ge(scaled, m + 1)
                    for q in range(SQT):
                        v = bb[:, m, q * PER:(q + 1) * PER, :].rearrange("p t c -> p (t c)")
                        nc.tensor.transpose(banks[m * SQT + q][:], v, core.const[:, C_ID:C_ID + P]).then_inc(turned, 1)


def state_space(core, u_t, mag, cos_t, sin_t, b_t, c_t, z):
    nc = core.nc
    with ExitStack() as st:
        b_s = [core.sb(f"b_slot{p}", [P, 2, P], ctx=st) for p in range(2)]
        c_s = [core.sb(f"c_slot{p}", [P, 3, PER, 2 * GROUP], ctx=st) for p in range(2)]
        u_s = [core.sb(f"u_slot{p}", [P, SEQ], ctx=st) for p in range(2)]
        y_ps = [core.psum(f"y_ps{p}", [P, SEQ], st) for p in range(2)]
        prods = [core.sb(f"turn_in{s}", [P, 4, SEQ], ctx=st) for s in range(2)]
        scanned = [core.sb(f"scanned{s}", [P, 2, SEQ], ctx=st) for s in range(2)]
        back = [core.sb(f"turn_back{s}", [P, 4, SEQ], ctx=st) for s in range(2)]
        in_ps = [[core.psum(f"bu_ps{s}{m}", [P, SEQ], st) for m in range(2)] for s in range(2)]
        slots = core.sem("ssm_slots", st)
        bu = core.sem("ssm_bu", st)
        mixed = core.sem("ssm_mixed", st)
        summed = core.sem("ssm_summed", st)
        scan = core.sem("ssm_scan", st)
        turned = core.sem("ssm_turned_back", st)
        read = core.sem("ssm_read", st)
        y_done = core.sem("ssm_y_done", st)

        def zero(q):
            return isinstance(q, int) and q == 0

        def reused(q, j):
            return not zero(q) or j >= 2

        with nc.Block() as block:
            @block.scalar
            def _(act):
                def load(q, p, first):
                    if not first:
                        act.wait_ge(bu, PER * (q - 1))
                        act.wait_ge(y_done, q - 1)
                        act.wait_ge(read, PER * (q - 1))
                    nc.scalar.copy(b_s[p][:], b_t[:, :, q, :]).then_inc(slots, 1)
                    nc.scalar.copy(u_s[p][:], u_t[:, q, :]).then_inc(slots, 1)
                    nc.scalar.copy(c_s[p][:, 0:2], c_t[:, :, bass.ds(q * PER, PER), :]).then_inc(slots, 1)
                    nc.scalar.activation(c_s[p][:, 2], c_t[:, 0, bass.ds(q * PER, PER), :], ACT.Copy, scale=-1.0).then_inc(slots, 1)

                load(0, 0, True)

                def step(q, p, first):
                    if not (isinstance(q, int) and q == SQT - 1):
                        load(q + 1, 1 - p, zero(q))
                    act.wait_ge(y_done, q + 1)
                    nc.scalar.activation(z[:, q, :], z[:, q, :], ACT.Gelu_apprx_tanh)
                pairs(act, SQT, step, peel_last=True)

            @block.tensor
            def _(pe):
                def inputs(q, p, j):
                    i, s = PER * q + j, j % 2
                    if reused(q, j):
                        pe.wait_ge(mixed, i - 1)
                    rows = slice(2 * GROUP * j, 2 * GROUP * (j + 1))
                    for m in range(2):
                        last = nc.tensor.matmul(in_ps[s][m][:], b_s[p][rows, m, :], u_s[p][rows, :], start=True, stop=True)
                    last.then_inc(bu, 1)

                def outputs(q, p, j, first):
                    pe.wait_ge(turned, PER * q + j + 1)
                    if j == 0 and not first:
                        pe.wait_ge(y_done, q - 1)
                    rows = slice(2 * GROUP * j, 2 * GROUP * (j + 1))
                    for n, plane in enumerate((0, 2, 1, 1)):
                        last = nc.tensor.matmul(y_ps[p][rows, :], c_s[p][:, plane, j, :], back[j % 2][:, n, :], start=n == 0, stop=n == 3)
                    last.then_inc(read, 1)

                def step(q, p, first):
                    pe.wait_ge(slots, 4 * q + 4)
                    for j in range(PER):
                        inputs(q, p, j)
                        if j >= 2:
                            outputs(q, p, j - 2, first)
                        elif not zero(q):
                            outputs(q - 1, 1 - p, PER - 2 + j, True)
                pairs(pe, SQT, step)
                for j in (PER - 2, PER - 1):
                    outputs(SQT - 1, (SQT - 1) % 2, j, True)

            @block.vector
            def _(dve):
                def mix(q, j):
                    i, s = PER * q + j, j % 2
                    dve.wait_ge(bu, i + 1)
                    if reused(q, j):
                        dve.wait_ge(scan, i - 1)
                    c, sn = cos_t[:, i, :], sin_t[:, i, :]
                    re, im = in_ps[s][0][:], in_ps[s][1][:]
                    nc.vector.tensor_tensor(prods[s][:, 0, :], re, c, ALU.mult)
                    nc.vector.tensor_tensor(prods[s][:, 1, :], im, sn, ALU.mult)
                    nc.vector.tensor_tensor(prods[s][:, 2, :], im, c, ALU.mult)
                    nc.vector.tensor_tensor(prods[s][:, 3, :], re, sn, ALU.mult).then_inc(mixed, 1)

                def add(q, j):
                    s = j % 2
                    dve.wait_ge(mixed, PER * q + j + 1)
                    nc.vector.tensor_tensor(prods[s][:, 0, :], prods[s][:, 0, :], prods[s][:, 1, :], ALU.add)
                    nc.vector.tensor_tensor(prods[s][:, 2, :], prods[s][:, 2, :], prods[s][:, 3, :], ALU.subtract).then_inc(summed, 1)

                def recur(q, j):
                    i, s = PER * q + j, j % 2
                    dve.wait_ge(summed, i + 1)
                    if reused(q, j):
                        dve.wait_ge(turned, i - 1)
                    factor = bcast(mag[:, bass.ds(i, 1)], [P, SEQ])
                    for m in range(2):
                        last = nc.vector.tensor_tensor_scan(scanned[s][:, m, :], factor, prods[s][:, 2 * m, :], 0.0, ALU.mult, ALU.add)
                    last.then_inc(scan, 1)

                def turn_back(q, j, part):
                    i, s = PER * q + j, j % 2
                    if part == 0:
                        dve.wait_ge(scan, i + 1)
                        if reused(q, j):
                            dve.wait_ge(read, i - 1)
                    phase = (cos_t, sin_t)[part][:, i, :]
                    nc.vector.tensor_tensor(back[s][:, 3 * part, :], scanned[s][:, 0, :], phase, ALU.mult)
                    last = nc.vector.tensor_tensor(back[s][:, 2 - part, :], scanned[s][:, 1, :], phase, ALU.mult)
                    if part:
                        last.then_inc(turned, 1)

                def make_y(q, p):
                    dve.wait_ge(read, PER * q + PER)
                    nc.vector.scalar_tensor_tensor(z[:, q, :], u_s[p][:], core.feature2[:, bass.ds(q + F_D, 1)], y_ps[p][:],
                                                   ALU.mult, ALU.add).then_inc(y_done, 1)

                def step(q, p, first):
                    for j in range(PER):
                        before = (q, j - 1) if j else (q - 1, PER - 1)
                        mix(q, j)
                        if j or not zero(q):
                            turn_back(*before, 0)
                        add(q, j)
                        if j or not zero(q):
                            turn_back(*before, 1)
                        recur(q, j)
                        if j == 2 and not zero(q):
                            make_y(q - 1, 1 - p)
                pairs(dve, SQT, step)
                turn_back(SQT - 1, PER - 1, 0)
                turn_back(SQT - 1, PER - 1, 1)
                make_y(SQT - 1, (SQT - 1) % 2)


def route_logits(core, w, hi, lo, logit):
    nc = core.nc
    with ExitStack() as st:
        raw = core.sb("route_raw", [P, KD, ROUTES], ctx=st)
        whi = core.sb("route_hi", [P, KD, ROUTES], F32R, ctx=st)
        wlo = core.sb("route_lo", [P, KD, ROUTES], F32R, ctx=st)
        logit_t = core.sb("route_logit_t", [ROUTES, SEQ], ctx=st)
        t_ps = core.psum("route_t_ps", [ROUTES, SEQ], st)
        ps = core.psum("route_ps", [P, TB * ROUTES], st)
        w_in = core.sem("route_w_in", st)
        hi_done = core.sem("route_hi_done", st)
        lo_done = core.sem("route_lo_done", st)
        summed = core.sem("route_summed", st)
        copied = core.sem("route_copied", st)
        turned = core.sem("route_turned", st)
        with nc.Block() as block:
            @block.sync
            def _(sp):
                sp.dma_start(raw[:].rearrange("p k n -> p (k n)"), w["w_route2"]).then_inc(w_in, 16)

            @block.tensor
            def _(pe):
                pe.wait_ge(lo_done, 1)
                n = 0
                for k in range(KD):
                    for aw, ww in ((hi, whi), (lo, whi), (hi, wlo)):
                        last = nc.tensor.matmul(t_ps[:], ww[:, k, :], aw[:, k, :], start=n == 0, stop=n == 3 * KD - 1)
                        n += 1
                last.then_inc(summed, 1)
                pe.wait_ge(copied, 1)
                for t in range(TB):
                    last = nc.tensor.transpose(ps[:, t * ROUTES:(t + 1) * ROUTES], logit_t[:, t * P:(t + 1) * P],
                                               core.const[0:ROUTES, C_ID:C_ID + ROUTES])
                last.then_inc(turned, 1)

            @block.scalar
            def _(act):
                act.wait_ge(w_in, 16)
                nc.scalar.copy(whi[:], raw[:]).then_inc(hi_done, 1)
                act.wait_ge(summed, 1)
                nc.scalar.copy(logit_t[:], t_ps[:]).then_inc(copied, 1)

            @block.vector
            def _(dve):
                dve.wait_ge(hi_done, 1)
                nc.vector.tensor_tensor(wlo[:], raw[:], whi[:].bitcast(F32), ALU.subtract).then_inc(lo_done, 1)
                dve.wait_ge(turned, 1)
                bias = bcast(core.par2[:, G_BIAS:G_BIAS + ROUTES].unsqueeze(1), [P, TB, ROUTES])
                nc.vector.tensor_tensor(logit[:], ps[:].rearrange("p (t r) -> p t r", t=TB), bias, ALU.add)


class Route:

    def __init__(self, core, logit, gates, ctx):
        self.core, self.logit, self.gates = core, logit, gates
        self.four = core.sb("route_four", [P, 9, TB, MOE_G], ctx=ctx)
        self.one = core.sb("route_one", [P, 7, TB], ctx=ctx)
        self.grid = core.sb("route_grid", [P, TB, MOE_G, MOE_E], ctx=ctx)
        self.shifted = core.sem("route_shifted", ctx)
        self.exped = core.sem("route_exped", ctx)
        self.chain = core.sem("route_chain", ctx)

    def on_scalar(self, act):
        nc, g_exp, prob = self.core.nc, self.four[:, 0], self.four[:, 4]
        act.wait_ge(self.shifted, 1)
        nc.scalar.activation(g_exp, g_exp, ACT.Exp).then_inc(self.exped, 1)
        act.wait_ge(self.shifted, 2)
        nc.scalar.activation(prob, prob, ACT.Exp).then_inc(self.exped, 1)

    def on_vector(self, dve):
        core, nc, grid, logit, gates = self.core, self.core.nc, self.grid, self.logit, self.gates
        shifted, exped = self.shifted, self.exped
        g_exp, one_g, pos, e_sel, prob, one_1, one_2, left, pair = (self.four[:, n] for n in range(9))
        g_max, g_prob, best, e_max, e_sum, p1, p2 = (self.one[:, n] for n in range(7))
        link = chained(dve, self.chain)

        def tt(o, a, b, op):
            link(nc.vector.tensor_tensor(o, a, b, op))

        def wide(v):
            return bcast(v.unsqueeze(2), [P, TB, MOE_G])

        rank = bcast(core.const[:, C_RANK:C_RANK + 4].unsqueeze(1), [P, TB, 4])

        def first_best(o, v, top):
            link(nc.vector.tensor_reduce(top, v, AX, ALU.max))
            tt(pos, v, wide(top), ALU.is_equal)
            tt(pos, pos, rank, ALU.mult)
            link(nc.vector.tensor_reduce(best, pos, AX, ALU.max))
            tt(o, pos, wide(best), ALU.is_equal)

        g_logit = logit[:, :, 0:MOE_G]
        first_best(one_g, g_logit, g_max)
        nc.vector.tensor_tensor(g_exp, g_logit, wide(g_max), ALU.subtract).then_inc(shifted, 1)
        e_logit = logit[:, :, MOE_G:ROUTES].rearrange("p t (g e) -> p t g e", g=MOE_G)
        chosen = bcast(one_g.unsqueeze(3), [P, TB, MOE_G, MOE_E])
        tt(grid[:], e_logit, chosen, ALU.mult)
        link(nc.vector.tensor_reduce(e_sel, grid[:].rearrange("p t g e -> p t e g"), AX, ALU.add))
        link(nc.vector.tensor_reduce(e_max, e_sel, AX, ALU.max))
        nc.vector.tensor_tensor(prob, e_sel, wide(e_max), ALU.subtract).then_inc(shifted, 1)
        dve.wait_ge(exped, 2)
        link(nc.vector.tensor_reduce(g_prob, g_exp, AX, ALU.add))
        link(nc.vector.reciprocal(g_prob, g_prob))
        link(nc.vector.tensor_reduce(e_sum, prob, AX, ALU.add))
        link(nc.vector.reciprocal(e_sum, e_sum))
        tt(prob, prob, wide(e_sum), ALU.mult)
        first_best(one_1, prob, p1)
        link(nc.vector.scalar_tensor_tensor(left, one_1, -2.0, prob, ALU.mult, ALU.add))
        first_best(one_2, left, p2)
        tt(pair, one_1, one_2, ALU.add)
        tt(pair, pair, prob, ALU.mult)
        tt(p1, p1, p2, ALU.add)
        link(nc.vector.reciprocal(p1, p1))
        tt(pair, pair, wide(p1), ALU.mult)
        tt(pair, pair, wide(g_prob), ALU.mult)
        out = gates[:].rearrange("p t (g e) -> p t g e", g=MOE_G)
        tt(out, chosen, bcast(pair.unsqueeze(2), [P, TB, MOE_G, MOE_E]), ALU.mult)


def second_block(core, w):
    nc = core.nc
    x = core.x
    with ExitStack() as blk:
        core.par2 = core.sb("par2", [P, PAR2_COLS], ctx=blk)
        core.feature2 = core.sb("feature2", [P, FEATURE_COLS], ctx=blk)
        gain = core.sb("norm_gain2", [P, KD], ctx=blk)
        par_in = core.sem("par2_in", blk)

        def load_first(sp, weights):
            sp.dma_start(core.par2[:], w["params2"].partition_broadcast(P)).then_inc(par_in, 16)
            sp.dma_start(core.feature2[:], w["feature2"]).then_inc(par_in, 16)
            weights.ahead(sp)
            sp.wait_ge(par_in, 32)

        with ExitStack() as mix:
            gate_t = core.sb("gate_t", [P, 2 * KD, SEQ], ctx=mix)
            a_hi = core.sb("a_hi", [P, SQT, SEQ], F32R, ctx=mix)
            a_lo = core.sb("a_lo", [P, SQT, SEQ], F32R, ctx=mix)
            u_t = core.sb("u_t", [P, SQT, SEQ], ctx=mix)
            FT = FEAT_COLS // P
            with ExitStack() as at:
                qkv = core.sb("qkv", [P, TB, 3 * ATTN2], ctx=at)
                with ExitStack() as b:
                    hi = core.sb("h2_hi", [P, KD, SEQ], F32R, ctx=b)
                    lo = core.sb("h2_lo", [P, KD, SEQ], F32R, ctx=b)
                    w_u = Weights(core, "u2", lambda c: w["w_u2"][c], SSM // FEAT_COLS, FEAT_COLS, b,
                                  width=KD * max(FEAT_COLS, QKV_COLS))
                    w_gate = Weights(core, "gate2", lambda c: w["w_gates2"][c], 2 * D // FEAT_COLS, FEAT_COLS, b, raw=w_u.flat)
                    w_qkv = Weights(core, "qkv2", lambda c: w["w_qkv2"][c], QKV_CHUNKS, QKV_COLS, b, raw=w_u.flat)
                    transpose_split(core, "m1", x, hi, lo, KD, gain, w["norm2"][0], norm=True,
                                    ahead=lambda sp: load_first(sp, w_u))
                    project(core, "u2", hi, lo, w_u, ahead=w_gate,
                            by_feature=lambda c, t, sums: nc.scalar.copy(u_t[:, c * FT + t, :], sums))
                    project(core, "gate2", hi, lo, w_gate, ahead=w_qkv,
                            by_feature=lambda c, t, sums: nc.scalar.activation(
                                gate_t[:, c * FT + t, :], sums, ACT.Sigmoid,
                                bias=core.feature2[:, bass.ds(c * FT + (F_GATE + t), 1)]))
                    project(core, "qkv2", hi, lo, w_qkv,
                            by_token=lambda c, t, sums: nc.vector.tensor_copy(qkv[:, t, bass.ds(c * QKV_COLS, QKV_COLS)], sums))
                T = core.sb("qk2_t", [HEAD, 2 * HEADS2, SEQ], ctx=at)
                o = core.sb("o2", [P, TB, ATTN2], ctx=at)
                prepare_second(core, qkv, T)
                attention(core, "rel", HEADS2, HEAD, lambda j: T[:, j, :], lambda j, n: T[:, HEADS2 + j, 0:n],
                          lambda j, b: qkv[:, b, bass.ds(j * HEAD + 2 * ATTN2, HEAD)], HEAD ** -0.5,
                          lambda i, s: s[:, (TB - 1 - i) * P:TB * P],
                          lambda j, i: o[:, i, bass.ds(j * HEAD, HEAD)], bias_dram=lambda j: w["rel"][j])
                transpose_split(core, "at", o, a_hi, a_lo, SQT)
            core.clear()
            z = core.sb("z", [P, SQT, SEQ], ctx=mix)
            with ExitStack() as ss:
                mag = core.sb("mag", [P, ST], ctx=ss)
                cos_t = core.sb("cos_t", [P, ST, SEQ], ctx=ss)
                sin_t = core.sb("sin_t", [P, ST, SEQ], ctx=ss)
                b_t = core.sb("b_t", [P, 2, SQT, P], ctx=ss)
                c_t = core.sb("c_t", [P, 2, ST, 2 * GROUP], ctx=ss)
                discretise(core, w, mag, cos_t, sin_t, b_t, c_t)
                state_space(core, u_t, mag, cos_t, sin_t, b_t, c_t, z)
            s_hi = core.sb("s_hi", [P, SQT, SEQ], F32R, ctx=mix)
            s_lo = core.sb("s_lo", [P, SQT, SEQ], F32R, ctx=mix)
            with ExitStack() as gl:
                glu = core.sb("glu", [P, SQT, SEQ], ctx=gl)
                w_glu = Weights(core, "glu", lambda c: w["w_glu2"][c], SSM // FEAT_COLS, FEAT_COLS, gl, kd=SQT)
                split(core, "z", z, s_hi, s_lo, SQT, ahead=w_glu.ahead)
                project(core, "glu", s_hi, s_lo, w_glu,
                        by_feature=lambda c, t, sums: nc.scalar.activation(
                            glu[:, c * FT + t, :], sums, ACT.Sigmoid, bias=core.feature2[:, c * FT + F_GLU + t:c * FT + F_GLU + t + 1]))
                split(core, "zg", z, s_hi, s_lo, SQT, b=glu, op=ALU.mult, res=glu)
            core.clear()

            def gated(half):
                def emit(c, t, sums):
                    g = gate_t[:, c * FT + (half * KD + t), :]
                    return nc.vector.tensor_tensor(g, sums, g, ALU.mult)
                return emit
            w_a = Weights(core, "bra", lambda c: w["w_branch_a2"][c], D // FEAT_COLS, FEAT_COLS, mix, kd=SQT, width=KD * FEAT_COLS)
            w_s = Weights(core, "brs", lambda c: w["w_branch_s2"][c], D // FEAT_COLS, FEAT_COLS, mix, kd=SQT, raw=w_a.flat)
            w_out = Weights(core, "out2", lambda c: w["w_out2"][c], D // FEAT_COLS, FEAT_COLS, mix, raw=w_a.flat)
            project(core, "bra", a_hi, a_lo, w_a, by_feature_dve=gated(0), ahead=w_s)
            project(core, "brs", s_hi, s_lo, w_s, by_feature_dve=gated(1), ahead=w_out)
            with ExitStack() as b:
                hi = core.sb("m_hi", [P, KD, SEQ], F32R, ctx=b)
                lo = core.sb("m_lo", [P, KD, SEQ], F32R, ctx=b)
                merged = gate_t[:, 0:KD, :]
                split(core, "mg", merged, hi, lo, KD, b=gate_t[:, KD:2 * KD, :], op=ALU.add, res=merged)
                project(core, "out2", hi, lo, w_out,
                        by_token=lambda c, t, sums: add_to_x(core, c, t, sums, FEAT_COLS))
        with ExitStack() as b:
            hi = core.sb("e_hi", [P, KD, SEQ], F32R, ctx=b)
            lo = core.sb("e_lo", [P, KD, SEQ], F32R, ctx=b)
            gates = core.sb("gates", [P, TB, EXPERTS], ctx=b)
            w_moe = GroupWeights(core, "moe", lambda e: w["w_e_gate2"][e], lambda e: w["w_e_up2"][e],
                                 lambda e: w["w_e_down2"][e], b)
            transpose_split(core, "m2", x, hi, lo, KD, gain, w["norm2"][1], norm=True, ahead=w_moe.ahead)
            logit = core.sb("route_logit", [P, TB, ROUTES], ctx=b)
            route = Route(core, logit, gates, b)
            route_logits(core, w, hi, lo, logit)
            feed_forward(core, "moe", hi, lo, EXPERTS, w_moe, beside=route, weight=lambda t, e: gates[:, t, bass.ds(e, 1)])
        core.clear()


def build(nc, w, out):
    with ExitStack() as ctx:
        core = Core(nc, ctx)
        core.x = core.sb("x", [P, TB, D])
        core.const = core.sb("const", [P, C_COLS])
        with ExitStack() as st:
            x_in = core.sem("x_in", st)
            with nc.Block() as block:
                @block.sync
                def _(sp):
                    sp.dma_start(core.x[:], w["x"].rearrange("a (t p) d -> p (a t) d", p=P)).then_inc(x_in, 16)
                    sp.dma_start(core.const[:], w["const"]).then_inc(x_in, 16)
                    sp.wait_ge(x_in, 32)
            core.clear()
        with nc.Fori(0, DEPTH) as layer:
            first_block(core, w, layer)
        second_block(core, w)
        with ExitStack() as st:
            stored = core.sem("stored", st)
            with nc.Block() as block:
                @block.sync
                def _(sp):
                    sp.dma_start(out.rearrange("a (t p) d -> p (a t) d", p=P), core.x[:]).then_inc(stored, 16)
                    sp.wait_ge(stored, 16)


def constants():
    import numpy as np
    f = np.float32
    r = np.arange(P)
    c = np.zeros((P, C_COLS), f)
    c[:, C_ID:C_ID + P] = np.eye(P)
    c[:, C_TRI:C_TRI + P] = r[:, None] <= r[None, :]
    c[:, C_ONE:C_ONE + P] = 1
    c[:, C_ROPE - P:C_ROPE] = np.where(r[None, :] <= r[:, None], 0, f(NEG))
    c[:, C_CHUNK:C_CHUNK + P] = np.where(r[None, :] // 64 <= r[:, None] // 64, 0, f(NEG))
    table = []
    for d in (HEAD, DIFF_D):
        rot = d // 4
        inv = (1.0 / (f(500000.0) ** (np.arange(0, rot, 2, dtype=f) / f(rot)))).astype(f)
        ang = np.arange(SEQ, dtype=f)[:, None] * inv[None, :]
        table += [np.cos(ang), np.sin(ang)]
    rope = np.concatenate(table, 1).reshape(TB, P, ROPE_COLS).transpose(1, 0, 2)
    c[:, C_ROPE:C_ROPE + TB * ROPE_COLS] = rope.reshape(P, -1)
    c[:HEAD, C_FOX] = HEAD ** -0.5
    c[HEAD:HEAD + 2, C_FOX] = 1
    c[:, C_RANK:C_RANK + 4] = [4, 3, 2, 1]
    return c


def kernel(**inputs):
    import numpy as np
    import concourse.bacc as bacc
    from concourse.bass_utils import run_bass_kernel_spmd as run

    a = {k: np.asarray(v) for k, v in inputs.items()}

    def chunks(m, n, cols):
        m = np.pad(m, [(0, 0)] * (m.ndim - 1) + [(0, n * cols - m.shape[-1])])
        m = m.reshape(*m.shape[:-2], m.shape[-2] // P, P, n, cols)
        nd = m.ndim
        m = m.transpose(*range(nd - 4), nd - 2, nd - 3, nd - 4, nd - 1)
        return m.reshape(*m.shape[:-2], -1)

    def rows(m, groups):
        m = m.reshape(*m.shape[:-2], groups, -1, P, m.shape[-1])
        m = m.swapaxes(-3, -2)
        return m.reshape(*m.shape[:-2], -1)

    def per_feature(g):
        return g.reshape(*g.shape[:-1], -1, P).swapaxes(-1, -2)

    lam = np.array([[0.8 - 0.6 * math.exp(-0.3 * l), 1 - (0.8 - 0.6 * math.exp(-0.3 * l))] for l in range(DEPTH)], np.float32)
    gu = a["w_gate_up"]
    w = {
        "x": a["x"], "const": constants(), "lam": lam,
        "params": np.concatenate([a[n] for n, _ in PARAMS], 1),
        "attn_norm": per_feature(a["attn_norm"]), "ffn_norm": per_feature(a["ffn_norm"]),
        "w_in": chunks(a["w_in"], IN_CHUNKS, IN_COLS), "w_out": chunks(a["w_out"], OUT_CHUNKS, OUT_COLS),
        "w_gate": chunks(gu[:, :, :FFN], FFN_GROUPS, HID), "w_up": chunks(gu[:, :, FFN:], FFN_GROUPS, HID),
        "w_down": rows(a["w_down"], FFN_GROUPS),
    }
    b = {k[:-2]: v[0] for k, v in a.items() if k.endswith("_2")}
    rel = np.clip(np.arange(P)[:, None] - np.arange(SEQ)[None, :] + SEQ - P, -REL_FUTURE, MAX_REL) + REL_FUTURE

    def by_state(m):
        m = m.reshape(ST, P, *m.shape[2:])
        return m.swapaxes(0, 1)

    def block_diagonal(m):
        wide = np.zeros((ST, 2, STATE, 2, GROUP), m.dtype)
        for n in range(2):
            wide[:, n, :, n] = m.reshape(ST, 2, STATE, GROUP)[:, n]
        return wide.reshape(ST, P, 2 * GROUP).swapaxes(0, 1)

    w.update({
        "params2": np.concatenate([b["q_gain"], b["k_gain"], b["group_bias"], b["expert_bias"]]),
        "norm2": np.stack([per_feature(b["mix_norm_gain"]), per_feature(b["ffn_norm_gain"])]),
        "rel": b["rel_bias"][:, rel],
        "w_qkv2": chunks(b["w_in"][:, :3 * ATTN2], QKV_CHUNKS, QKV_COLS),
        "w_u2": chunks(b["w_in"][:, 3 * ATTN2:3 * ATTN2 + SSM], SSM // FEAT_COLS, FEAT_COLS),
        "w_gates2": chunks(b["w_in"][:, 3 * ATTN2 + SSM:], 2 * D // FEAT_COLS, FEAT_COLS),
        "feature2": np.concatenate([per_feature(b["b_gate"]), per_feature(b["b_glu"]), per_feature(b["ssm_d"])], 1),
        "w_glu2": chunks(b["w_glu"], SSM // FEAT_COLS, FEAT_COLS),
        "w_branch_a2": chunks(b["w_branch"][:ATTN2], D // FEAT_COLS, FEAT_COLS),
        "w_branch_s2": chunks(b["w_branch"][ATTN2:], D // FEAT_COLS, FEAT_COLS),
        "w_out2": chunks(b["w_out"], D // FEAT_COLS, FEAT_COLS),
        "lambda2": np.concatenate([by_state(b["ssm_lambda_re"]), by_state(b["ssm_lambda_im"])], 1),
        "log_step2": b["ssm_log_step"].reshape(ST, 2).T,
        "b_diag2": np.stack([block_diagonal(b["ssm_b_re"]), block_diagonal(b["ssm_b_im"])], 1).reshape(P, -1),
        "c_diag2": np.stack([block_diagonal(b["ssm_c_re"].swapaxes(1, 2)),
                             block_diagonal(b["ssm_c_im"].swapaxes(1, 2))], 1).reshape(P, -1),
        "w_route2": chunks(np.concatenate([b["w_group_router"], b["w_expert_router"]], 1), 1, ROUTES)[0],
        "w_e_gate2": chunks(b["w_e_gate"], 1, HID)[:, 0], "w_e_up2": chunks(b["w_e_up"], 1, HID)[:, 0],
        "w_e_down2": rows(b["w_e_down"], 1)[:, 0],
    })
    nc = bacc.Bacc("TRN2", target_bir_lowering=False, num_devices=1)
    arrays = {f"in_{k}": np.ascontiguousarray(v) for k, v in w.items()}
    args = {k: nc.dram_tensor(f"in_{k}", list(arrays[f"in_{k}"].shape), F32, kind="ExternalInput").ap() for k in w}
    out = nc.dram_tensor("out_x", [1, SEQ, D], F32, kind="ExternalOutput").ap()
    build(nc, args, out)
    return run(nc, [arrays], core_ids=[0]).results[0]["out_x"]
```
